# Optimizing a Trainium2 kernel written in Bass

```python
import jax, jax.numpy as jnp
from jax import lax
import numpy as np

D_MODEL = 1024
BATCH = 1
SEQ = 512
DEPTH = 1
DEC_BATCH = 8
DEC_SEQ = 1
PAST_LEN = 4096
PAGE_SIZE = 128

D_MIX = D_MODEL
D_A = D_MIX // 4
W_A = 3
D_B = D_MIX // 4
W_B = 31
D_C = D_MIX // 2
H_C = 4
DK = D_C // H_C
DV = D_C // H_C
W_C = 4
CHUNK = 64
D_IN = 3 * D_A + 2 * D_B + 3 * D_C + D_C + 2 * H_C
N_GROUPS = 4
EXP_PER_GROUP = 8
N_EXPERTS = N_GROUPS * EXP_PER_GROUP
TOP_K = 2
D_EXPERT = D_MODEL // 4
EPS = 1e-6

kernel_name = 'hybrid_conv_conformer_gdn_hmoe_step'

def rms_norm(x, g):
    xf = x.astype(jnp.float32)
    y = xf * lax.rsqrt(jnp.mean(xf * xf, axis=-1, keepdims=True) + EPS)
    return (y * g.astype(jnp.float32)).astype(x.dtype)

def layer_norm(x, g, b):
    xf = x.astype(jnp.float32)
    mu = jnp.mean(xf, axis=-1, keepdims=True)
    xc = xf - mu
    y = xc * lax.rsqrt(jnp.mean(xc * xc, axis=-1, keepdims=True) + EPS)
    return (y * g.astype(jnp.float32) + b.astype(jnp.float32)).astype(x.dtype)

def l2_normalize(x):
    xf = x.astype(jnp.float32)
    return xf * lax.rsqrt(jnp.sum(xf * xf, axis=-1, keepdims=True) + 1e-6)

def causal_depthwise_conv(x, prev, w):
    width = w.shape[0]
    xx = jnp.concatenate([prev.astype(x.dtype), x], axis=1)
    y = lax.conv_general_dilated(xx, w[:, None, :].astype(x.dtype), window_strides=(1,), padding='VALID',
                                 dimension_numbers=('NWC', 'WIO', 'NWC'), feature_group_count=x.shape[-1])
    return y, xx[:, xx.shape[1] - (width - 1):]

def gated_delta_rule(q, k, v, g, beta, s0):
    n_b, t_len = q.shape[0], q.shape[1]
    c = min(CHUNK, t_len)
    n_c = -(-t_len // c)
    pad = n_c * c - t_len

    def blk(a):
        a = jnp.pad(a, [(0, 0), (0, pad), (0, 0), (0, 0)])
        return a.reshape(n_b, n_c, c, a.shape[2], a.shape[3]).transpose(1, 0, 3, 2, 4)

    def blk_s(a):
        a = jnp.pad(a, [(0, 0), (0, pad), (0, 0)])
        return a.reshape(n_b, n_c, c, a.shape[2]).transpose(1, 0, 3, 2)

    qb, kb, vb = blk(q), blk(k), blk(v)
    gb, bb = blk_s(g), blk_s(beta)
    G = jnp.cumsum(gb, axis=-1)
    diff = G[..., :, None] - G[..., None, :]
    idx = jnp.arange(c)
    strict = idx[:, None] > idx[None, :]
    incl = idx[:, None] >= idx[None, :]
    kk = jnp.einsum('nbhid,nbhjd->nbhij', kb, kb)
    a_mat = bb[..., :, None] * kk * jnp.exp(jnp.where(strict, diff, -jnp.inf))
    rhs = jnp.concatenate([vb * bb[..., None], kb * (bb * jnp.exp(G))[..., None]], axis=-1)
    sol = lax.linalg.triangular_solve(a_mat, rhs, left_side=True, lower=True, unit_diagonal=True)
    u, w = sol[..., :DV], sol[..., DV:]
    qk = jnp.einsum('nbhid,nbhjd->nbhij', qb, kb) * jnp.exp(jnp.where(incl, diff, -jnp.inf))
    q_dec = qb * jnp.exp(G)[..., None]
    k_dec = kb * jnp.exp(G[..., -1:] - G)[..., None]
    g_last = jnp.exp(G[..., -1])

    def step(s, xs):
        u_c, w_c, qd_c, qk_c, kd_c, gl_c = xs
        v_new = u_c - jnp.einsum('bhck,bhkv->bhcv', w_c, s)
        o_c = jnp.einsum('bhck,bhkv->bhcv', qd_c, s) + jnp.einsum('bhij,bhjv->bhiv', qk_c, v_new)
        s = s * gl_c[..., None, None] + jnp.einsum('bhck,bhcv->bhkv', kd_c, v_new)
        return s, o_c

    s_fin, o = lax.scan(step, s0, (u, w, q_dec, qk, k_dec, g_last))
    o = o.transpose(1, 0, 3, 2, 4).reshape(n_b, n_c * c, H_C, DV)[:, :t_len]
    return o, s_fin

def hier_moe(h, w_group, w_router, w_gate, w_up, w_down):
    g_logits = jnp.einsum('btd,dg->btg', h, w_group).astype(jnp.float32)
    g_prob = jax.nn.softmax(g_logits, axis=-1)
    g_idx = jnp.argmax(g_logits, axis=-1)
    g_p = jnp.max(g_prob, axis=-1)
    e_logits = jnp.einsum('btd,gde->btge', h, w_router).astype(jnp.float32)
    e_logits = jnp.take_along_axis(e_logits, g_idx[..., None, None], axis=2)[..., 0, :]
    e_prob = jax.nn.softmax(e_logits, axis=-1)
    top_p, top_i = lax.top_k(e_prob, TOP_K)
    top_p = top_p / jnp.sum(top_p, axis=-1, keepdims=True)
    e_idx = g_idx[..., None] * EXP_PER_GROUP + top_i
    combine = jnp.sum(jax.nn.one_hot(e_idx, N_EXPERTS, dtype=jnp.float32)
                      * (g_p[..., None] * top_p)[..., None], axis=-2).astype(h.dtype)
    gate = jnp.einsum('btd,edf->btef', h, w_gate)
    up = jnp.einsum('btd,edf->btef', h, w_up)
    act = jax.nn.silu(gate) * up * combine[..., None]
    return jnp.einsum('btef,efd->btd', act, w_down)

def decoder_layer(x, conv_a_prev, conv_b_prev, conv_qkv_prev, delta_prev, norm1_g, w_in, conv_a_w, conv_b_w,
                  ln_b_g, ln_b_b, conv_c_w, a_log, dt_bias, o_norm_g, w_out, norm2_g, w_group, w_router,
                  w_gate, w_up, w_down):
    n_b, t_len, _ = x.shape
    h = rms_norm(x, norm1_g)
    z = jnp.einsum('btd,de->bte', h, w_in)
    offs = np.cumsum([D_A, D_A, D_A, D_B, D_B, 3 * D_C, D_C, H_C]).tolist()
    a_b, a_c, a_h, b_val, b_gate, qkv, c_gate, c_beta, c_alpha = jnp.split(z, offs, axis=-1)
    conv_a_out, conv_a_new = causal_depthwise_conv(a_c * a_h, conv_a_prev, conv_a_w)
    y_a = a_b * conv_a_out
    conv_b_out, conv_b_new = causal_depthwise_conv(b_val * jax.nn.sigmoid(b_gate), conv_b_prev, conv_b_w)
    y_b = jax.nn.silu(layer_norm(conv_b_out, ln_b_g, ln_b_b))
    qkv_conv, conv_qkv_new = causal_depthwise_conv(qkv, conv_qkv_prev, conv_c_w)
    qkv_conv = jax.nn.silu(qkv_conv)
    q, k, v = jnp.split(qkv_conv, 3, axis=-1)
    q = l2_normalize(q.reshape(n_b, t_len, H_C, DK)) * (DK ** -0.5)
    k = l2_normalize(k.reshape(n_b, t_len, H_C, DK))
    v = v.reshape(n_b, t_len, H_C, DV).astype(jnp.float32)
    beta = jax.nn.sigmoid(c_beta.astype(jnp.float32))
    g = -jnp.exp(a_log.astype(jnp.float32)) * jax.nn.softplus(c_alpha.astype(jnp.float32) + dt_bias.astype(jnp.float32))
    o, delta_new = gated_delta_rule(q, k, v, g, beta, delta_prev.astype(jnp.float32))
    o = rms_norm(o, o_norm_g) * jax.nn.silu(c_gate.reshape(n_b, t_len, H_C, DV).astype(jnp.float32))
    y_c = o.reshape(n_b, t_len, D_C).astype(x.dtype)
    x = x + jnp.einsum('bte,ed->btd', jnp.concatenate([y_a, y_b, y_c], axis=-1), w_out)
    x = x + hier_moe(rms_norm(x, norm2_g), w_group, w_router, w_gate, w_up, w_down)
    return x, conv_a_new, conv_b_new, conv_qkv_new, delta_new.astype(delta_prev.dtype)

def setup_inputs(seed: int = 0) -> dict:
    key = jax.random.key(seed)
    ks = jax.random.split(key, 26)

    def nrm(k, shape, scale):
        return jax.random.normal(k, shape, jnp.float32) * scale

    dt = jnp.exp(jax.random.uniform(ks[15], (DEPTH, H_C), jnp.float32, float(np.log(1e-3)), float(np.log(1e-1))))
    return {
        'x_prompt': nrm(ks[0], (BATCH, SEQ, D_MODEL), 1.0),
        'x_sample': nrm(ks[1], (DEC_BATCH, DEC_SEQ, D_MODEL), 1.0),
        'state_conv_a': nrm(ks[2], (DEPTH, DEC_BATCH, W_A - 1, D_A), 1.0),
        'state_conv_b': nrm(ks[3], (DEPTH, DEC_BATCH, W_B - 1, D_B), 0.5),
        'state_conv_qkv': nrm(ks[4], (DEPTH, DEC_BATCH, W_C - 1, 3 * D_C), 1.0),
        'state_delta': nrm(ks[5], (DEPTH, DEC_BATCH, H_C, DK, DV), 0.3),
        'norm1_g': 1.0 + nrm(ks[6], (DEPTH, D_MODEL), 0.02),
        'w_in': nrm(ks[7], (DEPTH, D_MODEL, D_IN), D_MODEL ** -0.5),
        'conv_a_w': nrm(ks[8], (DEPTH, W_A, D_A), W_A ** -0.5),
        'conv_b_w': nrm(ks[9], (DEPTH, W_B, D_B), W_B ** -0.5),
        'ln_b_g': 1.0 + nrm(ks[10], (DEPTH, D_B), 0.02),
        'ln_b_b': nrm(ks[11], (DEPTH, D_B), 0.02),
        'conv_c_w': nrm(ks[12], (DEPTH, W_C, 3 * D_C), W_C ** -0.5),
        'a_log': jnp.log(jax.random.uniform(ks[13], (DEPTH, H_C), jnp.float32, 1.0, 16.0)),
        'dt_bias': jnp.log(jnp.expm1(dt)),
        'o_norm_g': 1.0 + nrm(ks[14], (DEPTH, DV), 0.02),
        'w_out': nrm(ks[16], (DEPTH, D_MIX, D_MODEL), D_MIX ** -0.5),
        'norm2_g': 1.0 + nrm(ks[17], (DEPTH, D_MODEL), 0.02),
        'w_group': nrm(ks[18], (DEPTH, D_MODEL, N_GROUPS), D_MODEL ** -0.5),
        'w_router': nrm(ks[19], (DEPTH, N_GROUPS, D_MODEL, EXP_PER_GROUP), D_MODEL ** -0.5),
        'w_gate': nrm(ks[20], (DEPTH, N_EXPERTS, D_MODEL, D_EXPERT), D_MODEL ** -0.5),
        'w_up': nrm(ks[21], (DEPTH, N_EXPERTS, D_MODEL, D_EXPERT), D_MODEL ** -0.5),
        'w_down': nrm(ks[22], (DEPTH, N_EXPERTS, D_EXPERT, D_MODEL), D_EXPERT ** -0.5),
        'final_g': 1.0 + nrm(ks[23], (D_MODEL,), 0.02),
    }

def reference(x_prompt, x_sample, state_conv_a, state_conv_b, state_conv_qkv, state_delta, norm1_g, w_in,
              conv_a_w, conv_b_w, ln_b_g, ln_b_b, conv_c_w, a_log, dt_bias, o_norm_g, w_out, norm2_g, w_group,
              w_router, w_gate, w_up, w_down, final_g):
    n_p = x_prompt.shape[0]
    xp, xs = x_prompt, x_sample
    pa, pb, pq, pd, sa, sb, sq, sd = [], [], [], [], [], [], [], []
    for l in range(DEPTH):
        params = (norm1_g[l], w_in[l], conv_a_w[l], conv_b_w[l], ln_b_g[l], ln_b_b[l], conv_c_w[l], a_log[l],
                  dt_bias[l], o_norm_g[l], w_out[l], norm2_g[l], w_group[l], w_router[l], w_gate[l], w_up[l], w_down[l])
        xp, ca, cb, cq, dd = decoder_layer(
            xp, jnp.zeros((n_p, W_A - 1, D_A), xp.dtype), jnp.zeros((n_p, W_B - 1, D_B), xp.dtype),
            jnp.zeros((n_p, W_C - 1, 3 * D_C), xp.dtype), jnp.zeros((n_p, H_C, DK, DV), state_delta.dtype), *params)
        pa.append(ca); pb.append(cb); pq.append(cq); pd.append(dd)
        xs, ca, cb, cq, dd = decoder_layer(xs, state_conv_a[l], state_conv_b[l], state_conv_qkv[l], state_delta[l], *params)
        sa.append(ca); sb.append(cb); sq.append(cq); sd.append(dd)
    y_prompt = rms_norm(xp, final_g)
    y_sample = rms_norm(xs, final_g)
    new_conv_a_prompt = jnp.stack(pa)
    new_conv_b_prompt = jnp.stack(pb)
    new_conv_qkv_prompt = jnp.stack(pq)
    new_delta_prompt = jnp.stack(pd)
    new_conv_a_sample = jnp.stack(sa)
    new_conv_b_sample = jnp.stack(sb)
    new_conv_qkv_sample = jnp.stack(sq)
    new_delta_sample = jnp.stack(sd)
    return (y_prompt, y_sample, new_conv_a_prompt, new_conv_b_prompt, new_conv_qkv_prompt, new_delta_prompt,
            new_conv_a_sample, new_conv_b_sample, new_conv_qkv_sample, new_delta_sample)


_drawn_inputs = setup_inputs


def setup_inputs(seed=0):
    import zlib

    import numpy as np

    out = dict(_drawn_inputs(seed))
    spreads = {}
    factors = {'ln_b_g': 35.011,
     'ln_b_b': 14.004,
     'o_norm_g': 31.129,
     'final_g': 23.889,
     'norm2_g': 4.275}
    for name, (base, spread) in spreads.items():
        noise = np.random.default_rng([zlib.crc32(name.encode()), seed]).standard_normal(out[name].shape)
        drawn = base * np.exp(spread * noise) if base else spread * noise
        out[name] = __import__('jax').numpy.asarray(drawn.astype(out[name].dtype))
    for name, factor in factors.items():
        out[name] = (out[name] * factor).astype(out[name].dtype)
    return out
```

```python
from contextlib import ExitStack

import concourse.bass as bass
import numpy as np
from concourse import mybir

ALU = mybir.AluOpType
ACT = mybir.ActivationFunctionType
F32 = mybir.dt.float32
I32 = mybir.dt.int32
F32R = mybir.dt.float32r
AX_X = mybir.AxisListType.X

P = 128
D = 1024
KT = D // P
SEQ, NS = 512, 8
T = SEQ + NS
TT = SEQ // P
NT = TT + 1
HT = T // 2
DA = DB = 256
H = 4
WA, WB, WC = 3, 31, 4
CQ = 3 * H
RAW = (WC - 1) + SEQ + NS * WC
CV = RAW - (WC - 1)
SC = SEQ + WC - 1
HC = CV // 2
EPS = 1e-6
NG, EG = 4, 8
NE = NG * EG
F = 256
CAP = 64
MAXROWS = 9 * CAP
MORE = MAXROWS // CAP - 1
NOWHERE = 1 << 20
LEVELS = 7

BLOCKS = [3, 4, 0, 1, 2, 5, 7, 9, 6, 8, 10, 11, 12]
NZ = 2 * len(BLOCKS)
ZA, ZQ, ZG = 4, 10, 22
QKV = [0, 1, 4, 5, 8, 9, 2, 3, 6, 7, 10, 11]
WSLOTS = 4
ROWS_AB = WB + 2 + WA + NS * (WA - 1)
LNG, LNB, CAW, STA = WB, WB + 1, WB + 2, WB + 2 + WA
ROWS_Q = WC + NS * (WC - 1)

C_ID, C_UI, C_US, C_MN, C_ONE, C_LM = 0, 128, 256, 384, 512, 640
C_COL = C_LM + 128 * LEVELS
C_IO = C_COL + 16
C_GI = C_IO + NE
C_HALF = C_GI + NE
C_ROWID = C_HALF + 1
C_TILE = C_ROWID + NT
C_PAD = C_TILE + NT
C_EC = C_PAD + NT
C_SEL = C_EC + NE
C_END = C_SEL + 8 * 128


def constants():
    c = np.zeros((P, C_END), np.float32)
    p = np.arange(P)
    c[:, C_ID:C_ID + P] = np.eye(P)
    c[:, C_UI:C_UI + P] = p[:, None] <= p[None, :]
    c[:, C_US:C_US + P] = p[:, None] < p[None, :]
    c[:, C_MN:C_MN + P] = np.where(p[:, None] <= p[None, :], 0.0, -1e30)
    c[:, C_ONE:C_ONE + P] = 1.0
    for n in range(LEVELS):
        m = 1 << n
        j, i = p[:, None] // m, p[None, :] // m
        c[:, C_LM + n * P:C_LM + (n + 1) * P] = (i // 2 == j // 2) & (i % 2 == 1) & (j % 2 == 0)
    c[:, C_COL + 7] = 1.0
    c[:, C_IO:C_IO + NE] = np.arange(NE)
    c[:, C_GI:C_GI + NE] = np.arange(NE) // EG
    c[:, C_HALF] = p // CAP
    c[:, C_EC:C_EC + NE] = np.arange(NE) % 2 * (NE // 2) + np.arange(NE) // 2
    for t in range(NT):
        real = t * P + p < T
        c[:, C_ROWID + t] = np.where(real, t * P + p, NOWHERE)
        c[:, C_TILE + t] = real
        c[:, C_PAD + t] = np.where(real, 0.0, NOWHERE)
    for m in range(8):
        c[m, C_SEL + m * P:C_SEL + (m + 1) * P] = 1.0
    return c


def bcast(ap, n):
    return ap.unsqueeze(2).broadcast_to([ap.shape[0], ap.shape[1], n])



def build(nc, A, R):
    with ExitStack() as ctx:
        base = (nc.sbuf_base + 31) // 32 * 32

        class Region:

            def __init__(self, start, end):
                self.at, self.end = (start + 31) // 32 * 32, end

            def __call__(self, name, shape, dt=F32):
                n = 2 if dt == mybir.dt.bfloat16 else 4
                for d in shape[1:]:
                    n *= d
                t = nc.alloc_sbuf_tensor_at(name, shape, dt, offset=base + self.at)
                self.at += (n + 31) // 32 * 32
                assert self.at <= self.end, (name, self.at, self.end)
                return t

        def sem(name):
            return ctx.enter_context(nc.semaphore(name))

        h2d = nc.dram_tensor("h2_rows", [T, D], F32, kind="Internal").ap()
        tab = nc.dram_tensor("slot_table", [MAXROWS * NE, 1], I32, kind="Internal").ap()
        yd = nc.dram_tensor("expert_rows", [2 * T * 2, D // 2], F32, kind="Internal").ap()

        ps = ctx.enter_context(nc.psum_tensor("ps", [P, 8, 512], F32))

        K1 = 44064 + 256
        K2 = K1 + 55840
        K3 = K2 + 26208
        K4 = K3 + 16672
        K5 = (nc.sbuf_usable_end - base) // 32 * 32
        keep = Region(0, K1)
        x = keep("x", [P, NT, D])
        cst = keep("cst", [P, C_END])
        gfb = keep("gfb", [P, D])
        parq = keep("parq", [P, CQ, ROWS_Q])
        parab = keep("parab", [P, 2, ROWS_AB])
        g1c = keep("g1c", [P, KT])
        wgt = keep("wgt", [P, 2, NT])
        pid = keep("pid", [P, 2, NT], I32)
        where = keep("where", [P, 2, NT], I32)
        graw = keep("graw", [P, NE // 2], I32)
        sraw = keep("sraw", [P, NE], I32)
        gidx = keep("gidx", [P, NE // 2], I32)
        sidx = keep("sidx", [P, NE], I32)
        idf = keep("idf", [P, 2, NE])
        more = keep("more", [1, NE], I32)
        moref = keep("moref", [1, 2, NE])
        ogc = keep("ogc", [P, 1])
        ogh = keep("ogh", [P, 1])
        epsc = keep("epsc", [P, 1])
        lnh = keep("lnh", [P, 2, 2])
        alog = keep("alog", [P, H])
        dtb = keep("dtb", [P, H])
        ss = keep("ss", [P, NT])
        rstd = keep("rstd", [P, NT])
        ba = keep("ba", [P, NT, 8])
        gw = keep("gw", [P, 10, NT, H])
        stq = keep("stq", [P, CQ, 27])
        sta = keep("sta", [P, 2, 2 + NS * 2])
        stp = keep("stp", [P, 2, WB - 1])
        small = keep("small", [P, CQ, NS])
        kq = keep("kq", [P, H, NS, 2])
        wr = keep("wr", [P, KT, NG + NE])
        nowhere = keep("nowhere", [P, MAXROWS * NE // P], I32)

        proj = Region(K1, K2)
        hhi = proj("hhi", [P, KT, T], F32R)
        hlo = proj("hlo", [P, KT, T], F32R)
        whi = [proj(f"whi{s}", [P, KT, P], F32R) for s in range(WSLOTS)]
        at = [proj.at]
        wraw = [proj("wraw0", [P, KT, P])]
        late = Region(K1, K2)
        wout = late("wout", [P, KT, D])
        s0 = late("s0", [P, H, NS, P])
        g2b = late("g2b", [P, D])
        stb = Region(K5 - 1920, K5)("stb", [P, 2, NS * (WB - 1)])

        hT = Region(K2, K3)("hT", [P, KT, T])
        convd = Region(K2, K3)
        cv = [convd(f"cv{n}", [P, CV]) for n in range(CQ)]
        mixed = Region(K3, K4)
        yT = mixed("yT", [P, 8, T])

        first = Region(K4, K5 - 1920)
        at += [first.at + n * 4096 for n in range(WSLOTS - 1)]
        wraw += [first(f"wraw{s}", [P, KT, P]) for s in range(1, WSLOTS)]
        wlo = [Region(a, a + 4096)(f"wlo{s}", [P, KT, P], F32R) for s, a in enumerate(at)]
        raw = [first(f"raw{s}", [P, RAW]) for s in range(3)]
        begin = Region(first.at, first.at + 8704)
        hrow = [begin(f"hrow{s}", [P, KT, P]) for s in range(2)]
        silu = Region(first.at, first.at + 8704)
        th = [silu(f"th{s}", [P, CV]) for s in range(2)]
        sq = [silu(f"sq{s}", [P, CV]) for s in range(2)]
        first.at += 8704
        rowq = first("rowq", [ROWS_Q, CQ * P])
        rowab = first("rowab", [ROWS_AB, DB])
        rowsb = first("rowsb", [120, 2, DB])
        wba = first("wba", [P, KT, 8])
        convolved = Region(first.at, first.at + 6528)
        acc = [convolved(f"acc{s}", [P, CV]) for s in range(3)]
        bval = [first(f"bval{t}", [P, T]) for t in range(2)]
        bth = [first(f"bth{t}", [P, T]) for t in range(2)]
        gates = Region(K3 + 16 * T, K4)
        mab = [gates(f"mab{t}", [P, T]) for t in range(2)]
        mac = [gates(f"mac{t}", [P, T]) for t in range(2)]
        mah = [first(f"mah{t}", [P, T]) for t in range(2)]
        ub = [first(f"ub{t}", [P, WB - 1 + SEQ]) for t in range(2)]
        usb = first("usb", [P, 2, NS, WB])
        sprod = first("sprod", [P, NS, WB])
        ua = [first(f"ua{t}", [P, WA - 1 + SEQ]) for t in range(2)]
        uas = first("uas", [P, 2, NS, WA])
        rn = first("rn", [8, 2, CV])

        delta = Region(K4, K5 - 1920)
        four = [P, TT, P]
        wT = [delta(f"wT{z}", four) for z in range(2)]
        t1 = [delta(f"t1{z}", four) for z in range(2)]
        vn = [delta(f"vn{z}", four) for z in range(2)]
        S = [[delta(f"S{z}{s}", [P, P]) for s in range(2)] for z in range(2)]
        grep = [delta(f"grep{z}", four) for z in range(2)]
        brep = [delta(f"brep{z}", four) for z in range(2)]
        kbG, kd = grep, brep
        eG = [delta(f"eG{z}", four) for z in range(2)]
        qG = [delta(f"qG{z}", four) for z in range(2)]
        kb = [delta(f"kb{z}", four) for z in range(2)]
        DT = [delta(f"DT{z}", four) for z in range(2)]
        AT = [delta(f"AT{z}", four) for z in range(2)]
        att = [delta(f"att{z}", four) for z in range(2)]
        BT = [[delta(f"BT{z}{s}", four) for s in range(2)] for z in range(2)]
        XX = [delta(f"XX{z}", [P, 2, TT, P]) for z in range(2)]
        vb = kb
        mix = Region(K4, K5 - 49152)
        samples = Region(K5 - 24576, K5)
        dg = samples("dg", [NS, 2, H, NS])
        sb = samples("sb", [P, 8, H * NS])
        kqs = samples("kqs", [P, H * NS, 2])
        srow = samples("srow", [NS, 2, H * P])
        vnd = samples("vnd", [NS, NS, P])
        osq = [mix(f"osq{s}", [P, T]) for s in range(2)]
        rno = mix("rno", [8, 2, T])
        bth2 = osq
        rowq2 = mix("rowq2", [27, CQ * P])
        rowab2 = mix("rowab2", [18, DB])
        rowsb2 = mix("rowsb2", [120, 2, DB])
        rowb = mix("rowb", [WB - 1, DB])
        route = Region(K4, K5 - 49152)
        h2row = [route(f"h2row{s}", [P, KT, P]) for s in range(2)]
        h2T = route("h2T", [P, KT, P])
        tail = Region(K2 + 24576, K3)
        L = tail("L", [P, NT, NG + NE])
        ns = tail("ns", [P, 12, NT])
        g4 = tail("g4", [P, 3, NT, NG])
        sqj = route("sqj", [P, D], mybir.dt.bfloat16)
        eight = [route(f"eight{n}", [P, NT, NE]) for n in range(7)]
        wslots = [Region(a, a + 24576) for a in (K2, K5 - 49152, K5 - 24576, K1)]
        gu = [r(f"gu{n}", [P, 2, KT, F]) for n, r in enumerate(wslots)]
        wd = [r(f"wd{n}", [P, 2, D]) for n, r in enumerate(wslots)]
        moe = Region(K1 + 24576, K2)
        xg = [moe(f"xg{s}", [P, D]) for s in range(2)]
        xT = [moe(f"xT{s}", [P, KT, P]) for s in range(2)]
        ysb = [moe(f"ysb{s}", [P, D // 2]) for s in range(4)]
        yk = [Region(a, a + 8192)(f"yk{i}", [P, 2, D]) for i, a in enumerate(
            (K2, K2 + 8192, K5 - 49152, K5 - 49152 + 8192, K5 - 24576))]
        fsq = Region(K2 + 16384, K3)("fsq", [P, D])
        moe2 = Region(K3, K4)
        gth = [moe2(f"gth{s}", [P, P]) for s in range(2)]
        gact = [moe2(f"gact{s}", [P, P]) for s in range(2)]
        aT = [moe2(f"aT{s}", [P, P]) for s in range(2)]
        gcur = [moe2(f"gcur{s}", [P, 1], I32) for s in range(2)]
        zero = moe2("zero", [P, 1], I32)
        scur = [moe2(f"scur{s}", [P, 1], I32) for s in range(4)]
        xTo = moe2("xTo", [P, KT, CAP])
        oth, oact, oaT = (moe2(n, [P, P]) for n in ("oth", "oact", "oaT"))
        yo = moe2("yo", [P, D // 2])
        otok = [moe2(f"otok{s}", [P, 1], I32) for s in range(2)]
        osid = moe2("osid", [P, 1], I32)
        further = Region(K4, K5 - 49152)
        oraw = further("oraw", [P, MORE, NE], I32)
        oidf = [further(f"oidf{n}", [P, MORE, NE]) for n in range(2)]
        otoks = further("otoks", [P, (MORE + 1) * NE], I32)
        osids = further("osids", [P, MORE * NE], I32)
        xo = [further(f"xo{s}", [CAP, D]) for s in range(2)]
        sfin = late("sfin", [P, H, P])
        nG, eGc, sc1, sc3, gdif, kds = (gw[:, n] for n in (2, 3, 4, 5, 6, 8))

        ident = cst[:, C_ID:C_ID + P]
        incl = cst[:, C_UI:C_UI + P]
        ones = cst[:, C_ONE:C_ONE + P]

        def column(m):
            return cst[:, C_COL + 7 - m:C_COL + 15 - m]

        def select(m):
            return cst[0:8, C_SEL + m * P:C_SEL + (m + 1) * P]

        def tokens(i):
            return slice(i * P, min((i + 1) * P, T))

        x_in = [sem(f"x_in{i}") for i in range(NT)]
        g1_in = sem("g1_in")
        consts_in, rows_in, small_in = sem("consts_in"), sem("rows_in"), sem("small_in")
        weights_in = [sem(f"weights_in{s}") for s in range(WSLOTS)]
        tiles_in = [16 * len(range(s, NZ, WSLOTS)) for s in range(WSLOTS)]
        w_hi, w_lo, h_hi, h_lo = sem("w_hi"), sem("w_lo"), sem("h_hi"), sem("h_lo")
        x_squared, rstd_ready = sem("x_squared"), sem("rstd_ready")
        hrow_ready, h_turned, hT_ready = sem("hrow_ready"), sem("h_turned"), sem("hT_ready")
        rows_turned, params_ready = sem("rows_turned"), sem("params_ready")
        ba_done, ba_ready = sem("ba_done"), sem("ba_ready")
        z_done, z_evac = sem("z_done"), sem("z_evac")
        glu_ready = sem("glu_ready")
        conv_done, tanh_done, cv_done, squared, sums_done = (
            sem("conv_done"), sem("tanh_done"), sem("cv_done"), sem("squared"), sem("sums_done"))
        raw_saved = sem("raw_saved")
        sums_ready, norms_ready, norms_spread, qk_ready = (
            sem("sums_ready"), sem("norms_ready"), sem("norms_spread"), sem("qk_ready"))
        gate_tanh, a_mixed, b_conved = sem("gate_tanh"), sem("a_mixed"), sem("b_conved")
        states_ready, states_out = sem("states_ready"), sem("states_out")
        g_scalar, g_vector, g_ready, g_summed = sem("g_scalar"), sem("g_vector"), sem("g_ready"), sem("g_summed")
        s_act, s_vec, s_pool = sem("act_step"), sem("vec_step"), sem("pool_step")
        g_cols, col_scales = sem("g_cols"), sem("col_scales")
        small_saved = sem("small_saved")

        def both(z, n, each=1):
            turns, rest = divmod(n - 1, each)
            return (2 * turns + z) * each + rest + 1

        def pair(name):
            return [sem(f"{name}{z}") for z in range(2)]

        rep_ready, spread, eG_ready, D_ready, DT_ready = sem("rep_ready"), sem("spread"), sem("eG_ready"), sem("D_ready"), sem("DT_ready")
        kb_ready, scored, rows_done, A_ready, rows_scaled = (
            sem("kb_ready"), sem("scored"), sem("rows_done"), sem("A_ready"), sem("rows_scaled"))
        XT0_ready, X0_done, X0_ready, BT_ready, T1_done, T1_ready, T2_done, X_ready = (
            sem("XT0_ready"), sem("X0_done"), sem("X0_ready"), sem("BT_ready"), sem("T1_done"), sem("T1_ready"),
            sem("T2_done"), sem("X_ready"))
        wT_done, wT_ready, vn_done, vn_ready, S_done, S_ready, o_done, o_ready = (
            sem("wT_done"), sem("wT_ready"), sem("vn_done"), sem("vn_ready"), sem("S_done"), sem("S_ready"),
            sem("o_done"), sem("o_ready"))
        finals_out = sem("finals_out")
        s0_in, wout_in = sem("s0_in"), sem("wout_in")
        ds_vec, ds_prod, ds_act, ds_row, ds_rowed, ds_diag = (
            sem("ds_vec"), sem("ds_prod"), sem("ds_act"), sem("ds_row"), sem("ds_rowed"), sem("ds_diag"))
        s0_decayed, s0_outer, s0_ready = sem("s0_decayed"), sem("s0_outer"), sem("s0_ready")
        osq_ready, osum_done, mean_done, xc_ready, oroot_ready, onorm_ready, ospread, oscaled = (
            sem("osq_ready"), sem("osum_done"), sem("mean_done"), sem("xc_ready"), sem("oroot_ready"),
            sem("onorm_ready"), sem("ospread"), sem("oscaled"))
        bnorm_ready, btanh_ready, yb_ready = sem("bnorm_ready"), sem("btanh_ready"), sem("yb_ready")
        wout_done, x1_ready, x1_squared, r2_ready = sem("wout_done"), sem("x1_ready"), sem("x1_squared"), sem("r2_ready")
        h2_ready, h2_turned, h2T_ready, logits_done, logits_ready, h2_stored = (
            sem("h2_ready"), sem("h2_turned"), sem("h2T_ready"), sem("logits_done"), sem("logits_ready"), pair("h2_stored"))
        rt_vec, rt_act, routed, ranked = sem("rt_vec"), sem("rt_act"), sem("routed"), sem("ranked")
        tab_written, slots_in, idx_ready = sem("tab_written"), sem("slots_in"), sem("idx_ready")
        xg_in = pair("xg_in")
        y_out = [sem(f"y_out{n}") for n in range(4)]
        gidx_set, sidx_set, xg_turned, xT_ready = sem("gidx_set"), sem("sidx_set"), sem("xg_turned"), sem("xT_ready")
        up_done, up_tanh, act_half, act_ready, act_turned, aT_ready, down_done, y_ready = (
            sem("up_done"), sem("up_tanh"), sem("act_half"), sem("act_ready"), sem("act_turned"), sem("aT_ready"),
            sem("down_done"), sem("y_ready"))
        expert_done, moe_done = sem("expert_done"), sem("moe_done")
        m_rows = pair("more_rows")
        m_otok, m_osid, m_pe, m_act, m_vec, m_out, m_saved = (
            sem("more_" + n) for n in ("otok", "osid", "pe", "act", "vec", "out", "saved"))
        fin_added, fin_ready = sem("fin_added"), sem("fin_ready")
        wr_in, pool_passed = sem("wr_in"), sem("pool_passed")
        cleared = sem("cleared")

        block = ctx.enter_context(nc.Block())

        def linker(eng, semaphore):
            n = [0]

            def link(ins):
                n[0] += 1
                ins.then_inc(semaphore, 1)
                eng.wait_ge(semaphore, n[0])
            return link

        qk_index = {}
        for m, tile in enumerate(QKV):
            if tile < 8:
                qk_index[m] = len(qk_index)

        LAST_SUM = [ZQ + 3 + m for m, j in qk_index.items() if j % 4 == 3]
        SPREAD = [LAST_SUM[j // 4] + 2 + j % 4 for j in range(8)]

        def more_groups(eng, e, body):
            n = eng.value_load(more[0:1, bass.ds(e, 1)], min_val=0, max_val=MORE)
            with eng.If(n > 0):
                with eng.Fori(0, MORE) as g:
                    with eng.If(n > g):
                        body(g, eng.snap(groups_done[eng]), n)
                        eng.reg_add(groups_done[eng], groups_done[eng], 1)

        groups_done = {}

        def count_groups(eng, name):
            groups_done[eng] = eng.alloc_register(f"groups_done_{name}")
            eng.reg_mov(groups_done[eng], 0)

        ROUND = 4
        ROUNDS = NE // ROUND

        def rounds(eng, body):
            body(0, True, False)
            with eng.Fori(1, ROUNDS - 1) as it:
                body(it, False, False)
            body(ROUNDS - 1, False, True)

        def rest_of_tokens(eng, i):
            eng.wait_ge(h_hi, i + 1)
            eng.tensor_tensor(hlo[:, :, tokens(i)], hT[:, :, tokens(i)], hhi[:, :, tokens(i)], ALU.subtract).then_inc(h_lo, 1)

        @block.sync
        def _(sp):
            xp = A["x_prompt"].rearrange("o (i p) d -> (o i) p d", p=P)
            w_in_cols = A["w_in"].rearrange("o (p c) e -> (o p) c e", c=KT)

            def load_tile(n):
                if n >= WSLOTS:
                    sp.wait_ge(z_done, n - WSLOTS + 1)
                column = BLOCKS[n // 2] * 256 + n % 2 * P
                sp.dma_start(wraw[n % WSLOTS][:, :, :], w_in_cols[:, :, column:column + P]).then_inc(weights_in[n % WSLOTS], 16)

            for i in range(TT):
                sp.dma_start(x[:, i, :], xp[i]).then_inc(x_in[i], 16)
            sp.dma_start(x[0:NS, TT, :], A["x_sample"].rearrange("b o d -> (b o) d")).then_inc(x_in[TT], 16)
            sp.dma_start(g1c[:, :], A["norm1_g"].rearrange("o (p c) -> (o p) c", c=KT)).then_inc(g1_in, 16)
            sp.dma_start(cst[:, :], A["consts"]).then_inc(consts_in, 16)
            for n in range(WSLOTS):
                load_tile(n)
            for dst, src in (
                (rowq[0:WC, :], A["conv_c_w"][0]),
                (rowq[WC:ROWS_Q, :], A["state_conv_qkv"].rearrange("o b j e -> (o b j) e")),
                (rowab[0:WB, :], A["conv_b_w"][0]),
                (rowab[LNG:LNG + 1, :], A["ln_b_g"]),
                (rowab[LNB:LNB + 1, :], A["ln_b_b"]),
                (rowab[CAW:STA, :], A["conv_a_w"][0]),
                (rowab[STA:ROWS_AB, :], A["state_conv_a"].rearrange("o b j e -> (o b j) e")),
                (rowsb[:, :, :], A["state_conv_b"].rearrange("o (a b) j e -> (o b j) a e", a=2)),
            ):
                sp.dma_start(dst, src).then_inc(rows_in, 16)
            for dst, src in (
                (wba[:, :, :], w_in_cols[:, :, 3328:3336]),
                (ogc[:, :], A["o_norm_g"].rearrange("o p -> p o")),
                (alog[:, :], A["a_log"].broadcast_to([P, H])),
                (dtb[:, :], A["dt_bias"].broadcast_to([P, H])),
                (gfb[:, :], A["final_g"].unsqueeze(0).broadcast_to([P, D])),
            ):
                sp.dma_start(dst, src).then_inc(small_in, 16)
            for n in range(WSLOTS, NZ):
                load_tile(n)
            w_router = A["w_router"][0]
            sp.dma_start(wr[:, :, 0:NG], A["w_group"].rearrange("o (p c) g -> (o p) c g", c=KT)).then_inc(wr_in, 16)
            for g in range(NG):
                sp.dma_start(wr[:, :, NG + g * EG:NG + (g + 1) * EG], w_router[g].rearrange("(p c) e -> p c e", c=KT)).then_inc(
                    wr_in, 16)
            sp.wait_ge(cleared, 3)
            sp.dma_start(tab.rearrange("(p n) o -> p (n o)", p=P), nowhere[:, :]).then_inc(slots_in, 16)
            sp.wait_ge(z_done, NZ)
            sp.wait_ge(cv_done, CQ)
            sp.wait_ge(raw_saved, 3 + 2 * CQ)
            for h in range(H):
                sp.dma_start(s0[:, h], A["state_delta"][0, :, h].rearrange("b k v -> k b v")).then_inc(s0_in, 16)
            sp.dma_start(wout[:, :, :], A["w_out"].rearrange("o (k p) d -> (o p) k d", p=P)).then_inc(wout_in, 16)
            sp.dma_start(g2b[:, :], A["norm2_g"].broadcast_to([P, D])).then_inc(wout_in, 16)
            w_gu = [A[n].rearrange("o e (p c) f -> (o e) p c f", c=KT) for n in ("w_gate", "w_up")]
            w_down = A["w_down"].rearrange("o e (c p) d -> (o e) p c d", c=2)

            def load_expert(e, u):
                for n in range(2):
                    sp.dma_start(gu[u][:, n], w_gu[n][bass.ds(e, 1)].rearrange("o p c f -> (o p) c f")).then_inc(weights_in[u], 16)
                sp.dma_start(wd[u][:, :, :], w_down[bass.ds(e, 1)].rearrange("o p c d -> (o p) c d")).then_inc(weights_in[u], 16)

            for z in range(2):
                sp.wait_ge(S_ready, both(z, 2 * TT))
                sp.wait_ge(o_ready, both(z, 2))
            load_expert(1, 1)
            sp.dma_start(R["d_p"][0, 0].rearrange("h k v -> k h v"), sfin[:, :, :]).then_inc(finals_out, 16)
            sp.wait_ge(finals_out, 16)
            sp.wait_ge(states_ready, 4)
            for dst, src in (
                (R["cq_p"][0, 0], rowq2[0:3, :]),
                (R["cq_s"].rearrange("o b j e -> (o b j) e"), rowq2[3:27, :]),
                (R["ca_p"][0, 0], rowab2[0:2, :]),
                (R["ca_s"].rearrange("o b j e -> (o b j) e"), rowab2[2:18, :]),
                (R["cb_p"][0, 0], rowb[:, :]),
                (R["cb_s"].rearrange("o (a b) j e -> (o b j) a e", a=2), rowsb2[:, :, :]),
            ):
                sp.dma_start(dst, src).then_inc(states_out, 16)
            sp.wait_ge(oscaled, 5)
            load_expert(0, 0)
            for i in range(NT):
                n = P if i < TT else NS
                if 1 <= i <= H:
                    sp.wait_ge(s0_ready, 2 * i)
                    sp.dma_start(R["d_s"][0, :, i - 1].rearrange("b k v -> k b v"), s0[:, i - 1]).then_inc(finals_out, 16)
                sp.wait_ge(h2_ready, i + 1)
                if i == NT - 1:
                    load_expert(2, 2)
                    sp.wait_ge(finals_out, (H + 1) * 16)
                    sp.wait_ge(wout_done, NT)
                    load_expert(3, 3)
                sp.dma_start(h2d[i * P:i * P + n, :], h2row[i % 2][0:n].rearrange("t c p -> t (c p)")).then_inc(h2_stored[i % 2], 16)
            sp.wait_ge(tab_written, 2 * NT * 16)
            slots = tab.rearrange("(r e) o -> r (e o)", e=NE)[0:CAP]
            sp.dma_start(graw[0:CAP, :], slots[:, 0:NE // 2]).then_inc(slots_in, 16)
            sp.dma_start(graw[CAP:P, :], slots[:, NE // 2:NE]).then_inc(slots_in, 16)
            for half in range(2):
                sp.dma_start(sraw[half * CAP:(half + 1) * CAP, :], slots[:, :]).then_inc(slots_in, 16)
            for s in range(2):
                sp.wait_ge(h2_stored[s], 16 * ((NT + 1 - s) // 2))
            sp.wait_ge(logits_done, NT)
            for half in range(2):
                sp.dma_start(oraw[half * CAP:(half + 1) * CAP], tab.rearrange("(g r e) o -> r g (e o)", r=CAP, e=NE)[:, 1:]).then_inc(
                    slots_in, 16)
            with sp.Fori(1, ROUNDS) as it:
                for u in range(ROUND):
                    sp.wait_ge(expert_done, ROUND * (it - 1) + u + 1)
                    load_expert(ROUND * it + u, u)
            sp.wait_ge(moe_done, 1)
            yrows = yd.rearrange("(r b) d -> r (b d)", b=2)
            for i in range(NT):
                n = P if i < TT else NS
                for k in range(2):
                    sp.dma_start(yk[i][0:n, k, :], yrows[k * T + i * P:k * T + i * P + n]).then_inc(x_in[i], 16)
            for i in range(NT):
                n = P if i < TT else NS
                sp.wait_ge(fin_ready, i + 1)
                dst = R["y_p"][0, i * P:(i + 1) * P, :] if i < TT else R["y_s"].rearrange("b o d -> (b o) d")
                sp.dma_start(dst, x[0:n, i, :]).then_inc(finals_out, 16)
            sp.wait_ge(finals_out, (H + 1 + NT) * 16)

        @block.scalar
        def _(act):
            link = linker(act, s_act)
            copy = nc.scalar.activation

            for i in range(NT):
                act.wait_ge(x_in[i], 16)
                n = P if i < TT else NS
                if i == 0:
                    act.wait_ge(cleared, 1)
                if i >= 2:
                    act.wait_ge(x_squared, i - 1)
                copy(yT[0:n, 2 * (i % 2):2 * (i % 2) + 2, 0:512], x[0:n, i, :].rearrange("p (a b) -> p a b", a=2), ACT.Square,
                     accum_out=ss[0:n, i:i + 1]).then_inc(x_squared, 1)
            act.wait_ge(x_squared, NT)
            act.wait_ge(cleared, 2)
            copy(ss[:, :], ss[:, :], ACT.Sqrt, scale=1.0 / D, bias=epsc[:, :]).then_inc(x_squared, 1)
            def round_tokens(i):
                act.wait_ge(hT_ready, i + 1)
                copy(hhi[:, :, tokens(i)], hT[:, :, tokens(i)], ACT.Copy).then_inc(h_hi, 1)

            def round_weights(n):
                act.wait_ge(weights_in[n % WSLOTS], 16 * (n // WSLOTS + 1))
                copy(whi[n % WSLOTS][:, :, :], wraw[n % WSLOTS][:, :, :], ACT.Copy).then_inc(w_hi, 1)

            for i in range(NT):
                round_tokens(i)
                if i < WSLOTS - 1:
                    round_weights(i)
            def decays():
                act.wait_ge(ba_done, 1)
                act.wait_ge(cleared, 4)
                copy(ba[:, 0:TT, :], ps[:, 7, 0:TT * 8].rearrange("p (i e) -> p i e", e=8), ACT.Copy).then_inc(ba_ready, 1)
                copy(ba[0:NS, TT, :], ps[0:NS, 7, TT * 8:NT * 8], ACT.Copy).then_inc(ba_ready, 1)
                act.wait_ge(ba_ready, 2)
                act.wait_ge(small_in, 5 * 16)
                copy(gw[:, 0, :, :], ba[:, :, 0:4], ACT.Exp, scale=-1.0).then_inc(g_scalar, 1)
                copy(gw[:, 9, 0, :], alog[:, :], ACT.Exp).then_inc(g_scalar, 1)
                act.wait_ge(g_vector, 1)
                copy(gw[:, 3, :, :], gw[:, 2, :, :], ACT.Exp, scale=-1.0).then_inc(g_scalar, 1)
                act.wait_ge(g_vector, 2)
                copy(gw[:, 5, :, :], gw[:, 4, :, :], ACT.Ln).then_inc(g_scalar, 1)

            def evacuate(n):
                act.wait_ge(z_done, n + 1)
                b = 2 * (n % 2)
                prompt, sample = ps[:, b:b + 2, 0:256], ps[:, b + 1, 256:264]
                f, scale = ACT.Copy, 1.0
                if n < 2:
                    dst, scale = bval[n], 0.5
                elif n < 4:
                    dst, f, scale = bth[n - 2], ACT.Tanh, 0.5
                elif n < ZQ:
                    dst = (mab, mac, mah)[(n - ZA) // 2][n % 2]
                elif n < ZG:
                    m = n - ZQ
                    if m == 0:
                        act.wait_ge(h_turned, NT)
                    dst = raw[m % 3]
                    if m >= 3:
                        act.wait_ge(conv_done, m - 2)
                        act.wait_ge(raw_saved, 3 + 2 * (m - 2))
                    else:
                        act.wait_ge(raw_saved, 3)
                    act.wait_ge(params_ready, 3)
                    link(copy(dst[:, WC - 1 + SEQ:RAW].rearrange("p (b j) -> p b j", j=WC)[:, :, 0:WC - 1],
                              parq[:, QKV[m], WC:ROWS_Q].rearrange("p (b j) -> p b j", j=WC - 1), ACT.Copy))
                    copy(dst[:, WC - 1:WC - 1 + SEQ].rearrange("p (a b) -> p a b", a=2), prompt, ACT.Copy)
                    copy(dst[:, WC - 1 + SEQ:RAW].rearrange("p (b j) -> p b j", j=WC)[:, :, WC - 1:WC],
                         sample.unsqueeze(2), ACT.Copy).then_inc(z_evac, 1)
                    return
                else:
                    g = n - ZG
                    if g == 0:
                        act.wait_ge(a_mixed, 2)
                    yg = yT[:, 4 + g, :]
                    link(copy(yg[:, 0:SEQ].rearrange("p (a b) -> p a b", a=2), prompt, ACT.Copy))
                    link(copy(yg[:, SEQ:T], sample, ACT.Copy))
                    dst, f, scale = th[g % 2], ACT.Tanh, 0.5
                    if g < 2:
                        act.wait_ge(cv_done, CQ)
                    else:
                        act.wait_ge(gate_tanh, g - 1)
                copy(dst[:, 0:SEQ].rearrange("p (a b) -> p a b", a=2), prompt, f, scale=scale)
                copy(dst[:, SEQ:T], sample, f, scale=scale).then_inc(z_evac, 1)

            def tanh(m):
                act.wait_ge(conv_done, m + 1)
                if m >= 2:
                    act.wait_ge(cv_done, m - 1)
                copy(th[m % 2][:, :], acc[m % 3][:, :], ACT.Tanh, scale=0.5).then_inc(tanh_done, 1)

            def square(m):
                if QKV[m] >= 8:
                    return
                j = qk_index[m]
                act.wait_ge(cv_done, m + 1)
                if j >= 2:
                    act.wait_ge(sums_done, j - 1)
                copy(sq[j % 2][:, :], cv[QKV[m]][:, :], ACT.Square).then_inc(squared, 1)

            def root(g):
                act.wait_ge(sums_done, 4 * g + 4)
                if g:
                    act.wait_ge(norms_ready, g)
                copy(rn[:, 0, :].rearrange("p (a b) -> p a b", a=2), ps[0:8, 4:6, 0:HC], ACT.Sqrt, scale=0.25,
                     bias=epsc[0:8, :]).then_inc(sums_ready, 1)

            for n in range(NZ + 3):
                if 0 <= n - ZQ - 1 < CQ:
                    tanh(n - ZQ - 1)
                if 0 <= n - ZQ - 2 < CQ:
                    square(n - ZQ - 2)
                if n < NZ:
                    evacuate(n)
                if n + WSLOTS - 1 < NZ:
                    round_weights(n + WSLOTS - 1)
                if n == 3:
                    decays()
                for g in range(2):
                    if n == LAST_SUM[g] + 1:
                        root(g)

            act.wait_ge(g_summed, 1)
            act.wait_ge(g_ready, 2)
            copy(nG[:, 0:TT], ps[:, 6, 0:TT * H].rearrange("p (i h) -> p i h", h=H), ACT.Copy, scale=-1.0).then_inc(g_cols, 1)
            copy(eGc[:, 0:TT], ps[:, 6, 0:TT * H].rearrange("p (i h) -> p i h", h=H), ACT.Exp).then_inc(g_cols, 1)
            act.wait_ge(g_cols, 2)
            act.wait_ge(qk_ready, len(qk_index))
            for hp in range(2):
                pairs = [(z, 2 * hp + z, 4 * z) for z in range(2)]
                for z, h, B in pairs:
                    act.wait_ge(spread, both(z, 2 * hp + 1, 2))
                    act.wait_ge(rep_ready, both(z, 2 * hp + 2, 2))
                    copy(eG[z][:, :, :].rearrange("p a b -> p (a b)"), ps[:, B, :], ACT.Exp).then_inc(eG_ready, 1)
                for z, h, B in pairs:
                    act.wait_ge(D_ready, both(z, 2 * hp + 2, 2))
                    for i in range(TT):
                        copy(DT[z][:, i, :], DT[z][:, i, :], ACT.Exp, bias=nG[:, i, h:h + 1]).then_inc(DT_ready, 1)
                    copy(kds[:, 0:TT, h], gdif[:, 0:TT, h], ACT.Exp).then_inc(DT_ready, 1)
                for z, h, B in pairs:
                    act.wait_ge(X0_done, both(z, hp + 1))
                    copy(XX[z][:, 0].rearrange("p a b -> p (a b)"), ps[:, B + 2, :], ACT.Copy).then_inc(X0_ready, 1)
                for n in range(1, LEVELS):
                    for z, h, B in pairs:
                        act.wait_ge(T1_done, both(z, (LEVELS - 1) * hp + n))
                        copy(t1[z][:, :, :].rearrange("p a b -> p (a b)"), ps[:, B + 2, :], ACT.Copy).then_inc(T1_ready, 1)
                for z, h, B in pairs:
                    act.wait_ge(wT_done, both(z, hp + 1))
                    copy(wT[z][:, :, :].rearrange("p a b -> p (a b)"), ps[:, B + 2, :], ACT.Copy).then_inc(wT_ready, 1)
                for i in range(TT):
                    for z, h, B in pairs:
                        act.wait_ge(vn_done, both(z, TT * hp + i + 1))
                        copy(vn[z][:, i, :], ps[:, B + 3, i * P:(i + 1) * P], ACT.Copy).then_inc(vn_ready, 1)
                for z, h, B in pairs:
                    act.wait_ge(o_done, both(z, hp + 1))
                    act.wait_ge(small_saved, 2)
                    copy(cv[8 + h][:, 0:SEQ], ps[:, B + 1, :], ACT.Copy).then_inc(o_ready, 1)

            act.wait_ge(rows_turned, 4)
            copy(rowq2[:, :].rearrange("p (a b) -> p a b", a=3), ps[0:27, 5:8, :], ACT.Copy).then_inc(states_ready, 1)
            act.wait_ge(rows_turned, 5)
            copy(rowab2[:, :], ps[0:18, 7, 0:DB], ACT.Copy).then_inc(states_ready, 1)
            copy(rowb[:, :], ps[0:WB - 1, 7, DB:2 * DB], ACT.Copy).then_inc(states_ready, 1)
            act.wait_ge(rows_turned, 6)
            copy(rowsb2[:, :, :].rearrange("p a b -> p (a b)"), ps[0:120, 7, :], ACT.Copy).then_inc(states_ready, 1)
            act.wait_ge(ds_prod, 1)
            copy(kqs[:, :, :].rearrange("p a b -> p (a b)"), ps[:, 0, 0:2 * H * NS], ACT.Copy).then_inc(ds_act, 1)
            act.wait_ge(ds_prod, 3)
            copy(sb[:, 1, :], ps[:, 1, 0:H * NS], ACT.Copy).then_inc(ds_act, 1)
            copy(sb[:, 2, :], ps[:, 2, 0:H * NS], ACT.Exp).then_inc(ds_act, 1)
            copy(sb[:, 3, :], ps[:, 2, H * NS:2 * H * NS], ACT.Copy).then_inc(ds_act, 1)
            act.wait_ge(ds_row, 1)
            copy(srow[:, 0, :], ps[0:NS, 3, :], ACT.Copy).then_inc(ds_rowed, 1)
            copy(srow[:, 1, :], ps[0:NS, 4, :], ACT.Copy).then_inc(ds_rowed, 1)
            for n in range(6):
                if n >= 2:
                    act.wait_ge(osum_done, n - 1)
                if n == 0:
                    act.wait_ge(ds_vec, 8)
                if n >= 4:
                    act.wait_ge(xc_ready, 2)
                    copy(osq[n % 2][:, :], yT[:, n - 2, :], ACT.Square, scale=0.5 ** 0.5).then_inc(osq_ready, 1)
                else:
                    copy(osq[n % 2][:, :], cv[8 + n][:, 0:T], ACT.Square).then_inc(osq_ready, 1)
            act.wait_ge(osum_done, 6)
            copy(rno[:, 0, :].rearrange("p (a b) -> p a b", a=2), ps[0:8, 1:3, 0:HT], ACT.Sqrt, scale=1.0 / P,
                 bias=epsc[0:8, :]).then_inc(oroot_ready, 1)
            for t in range(2):
                act.wait_ge(bnorm_ready, t + 1)
                copy(bth2[t][:, :], yT[:, 2 + t, :], ACT.Tanh).then_inc(btanh_ready, 1)

            def square_x1(i):
                n = P if i < TT else NS
                act.wait_ge(x1_ready, i + 1)
                if i == 0:
                    act.wait_ge(yb_ready, 2)
                    act.wait_ge(x_squared, NT)
                if i >= 1:
                    act.wait_ge(h2T_ready, i)
                copy(sqj[0:n, :], x[0:n, i, :], ACT.Square, accum_out=ss[0:n, i:i + 1]).then_inc(x1_squared, 1)
                act.wait_ge(x1_squared, 2 * i + 1)
                copy(ss[0:n, i:i + 1], ss[0:n, i:i + 1], ACT.Sqrt, scale=1.0 / D, bias=epsc[0:n, :]).then_inc(x1_squared, 1)

            def evacuate_h2(i):
                n = P if i < TT else NS
                act.wait_ge(h2_turned, i + 1)
                if i >= 1:
                    act.wait_ge(logits_done, i)
                copy(h2T[:, :, 0:n], ps[:, 4:6, :].rearrange("p b (c t) -> p (b c) t", t=P)[:, :, 0:n], ACT.Copy).then_inc(
                    h2T_ready, 1)

            for i in range(NT):
                square_x1(i)
                evacuate_h2(i)
            act.wait_ge(logits_done, NT)
            act.wait_ge(cleared, 5)
            copy(L[:, 0:TT, :], ps[:, 6, 0:TT * (NG + NE)].rearrange("p (i e) -> p i e", i=TT), ACT.Copy).then_inc(logits_ready, 1)
            copy(L[0:NS, TT, :], ps[0:NS, 6, TT * (NG + NE):NT * (NG + NE)], ACT.Copy).then_inc(logits_ready, 1)
            act.wait_ge(rt_vec, 1)
            copy(g4[:, 1], g4[:, 0], ACT.Exp).then_inc(rt_act, 1)
            act.wait_ge(rt_vec, 2)
            copy(ns[:, 5], ns[:, 4], ACT.Exp).then_inc(rt_act, 1)
            count_groups(act, "act")
            act.wait_ge(routed, 4)
            act.wait_ge(ranked, 1)

            def act_round(it, first, last):
                for u in range(ROUND):
                    e = ROUND * it + u
                    if u == 1 or (u == 3 and not last):
                        xT_out(2 * it + (u + 1) // 2, (u + 1) // 2 % 2)
                    if u < 3:
                        if u == 0:
                            tanh_gate(e, 0)
                        tanh_gate(e + 1, (u + 1) % 2)
                    act_T(e, u % 2)

                    def body(g, done, needed):
                        act.wait_ge(m_pe, done * 4 + 1)
                        copy(xTo[:, :, :].rearrange("p a b -> p (a b)"), ps[:, 3, :], ACT.Copy).then_inc(m_act, 1)
                        act.wait_ge(m_pe, done * 4 + 2)
                        copy(oth[:, :], ps[:, 3, 0:P], ACT.Tanh, scale=0.5).then_inc(m_act, 1)
                        act.wait_ge(m_pe, done * 4 + 3)
                        copy(oaT[:, :], ps[:, 3, 0:P], ACT.Copy).then_inc(m_act, 1)

                    more_groups(act, e, body)

            def xT_out(j, s):
                act.wait_ge(xg_turned, j + 1)
                copy(xT[s][:, :, :], ps[:, 6:8, :].rearrange("p b (c t) -> p (b c) t", t=P), ACT.Copy).then_inc(xT_ready, 1)

            def tanh_gate(e, s):
                act.wait_ge(up_done, e + 1)
                copy(gth[s][:, :], ps[:, s, 0:P], ACT.Tanh, scale=0.5).then_inc(up_tanh, 1)

            def act_T(e, s):
                act.wait_ge(act_turned, e + 1)
                copy(aT[s][:, :], ps[:, 2, 0:P], ACT.Copy).then_inc(aT_ready, 1)

            xT_out(0, 0)
            rounds(act, act_round)
            for i in range(NT):
                n = P if i < TT else NS
                act.wait_ge(fin_added, 2 * i + 2)
                if i:
                    act.wait_ge(x1_squared, 2 * (NT + i))
                copy(fsq[0:n, :], x[0:n, i, :], ACT.Square, accum_out=ss[0:n, i:i + 1]).then_inc(x1_squared, 1)
                act.wait_ge(x1_squared, 2 * (NT + i) + 1)
                copy(ss[0:n, i:i + 1], ss[0:n, i:i + 1], ACT.Sqrt, scale=1.0 / D, bias=epsc[0:n, :]).then_inc(x1_squared, 1)

        @block.gpsimd
        def _(pool):
            link = linker(pool, s_pool)
            nc.gpsimd.memset(ss[:, :], 1.0).then_inc(cleared, 1)
            nc.gpsimd.memset(epsc[:, :], EPS).then_inc(cleared, 1)
            nc.gpsimd.memset(nowhere[:, :], NOWHERE).then_inc(cleared, 1)
            nc.gpsimd.memset(ba[:, :, :], 0.0).then_inc(cleared, 1)
            for r in raw:
                nc.gpsimd.memset(r[:, 0:WC - 1], 0.0).then_inc(raw_saved, 1)
            for t in range(2):
                link(nc.gpsimd.memset(ub[t][:, 0:WB - 1], 0.0))
                link(nc.gpsimd.memset(ua[t][:, 0:WA - 1], 0.0))
            for i in range(2):
                rest_of_tokens(pool, i)

            def rest_of_weights(n):
                pool.wait_ge(w_hi, n + 1)
                s = n % WSLOTS
                nc.gpsimd.tensor_tensor(wlo[s][:, :, :], wraw[s][:, :, :], whi[s][:, :, :], ALU.subtract).then_inc(w_lo, 1)

            def glu():
                pool.wait_ge(z_evac, ZA)
                for t in range(2):
                    for out, c in ((ub[t][:, WB - 1:], slice(0, SEQ)), (usb[:, t, :, WB - 1], slice(SEQ, T))):
                        link(nc.gpsimd.tensor_tensor(bth[t][:, c], bth[t][:, c], bval[t][:, c], ALU.mult))
                        nc.gpsimd.tensor_tensor(out, bth[t][:, c], bval[t][:, c], ALU.add).then_inc(glu_ready, 1)
                pool.wait_ge(glu_ready, 4)
                pool.wait_ge(params_ready, 3)
                nc.gpsimd.tensor_copy(stp[:, 0, :], ub[0][:, SEQ:]).then_inc(glu_ready, 1)
                nc.gpsimd.tensor_copy(stp[:, 1, :], ub[1][:, SEQ:]).then_inc(glu_ready, 1)
                for t in range(2):
                    nc.gpsimd.tensor_copy(stb[:, t, :].rearrange("p (b j) -> p b j", j=WB - 1), usb[:, t, :, 1:WB]).then_inc(
                        glu_ready, 1)

            def mix_a(t, step):
                parts = ((slice(0, SEQ), lambda j: ua[t][:, j:j + SEQ]), (slice(SEQ, T), lambda j: uas[:, t, :, j]))
                if step == 0:
                    pool.wait_ge(z_evac, ZA + 5 + t)
                    link(nc.gpsimd.tensor_copy(uas[:, t, :, 0:WA - 1],
                                               parab[:, t, STA:ROWS_AB].rearrange("p (b j) -> p b j", j=WA - 1)))
                    link(nc.gpsimd.tensor_tensor(ua[t][:, WA - 1:], mac[t][:, 0:SEQ], mah[t][:, 0:SEQ], ALU.mult))
                    link(nc.gpsimd.tensor_tensor(uas[:, t, :, WA - 1], mac[t][:, SEQ:T], mah[t][:, SEQ:T], ALU.mult))
                    link(nc.gpsimd.tensor_copy(sta[:, t, 0:WA - 1], ua[t][:, SEQ:SEQ + WA - 1]))
                    link(nc.gpsimd.tensor_copy(sta[:, t, WA - 1:].rearrange("p (b j) -> p b j", j=WA - 1), uas[:, t, :, 1:WA]))
                    for c, u in parts:
                        link(nc.gpsimd.tensor_scalar(yT[:, t, c], u(0), parab[:, t, CAW:CAW + 1], None, ALU.mult))
                    return
                for c, u in parts:
                    link(nc.gpsimd.tensor_scalar(mac[t][:, c], u(step), parab[:, t, CAW + step:CAW + step + 1], None, ALU.mult))
                    link(nc.gpsimd.tensor_tensor(yT[:, t, c], yT[:, t, c], mac[t][:, c], ALU.add))
                if step == WA - 1:
                    nc.gpsimd.tensor_tensor(yT[:, t, :], yT[:, t, :], mab[t][:, :], ALU.mult).then_inc(a_mixed, 1)

            def save_columns(m):
                pool.wait_ge(z_evac, ZQ + m + 1)
                r, s = raw[m % 3], stq[:, QKV[m], :]
                nc.gpsimd.tensor_copy(s[:, 0:WC - 1], r[:, SEQ:SEQ + WC - 1]).then_inc(raw_saved, 1)
                nc.gpsimd.tensor_copy(s[:, WC - 1:].rearrange("p (b j) -> p b j", j=WC - 1),
                                      r[:, WC - 1 + SEQ:].rearrange("p (b j) -> p b j", j=WC)[:, :, 1:]).then_inc(raw_saved, 1)

            for n in range(NZ):
                rest_of_weights(n)
                done = n - WSLOTS + 1
                if done == ZA - 1:
                    glu()
                if 0 <= done - ZQ + 1 < 2 * WA:
                    mix_a(*divmod(done - ZQ + 1, WA))
                if 0 <= done - ZQ < CQ:
                    save_columns(done - ZQ)
            pool.wait_ge(qk_ready, len(qk_index))
            pool.wait_ge(cv_done, CQ)
            for h in range(H):
                for j, tile in enumerate((4 + h, h)):
                    link(nc.gpsimd.tensor_copy(kq[:, h, :, j], cv[tile][:, SC:CV:WC]))
            for n in range(CQ):
                ins = nc.gpsimd.tensor_copy(small[:, n, :], cv[n][:, SC:CV:WC])
                if n < CQ - 1:
                    link(ins)
            ins.then_inc(small_saved, 2)
            pool.wait_ge(ds_act, 4)
            for h in range(H):
                nc.gpsimd.tensor_tensor(s0[:, h], s0[:, h], bcast(sb[:, 2, h * NS:(h + 1) * NS], P), ALU.mult).then_inc(s0_decayed, 1)
            pool.wait_ge(yb_ready, 2)
            nc.gpsimd.memset(L[:, :, :], 0.0).then_inc(cleared, 1)
            pool.wait_ge(slots_in, 16)
            pool.wait_ge(routed, 3)
            for n in range(2):
                for i in range(NT):
                    nc.gpsimd.indirect_dma_start(out=tab, out_offset=bass.IndirectOffsetOnAxis(ap=where[:, n, i:i + 1], axis=0),
                                                 in_=pid[:, n, i:i + 1], in_offset=None, bounds_check=MAXROWS * NE - 1,
                                                 oob_is_err=False).then_inc(tab_written, 16)
            count_groups(pool, "pool")
            otok_set = pool.alloc_register("otok_set")
            pool.reg_mov(otok_set, 0)
            pool.sem_inc(m_saved, 1)
            pool.wait_ge(routed, 4)
            for s in range(2):
                pool.wait_ge(h2_stored[s], 16 * ((NT + 1 - s) // 2))
            for t in (*xg, *xo, zero):
                nc.gpsimd.memset(t[:, :], 0).then_inc(cleared, 1)
            pool.wait_ge(cleared, 10)
            pool.wait_ge(idx_ready, 2)

            def gather(j, s):
                nc.gpsimd.tensor_tensor(gcur[s][:, :], gidx[:, bass.ds(j, 1)], zero[:, :], ALU.add).then_inc(gidx_set, 1)
                pool.wait_ge(gidx_set, j + 1)
                pool.sem_inc(pool_passed, 1)
                nc.gpsimd.indirect_dma_start(out=xg[s][:, :], out_offset=None, in_=h2d,
                                             in_offset=bass.IndirectOffsetOnAxis(ap=gcur[s][:, 0:1], axis=0),
                                             bounds_check=T - 1, oob_is_err=False).then_inc(xg_in[s], 16)

            def pool_round(it, first, last):
                for u in range(ROUND):
                    e = ROUND * it + u
                    if u % 2 == 0 and not last:
                        j = 2 * it + u // 2 + 2
                        pool.wait_ge(xg_turned, j - 1)
                        gather(j, u // 2)
                    column = 2 * it + u // 2 + u % 2 * (NE // 2)
                    if not first:
                        pool.wait_ge(y_out[u], 16 * it)
                    nc.gpsimd.tensor_tensor(scur[u][:, :], sidx[:, bass.ds(column, 1)], zero[:, :], ALU.add).then_inc(sidx_set, 1)
                    pool.wait_ge(sidx_set, e + 1)
                    pool.wait_ge(y_ready, e + 1)
                    pool.sem_inc(pool_passed, 1)
                    nc.gpsimd.indirect_dma_start(out=yd, out_offset=bass.IndirectOffsetOnAxis(ap=scur[u][:, 0:1], axis=0),
                                                 in_=ysb[u][:, :], in_offset=None, bounds_check=4 * T - 1,
                                                 oob_is_err=False).then_inc(y_out[u], 16)

                    def body(g, done, needed):
                        nc.gpsimd.tensor_tensor(osid[:, :], osids[:, bass.ds(g * NE + column, 1)], zero[:, :], ALU.add).then_inc(
                            m_osid, 1)
                        with pool.If(needed - 1 > g):
                            pool.wait_ge(m_pe, done * 4 + 1)
                            gather_more(g + 1, column, u % 2)
                        pool.wait_ge(m_osid, done + 1)
                        pool.wait_ge(m_vec, done * 3 + 3)
                        pool.sem_inc(pool_passed, 1)
                        nc.gpsimd.indirect_dma_start(out=yd, out_offset=bass.IndirectOffsetOnAxis(ap=osid[:, 0:1], axis=0),
                                                     in_=yo[:, :], in_offset=None, bounds_check=4 * T - 1,
                                                     oob_is_err=False).then_inc(m_out, 16)
                        pool.wait_ge(m_out, done * 16 + 16)
                        pool.sem_inc(m_saved, 1)

                    more_groups(pool, e, body)
                    if not (last and u >= 2):
                        first_further(e + 2, column + 1, u % 2)

            def gather_more(g, column, s):
                nc.gpsimd.tensor_tensor(otok[s][:, :], otoks[:, bass.ds(g * NE + column, 1)], zero[:, :], ALU.add).then_inc(
                    m_otok, 1)
                pool.reg_add(otok_set, otok_set, 1)
                pool.wait_ge(m_otok, pool.snap(otok_set))
                pool.sem_inc(pool_passed, 1)
                nc.gpsimd.indirect_dma_start(out=xo[s][:, :], out_offset=None, in_=h2d,
                                             in_offset=bass.IndirectOffsetOnAxis(ap=otok[s][0:CAP, 0:1], axis=0),
                                             bounds_check=T - 1, oob_is_err=False).then_inc(m_rows[s], 16)

            def first_further(e, column, s):
                with pool.If(pool.value_load(more[0:1, bass.ds(e, 1)], min_val=0, max_val=MORE) > 0):
                    gather_more(0, column, s)

            for s in range(2):
                gather(s, s)
            pool.wait_ge(idx_ready, 4)
            for s in range(2):
                first_further(s, s * (NE // 2), s)
            rounds(pool, pool_round)
            for u in range(ROUND):
                pool.wait_ge(y_out[u], 16 * ROUNDS)
            pool.sem_inc(moe_done, 1)

        @block.vector
        def _(vec):
            link = linker(vec, s_vec)
            stt = nc.vector.scalar_tensor_tensor
            def scale_rows(i):
                n = P if i < TT else NS
                if i >= 2:
                    vec.wait_ge(h_turned, i - 1)
                nc.vector.tensor_scalar(hrow[i % 2][0:n].rearrange("t c p -> t p c"), x[0:n, i, :].rearrange("t (p c) -> t p c", c=KT),
                                        rstd[0:n, i:i + 1], None, ALU.mult).then_inc(hrow_ready, 1)

            def evacuate_h(i):
                n = P if i < TT else NS
                vec.wait_ge(h_turned, i + 1)
                b = 2 * (i % 2)
                nc.vector.tensor_tensor(hT[:, :, tokens(i)], ps[:, b:b + 2, :].rearrange("p b (c t) -> p (b c) t", t=P)[:, :, 0:n],
                                        bcast(g1c[:, :], n), ALU.mult).then_inc(hT_ready, 1)

            vec.wait_ge(g1_in, 16)
            vec.wait_ge(x_squared, NT + 1)
            nc.vector.reciprocal(rstd[:, :], ss[:, :]).then_inc(rstd_ready, 1)
            vec.wait_ge(rstd_ready, 1)
            for i in range(NT + 1):
                if i < NT:
                    scale_rows(i)
                if i >= 1:
                    evacuate_h(i - 1)
            for i in range(2, NT):
                rest_of_tokens(vec, i)

            for n, (dst, src) in enumerate((
                (parq[:, :, :], ps[:, 4, 0:CQ * ROWS_Q].rearrange("p (n r) -> p n r", n=CQ)),
                (parab[:, :, :], ps[:, 5, 0:2 * ROWS_AB].rearrange("p (n r) -> p n r", n=2)),
                (usb[:, :, :, 0:WB - 1], ps[:, 6, 0:480].rearrange("p (t b j) -> p t b j", t=2, b=NS)),
            )):
                vec.wait_ge(rows_turned, n + 1)
                if n == 2:
                    for t in range(2):
                        link(nc.vector.tensor_copy(dst[:, t], src[:, t]))
                    nc.vector.tensor_scalar(lnh[:, :, :], parab[:, :, LNG:LNB + 1], 0.5, None, ALU.mult).then_inc(params_ready, 1)
                else:
                    nc.vector.tensor_copy(dst, src).then_inc(params_ready, 1)
                vec.wait_ge(params_ready, n + 1)
            vec.wait_ge(small_in, 5 * 16)
            link(nc.vector.tensor_scalar(ogh[:, :], ogc[:, :], 0.5, None, ALU.mult))

            def rows_of(ap):
                return ap.unsqueeze(1).broadcast_to([P, NT, H])

            vec.wait_ge(ba_ready, 2)
            link(nc.vector.tensor_tensor(gw[:, 6], ba[:, :, 4:8], rows_of(dtb[:, :]), ALU.add))
            stt(out=gw[:, 2], in0=gw[:, 6], scalar=-1.0, in1=gw[:, 6], op0=ALU.mult, op1=ALU.max).then_inc(g_vector, 1)
            vec.wait_ge(g_scalar, 3)
            nc.vector.tensor_scalar(gw[:, 4], gw[:, 3], 1.0, None, ALU.add).then_inc(g_vector, 1)
            link(nc.vector.tensor_scalar(gw[:, 8], gw[:, 0], 1.0, None, ALU.add))
            nc.vector.reciprocal(gw[:, 1], gw[:, 8]).then_inc(g_ready, 1)
            vec.wait_ge(g_scalar, 4)
            vec.wait_ge(g_ready, 1)
            link(stt(out=gw[:, 8], in0=gw[:, 6], scalar=0.0, in1=gw[:, 5], op0=ALU.max, op1=ALU.add))
            stt(out=gw[:, 7], in0=gw[:, 8], scalar=-1.0, in1=rows_of(gw[:, 9, 0, :]), op0=ALU.mult,
                op1=ALU.mult).then_inc(g_ready, 1)

            vec.wait_ge(glu_ready, 4)
            for t in range(2):
                link(nc.vector.tensor_tensor(sprod[:, :, :], usb[:, t, :, :],
                                             parab[:, t, 0:WB].unsqueeze(1).broadcast_to([P, NS, WB]), ALU.mult))
                link(nc.vector.tensor_reduce(yT[:, 2 + t, SEQ:T], sprod[:, :, :], AX_X, ALU.add))
            def taps(start, end):
                for k in range(start, min(end, 2 * WB)):
                    j, t = divmod(k, 2)
                    y, tap = yT[:, 2 + t, 0:SEQ], ub[t][:, j:j + SEQ]
                    if j >= 1:
                        vec.wait_ge(b_conved, 2 * j + t - 1)
                    if j == 0:
                        ins = nc.vector.tensor_scalar(y, tap, parab[:, t, 0:1], None, ALU.mult)
                    else:
                        ins = stt(out=y, in0=tap, scalar=parab[:, t, j:j + 1], in1=y, op0=ALU.mult, op1=ALU.add)
                    ins.then_inc(b_conved, 1)

            taps(0, 36)

            def convolve(m):
                vec.wait_ge(z_evac, ZQ + m + 1)
                a, r = acc[m % 3], raw[m % 3]
                link(nc.vector.tensor_scalar(a[:, :], r[:, 0:CV], parq[:, QKV[m], 0:1], None, ALU.mult))
                for j in range(1, WC):
                    ins = stt(out=a[:, :], in0=r[:, j:j + CV], scalar=parq[:, QKV[m], j:j + 1], in1=a[:, :],
                              op0=ALU.mult, op1=ALU.add)
                    if j < WC - 1:
                        link(ins)
                ins.then_inc(conv_done, 1)

            def gate(m):
                vec.wait_ge(tanh_done, m + 1)
                stt(out=cv[QKV[m]][:, :], in0=th[m % 2][:, :], scalar=1.0, in1=acc[m % 3][:, :], op0=ALU.add,
                    op1=ALU.mult).then_inc(cv_done, 1)

            def invert(g):
                vec.wait_ge(sums_ready, g + 1)
                if g:
                    vec.wait_ge(norms_spread, 4 * g)
                nc.vector.reciprocal(rn[:, 1, :], rn[:, 0, :]).then_inc(norms_ready, 1)

            def normalize(j):
                tile = [QKV[m] for m in qk_index][j]
                vec.wait_ge(norms_spread, j + 1)
                t = cv[tile][:, :].rearrange("p (a b) -> p a b", a=2)
                stt(out=t, in0=t, scalar=0.5 * P ** -0.5 if tile < 4 else 0.5, in1=ps[:, 6:8, 0:HC], op0=ALU.mult,
                    op1=ALU.mult).then_inc(qk_ready, 1)

            def gate_output(g):
                vec.wait_ge(z_evac, ZG + g + 1)
                stt(out=yT[:, 4 + g, :], in0=th[g % 2][:, 0:T], scalar=1.0, in1=yT[:, 4 + g, :], op0=ALU.add,
                    op1=ALU.mult).then_inc(gate_tanh, 1)

            vec.wait_ge(ba_done, 1)
            vec.wait_ge(h_lo, NT)
            for n in range(ZQ, NZ + 4):
                m = n - ZQ
                if m < CQ:
                    convolve(m)
                if 1 <= m <= CQ:
                    gate(m - 1)
                if 0 <= n - ZG < H:
                    gate_output(n - ZG)
                if n - 1 in LAST_SUM:
                    invert(LAST_SUM.index(n - 1))
                if n in SPREAD:
                    normalize(SPREAD.index(n))
                taps(36 + 3 * m, 36 + 3 * m + 3)

            vec.wait_ge(g_cols, 2)
            vec.wait_ge(a_mixed, 2)
            vec.wait_ge(qk_ready, len(qk_index))
            stt(out=sc1[:, 0:TT], in0=gw[:, 1, 0:TT], scalar=-1.0, in1=eGc[:, 0:TT], op0=ALU.mult, op1=ALU.mult).then_inc(col_scales, 1)
            nc.vector.tensor_scalar(sc3[:, 0:TT], gw[:, 1, 0:TT], 0.5, None, ALU.mult).then_inc(col_scales, 1)
            vec.wait_ge(col_scales, 2)

            def flat(t):
                return t[:, :, :].rearrange("p a b -> p (a b)")

            def bank(b):
                return ps[:, b, :].rearrange("p (a b) -> p a b", b=P)

            def mask(n):
                return cst[:, C_LM + n * P:C_LM + (n + 1) * P].unsqueeze(1).broadcast_to([P, TT, P])

            def over_chunks(ap):
                return ap.unsqueeze(1).broadcast_to([P, TT, P])

            tt = nc.vector.tensor_tensor
            for hp in range(2):
                pairs = [(z, 2 * hp + z, 4 * z) for z in range(2)]
                for z, h, B in pairs:
                    if hp:
                        vec.wait_ge(o_done, both(z, hp))
                    nc.vector.tensor_copy(grep[z][:, :, :], bcast(gw[:, 7, 0:TT, h], P)).then_inc(rep_ready, 1)
                    nc.vector.tensor_copy(brep[z][:, :, :], bcast(gw[:, 1, 0:TT, h], P)).then_inc(rep_ready, 1)
                for z, h, B in pairs:
                    vec.wait_ge(spread, both(z, 2 * hp + 2, 2))
                    tt(kb[z][:, :, :], cv[4 + h][:, 0:SEQ].rearrange("p (a b) -> p a b", b=P), bank(B + 1), ALU.mult).then_inc(kb_ready, 1)
                    vec.wait_ge(eG_ready, both(z, hp + 1))
                    tt(DT[z][:, :, :], bank(B), over_chunks(cst[:, C_MN:C_MN + P]), ALU.add).then_inc(D_ready, 1)
                    tt(gdif[:, 0:TT, h], ps[:, B, P - 1:SEQ:P], nG[:, 0:TT, h], ALU.add).then_inc(D_ready, 1)
                    tt(qG[z][:, :, :], cv[h][:, 0:SEQ].rearrange("p (a b) -> p a b", b=P), eG[z][:, :, :], ALU.mult)
                for z, h, B in pairs:
                    vec.wait_ge(scored, both(z, hp + 1))
                    vec.wait_ge(DT_ready, both(z, (TT + 1) * (hp + 1), 5))
                    tt(AT[z][:, :, :], bank(B + 2), DT[z][:, :, :], ALU.mult).then_inc(A_ready, 1)
                    tt(att[z][:, :, :], bank(B + 3), DT[z][:, :, :], ALU.mult).then_inc(A_ready, 1)
                    vec.wait_ge(A_ready, both(z, 2 * hp + 2, 2))
                    link(tt(BT[z][0][:, :, :], AT[z][:, :, :], mask(0), ALU.mult))
                    tt(XX[z][:, 1], over_chunks(ident), BT[z][0][:, :, :], ALU.subtract).then_inc(XT0_ready, 1)
                    vec.wait_ge(rows_done, both(z, hp + 1))
                    tt(kbG[z][:, :, :], bank(B), bcast(sc1[:, 0:TT, h], P), ALU.mult).then_inc(rows_scaled, 1)
                    tt(kd[z][:, :, :], bank(B), bcast(kds[:, 0:TT, h], P), ALU.mult).then_inc(rows_scaled, 1)
                    tt(vb[z][:, :, :], bank(B + 1), bcast(sc3[:, 0:TT, h], P), ALU.mult).then_inc(rows_scaled, 1)

                def mask_level(z, n):
                    if n >= 3:
                        vec.wait_ge(T1_done, both(z, (LEVELS - 1) * hp + n - 2))
                    if n == 2:
                        vec.wait_ge(XT0_ready, both(z, hp + 1))
                    tt(BT[z][n % 2][:, :, :], AT[z][:, :, :], mask(n), ALU.mult).then_inc(BT_ready, 1)

                for z in range(2):
                    mask_level(z, 1)
                for n in range(1, LEVELS):
                    for z, h, B in pairs:
                        if n < LEVELS - 1:
                            mask_level(z, n + 1)
                    for z, h, B in pairs:
                        vec.wait_ge(T2_done, both(z, (LEVELS - 1) * hp + n))
                        if n < LEVELS - 1:
                            xx, new = XX[z][:, :, :, :].rearrange("p x a b -> p x (a b)"), ps[:, B:B + 2, :]
                        else:
                            xx, new = XX[z][:, 1].rearrange("p a b -> p (a b)"), ps[:, B + 1, :]
                        tt(xx, xx, new, ALU.subtract).then_inc(X_ready, 1)
                for i in range(TT):
                    for z, h, B in pairs:
                        vec.wait_ge(S_done, both(z, TT * hp + i + 1))
                        dst = S[z][i % 2][:, :] if i < TT - 1 else sfin[:, h, :]
                        new = ps[:, B, i * P:(i + 1) * P]
                        if i == 0:
                            ins = nc.vector.tensor_copy(dst, new)
                        else:
                            vec.wait_ge(S_ready, both(z, TT * hp + i))
                            ins = stt(out=dst, in0=S[z][(i - 1) % 2][:, :], scalar=eG[z][:, i, P - 1:P], in1=new,
                                      op0=ALU.mult, op1=ALU.add)
                        ins.then_inc(S_ready, 1)

            for z in range(2):
                vec.wait_ge(o_ready, both(z, 2))
            vec.wait_ge(small_saved, 2)
            by_head = [P, H, NS]
            tt(sb[:, 0, :].rearrange("p (h b) -> p h b", h=H), kq[:, :, :, 0], kq[:, :, :, 1], ALU.mult).then_inc(ds_vec, 1)
            for n, slot in enumerate((7, 1)):
                tt(dg[:, n], bcast(gw[0:NS, slot, TT, :], NS), ident[0:NS, 0:NS].unsqueeze(1).broadcast_to([NS, H, NS]),
                   ALU.mult).then_inc(ds_vec, 1)
            vec.wait_ge(ds_act, 4)
            link(tt(sb[:, 4, :], kqs[:, :, 0], sb[:, 2, :], ALU.mult))
            link(stt(out=sb[:, 6, :], in0=small[:, 8:12, :].rearrange("p a b -> p (a b)"), scalar=0.5, in1=sb[:, 4, :],
                     op0=ALU.mult, op1=ALU.subtract))
            tt(sb[:, 5, :], sb[:, 6, :], sb[:, 3, :], ALU.mult).then_inc(ds_vec, 1)
            vec.wait_ge(ds_vec, 4)
            link(tt(sb[:, 7, :], kqs[:, :, 1], sb[:, 2, :], ALU.mult))
            link(tt(sb[:, 4, :], sb[:, 1, :], sb[:, 5, :], ALU.mult))
            for h in range(H):
                tt(cv[8 + h][:, SEQ:T], sb[:, 7, h * NS:(h + 1) * NS], sb[:, 4, h * NS:(h + 1) * NS], ALU.add).then_inc(ds_vec, 1)
            vec.wait_ge(mean_done, 1)
            vec.wait_ge(b_conved, 2 * WB)
            for t in range(2):
                y = yT[:, 2 + t, :].rearrange("p (a b) -> p a b", a=2)
                stt(out=y, in0=ps[:, 5:7, 0:HT], scalar=-1.0 / DB, in1=y, op0=ALU.mult, op1=ALU.add).then_inc(xc_ready, 1)
            vec.wait_ge(oroot_ready, 1)
            nc.vector.reciprocal(rno[:, 1, :], rno[:, 0, :]).then_inc(onorm_ready, 1)
            vec.wait_ge(ds_vec, 8)
            for n in range(4):
                vec.wait_ge(ospread, n + 1)
                o = cv[8 + n][:, 0:T].rearrange("p (a b) -> p a b", a=2)
                b = (1, 5)[n % 2]
                stt(out=o, in0=o, scalar=ogh[:, :], in1=ps[:, b:b + 2, 0:HT], op0=ALU.mult, op1=ALU.mult).then_inc(oscaled, 1)
                vec.wait_ge(oscaled, n + 1)
                link(tt(yT[:, 4 + n, :], yT[:, 4 + n, :], cv[8 + n][:, 0:T], ALU.mult))
            vec.wait_ge(ospread, 5)
            vec.wait_ge(xc_ready, 2)
            for t in range(2):
                y = yT[:, 2 + t, :].rearrange("p (a b) -> p a b", a=2)
                ins = tt(y, y, ps[:, 1:3, 0:HT], ALU.mult)
                if t == 0:
                    link(ins)
            ins.then_inc(oscaled, 1)
            vec.wait_ge(oscaled, 5)
            for t in range(2):
                nc.vector.tensor_scalar(yT[:, 2 + t, :], yT[:, 2 + t, :], lnh[:, t, 0:1], lnh[:, t, 1:2], ALU.mult, ALU.add).then_inc(
                    bnorm_ready, 1)
            for t in range(2):
                vec.wait_ge(btanh_ready, t + 1)
                stt(out=yT[:, 2 + t, :], in0=bth2[t][:, :], scalar=1.0, in1=yT[:, 2 + t, :], op0=ALU.add, op1=ALU.mult).then_inc(
                    yb_ready, 1)
            vec.wait_ge(ds_rowed, 2)

            def spread_values(h):
                if h >= 1:
                    vec.wait_ge(s0_outer, 2 * h)
                tt(vnd[:, :, :], srow[:, 0, h * P:(h + 1) * P].unsqueeze(1).broadcast_to([NS, NS, P]), bcast(ident[0:NS, 0:NS], P),
                   ALU.mult).then_inc(ds_diag, 1)

            def add_outer(h, half):
                vec.wait_ge(s0_outer, 2 * h + half + 1)
                vec.wait_ge(s0_decayed, h + 1)
                s = s0[:, h, 4 * half:4 * half + 4].rearrange("p b v -> p (b v)")
                tt(s, s, ps[:, 7, :], ALU.add).then_inc(s0_ready, 1)

            spread_values(0)
            vec.wait_ge(wout_in, 32)
            vec.wait_ge(states_out, 6 * 16)
            for i in range(NT):
                n = P if i < TT else NS
                vec.wait_ge(wout_done, i + 1)
                if i < TT:
                    xi = x[0:n, i, :].rearrange("p (a b) -> p a b", a=2)
                    ins = tt(xi, xi, ps[0:n, 2 * (i % 2):2 * (i % 2) + 2, :], ALU.add)
                else:
                    for g in range(4):
                        xi = x[0:n, i, g * D // 4:(g + 1) * D // 4]
                        ins = tt(xi, xi, ps[32 * g:32 * g + n, 2 * (i % 2), 0:D // 4], ALU.add)
                ins.then_inc(x1_ready, 1)
                if i < H:
                    add_outer(i, 0)
                vec.wait_ge(x1_squared, 2 * i + 2)
                nc.vector.reciprocal(rstd[0:n, i:i + 1], ss[0:n, i:i + 1]).then_inc(r2_ready, 1)
                vec.wait_ge(r2_ready, i + 1)
                if i >= 2:
                    vec.wait_ge(h2_turned, i - 1)
                    vec.wait_ge(h2_stored[i % 2], 16 * (i // 2))
                stt(out=h2row[i % 2][0:n].rearrange("t c p -> t p c"), in0=x[0:n, i, :].rearrange("t (p c) -> t p c", c=KT),
                    scalar=rstd[0:n, i:i + 1], in1=g2b[0:n, :].rearrange("t (p c) -> t p c", c=KT), op0=ALU.mult,
                    op1=ALU.mult).then_inc(h2_ready, 1)
                if i < H:
                    add_outer(i, 1)
                if i + 1 < H:
                    spread_values(i + 1)

            gl, el = L[:, :, 0:NG], L[:, :, NG:]
            iota = cst[:, C_IO:C_IO + NE].unsqueeze(1).broadcast_to([P, NT, NE])
            ts = nc.vector.tensor_scalar
            reduce = nc.vector.tensor_reduce

            def first_of(hit, top, index, onehot, scratch, n, steps):
                link(ts(scratch, hit, -99.0, 99.0, ALU.mult, ALU.add))
                link(tt(scratch, scratch, steps, ALU.add))
                link(reduce(index, scratch, AX_X, ALU.min))
                link(tt(onehot, steps, bcast(index, n), ALU.is_equal))

            vec.wait_ge(logits_ready, 2)
            link(reduce(ns[:, 0], gl, AX_X, ALU.max))
            tt(g4[:, 0], gl, bcast(ns[:, 0], NG), ALU.subtract).then_inc(rt_vec, 1)
            link(tt(g4[:, 2], gl, bcast(ns[:, 0], NG), ALU.is_equal))
            vec.wait_ge(rt_act, 1)
            link(reduce(ns[:, 1], g4[:, 1], AX_X, ALU.add))
            link(nc.vector.reciprocal(ns[:, 2], ns[:, 1]))
            link(ts(g4[:, 2], g4[:, 2], -99.0, 99.0, ALU.mult, ALU.add))
            link(tt(g4[:, 2], g4[:, 2], iota[:, :, 0:NG], ALU.add))
            link(reduce(ns[:, 3], g4[:, 2], AX_X, ALU.min))
            m, other, hit, one, chosen, two, rank = (eight[n][:, :, :] for n in (0, 1, 2, 3, 4, 5, 6))
            scratch = hit
            link(tt(m, cst[:, C_GI:C_GI + NE].unsqueeze(1).broadcast_to([P, NT, NE]), bcast(ns[:, 3], NE), ALU.is_equal))
            link(ts(other, m, 1e30, -1e30, ALU.mult, ALU.add))
            link(tt(m, m, el, ALU.mult))
            link(tt(m, m, other, ALU.add))
            link(reduce(ns[:, 6], m, AX_X, ALU.max))
            link(tt(hit, m, bcast(ns[:, 6], NE), ALU.is_equal))
            first_of(hit, None, ns[:, 8], one, scratch, NE, iota)
            link(stt(out=m, in0=one, scalar=-3e30, in1=m, op0=ALU.mult, op1=ALU.add))
            link(reduce(ns[:, 7], m, AX_X, ALU.max))
            tt(ns[:, 4], ns[:, 7], ns[:, 6], ALU.subtract).then_inc(rt_vec, 1)
            link(tt(hit, m, bcast(ns[:, 7], NE), ALU.is_equal))
            first_of(hit, None, ns[:, 9], two, scratch, NE, iota)
            link(tt(chosen, one, two, ALU.add))
            tt(chosen, chosen, bcast(cst[:, C_TILE:C_TILE + NT], NE), ALU.mult).then_inc(routed, 1)
            vec.wait_ge(rt_act, 2)
            link(ts(ns[:, 10], ns[:, 5], 1.0, None, ALU.add))
            link(nc.vector.reciprocal(ns[:, 11], ns[:, 10]))
            link(tt(wgt[:, 0], ns[:, 11], ns[:, 2], ALU.mult))
            link(tt(wgt[:, 1], wgt[:, 0], ns[:, 5], ALU.mult))
            link(nc.vector.tensor_copy(pid[:, 0], cst[:, C_ROWID:C_ROWID + NT]))
            link(ts(pid[:, 1], cst[:, C_ROWID:C_ROWID + NT], float(T), None, ALU.add))
            vec.wait_ge(ranked, 1)
            total = other
            link(nc.vector.tensor_copy(total, ps[:, 1, 0:NT * NE].rearrange("p (a b) -> p a b", a=NT)))
            for i in range(1, NT):
                link(tt(total[:, i], total[:, i], total[:, i - 1], ALU.add))
            link(nc.vector.tensor_copy(rank, ps[:, 0, 0:NT * NE].rearrange("p (a b) -> p a b", a=NT)))
            link(tt(rank[:, 1:NT], rank[:, 1:NT], total[:, 0:NT - 1], ALU.add))
            link(stt(out=rank, in0=rank, scalar=float(NE), in1=cst[:, C_EC:C_EC + NE].unsqueeze(1).broadcast_to([P, NT, NE]),
                     op0=ALU.mult, op1=ALU.add))
            for n, onehot in enumerate((one, two)):
                link(tt(scratch, onehot, rank, ALU.mult))
                link(reduce(ns[:, 8 + n], scratch, AX_X, ALU.add))
                tt(where[:, n], ns[:, 8 + n], cst[:, C_PAD:C_PAD + NT], ALU.add).then_inc(routed, 1)
            count = total[0:1, NT - 1, :]
            link(ts(moref[:, 0, :], count, float(CAP), None, ALU.is_gt))
            for n in range(2, MORE + 1):
                link(ts(moref[:, 1, :], count, float(n * CAP), None, ALU.is_gt))
                link(tt(moref[:, 0, :], moref[:, 0, :], moref[:, 1, :], ALU.add))
            nc.vector.tensor_copy(more[:, :], moref[:, 0, :]).then_inc(routed, 1)
            vec.wait_ge(slots_in, 7 * 16)
            link(nc.vector.tensor_copy(idf[:, 0, 0:NE // 2], graw[:, :]))
            link(ts(idf[:, 1, 0:NE // 2], idf[:, 0, 0:NE // 2], float(T), -float(T), ALU.is_ge, ALU.mult))
            tt(gidx[:, :], idf[:, 0, 0:NE // 2], idf[:, 1, 0:NE // 2], ALU.add).then_inc(idx_ready, 1)
            vec.wait_ge(idx_ready, 1)
            link(nc.vector.tensor_copy(idf[:, 0, :], sraw[:, :]))
            ts(sidx[:, :], idf[:, 0, :], 2.0, cst[:, C_HALF:C_HALF + 1], ALU.mult, ALU.add).then_inc(idx_ready, 1)
            slot_of, past = (t[:, :, :].rearrange("p a b -> p (a b)") for t in oidf)
            link(nc.vector.tensor_copy(slot_of, oraw[:, :, :].rearrange("p a b -> p (a b)")))
            link(ts(past, slot_of, float(T), -float(T), ALU.is_ge, ALU.mult))
            tt(otoks[:, 0:MORE * NE], slot_of, past, ALU.add).then_inc(idx_ready, 1)
            ts(osids[:, :], slot_of, 2.0, cst[:, C_HALF:C_HALF + 1], ALU.mult, ALU.add).then_inc(idx_ready, 1)
            count_groups(vec, "vec")
            vec.wait_ge(routed, 4)

            def swiglu(e, s):
                vec.wait_ge(up_tanh, e + 1)
                stt(out=gact[s][:, :], in0=gth[s][:, :], scalar=1.0, in1=ps[:, s, 0:P], op0=ALU.add, op1=ALU.mult).then_inc(act_half, 1)
                vec.wait_ge(act_half, e + 1)
                stt(out=gact[s][:, :], in0=gact[s][:, :], scalar=0.5, in1=ps[:, s, P:2 * P], op0=ALU.mult, op1=ALU.mult).then_inc(
                    act_ready, 1)

            def vec_round(it, first, last):
                for u in range(ROUND):
                    e = ROUND * it + u
                    if u < 3:
                        if u == 0:
                            swiglu(e, 0)
                        swiglu(e + 1, (u + 1) % 2)
                    vec.wait_ge(down_done, e + 1)
                    if not first:
                        vec.wait_ge(y_out[u], 16 * it)
                    nc.vector.tensor_copy(ysb[u][:, :], ps[:, 4 + u % 2, :]).then_inc(y_ready, 1)

                    def body(g, done, needed):
                        vec.wait_ge(m_act, done * 3 + 2)
                        stt(out=oact[:, :], in0=oth[:, :], scalar=1.0, in1=ps[:, 3, 0:P], op0=ALU.add, op1=ALU.mult).then_inc(m_vec, 1)
                        vec.wait_ge(m_vec, done * 3 + 1)
                        stt(out=oact[:, :], in0=oact[:, :], scalar=0.5, in1=ps[:, 3, P:2 * P], op0=ALU.mult, op1=ALU.mult).then_inc(m_vec, 1)
                        vec.wait_ge(m_pe, done * 4 + 4)
                        vec.wait_ge(m_saved, done + 1)
                        nc.vector.tensor_copy(yo[:, :], ps[:, 3, :]).then_inc(m_vec, 1)

                    more_groups(vec, e, body)
                    vec.sem_inc(expert_done, 1)

            rounds(vec, vec_round)
            def add_rows(i):
                n = P if i < TT else NS
                for k in range(2):
                    vec.wait_ge(x_in[i], 16 + 2 * 16)
                    if k:
                        vec.wait_ge(fin_added, 2 * i + 1)
                    stt(out=x[0:n, i, :], in0=yk[i][0:n, k, :], scalar=wgt[0:n, k, i:i + 1], in1=x[0:n, i, :], op0=ALU.mult,
                        op1=ALU.add).then_inc(fin_added, 1)

            def finish(i):
                n = P if i < TT else NS
                vec.wait_ge(x1_squared, 2 * (NT + i) + 2)
                nc.vector.reciprocal(rstd[0:n, i:i + 1], ss[0:n, i:i + 1]).then_inc(r2_ready, 1)
                vec.wait_ge(r2_ready, NT + i + 1)
                stt(out=x[0:n, i, :], in0=x[0:n, i, :], scalar=rstd[0:n, i:i + 1], in1=gfb[0:n, :], op0=ALU.mult,
                    op1=ALU.mult).then_inc(fin_ready, 1)

            for i in range(NT + 1):
                if i < NT:
                    add_rows(i)
                if i >= 1:
                    finish(i - 1)

        @block.tensor
        def _(pe):
            mm = nc.tensor.matmul
            turn = nc.tensor.transpose
            pe.wait_ge(consts_in, 16)
            for i in range(NT):
                n = P if i < TT else NS
                pe.wait_ge(hrow_ready, i + 1)
                if i >= 2:
                    pe.wait_ge(hT_ready, i - 1)
                for c in range(KT):
                    last = turn(ps[:, 2 * (i % 2) + c // 4, c % 4 * P:c % 4 * P + n], hrow[i % 2][0:n, c, :], ident[0:n, 0:n])
                last.then_inc(h_turned, 1)
            pe.wait_ge(rows_in, 8 * 16)
            for n in range(CQ):
                last = turn(ps[:, 4, n * ROWS_Q:(n + 1) * ROWS_Q], rowq[:, n * P:(n + 1) * P], ident[0:ROWS_Q, 0:ROWS_Q])
            last.then_inc(rows_turned, 1)
            for t in range(2):
                last = turn(ps[:, 5, t * ROWS_AB:(t + 1) * ROWS_AB], rowab[:, t * P:(t + 1) * P], ident[0:ROWS_AB, 0:ROWS_AB])
            last.then_inc(rows_turned, 1)
            for t in range(2):
                for a in range(2):
                    last = turn(ps[:, 6, (2 * t + a) * 120:(2 * t + a + 1) * 120], rowsb[:, a, t * P:(t + 1) * P],
                                ident[0:120, 0:120])
            last.then_inc(rows_turned, 1)
            def project_scalars():
                pe.wait_ge(small_in, 5 * 16)
                pe.wait_ge(hT_ready, NT)
                for i in range(NT):
                    n = P if i < TT else NS
                    for c in range(KT):
                        last = mm(ps[0:n, 7, i * 8:(i + 1) * 8], hT[:, c, tokens(i)], wba[:, c, :], start=c == 0, stop=c == KT - 1)
                last.then_inc(ba_done, 1)

            def project(n):
                s = n % WSLOTS
                pe.wait_ge(w_lo, n + 1)
                if n == 0:
                    pe.wait_ge(hT_ready, NT)
                if n >= 2:
                    pe.wait_ge(z_evac, n - 1)
                for half, (lo, hi) in enumerate(((0, 256), (256, T))):
                    if n == 0:
                        pe.wait_ge(h_lo, NT)
                    parts = [(weights[s], h) for weights, h in ((whi, hhi), (wlo, hhi), (whi, hlo))]
                    for c in range(KT):
                        for j, (weights, h) in enumerate(parts):
                            last = mm(ps[:, 2 * (n % 2) + half, 0:hi - lo], weights[:, c, :], h[:, c, lo:hi],
                                      start=c == 0 and j == 0, stop=c == KT - 1 and j == len(parts) - 1)
                last.then_inc(z_done, 1)

            def sum_squares(m):
                if m not in qk_index:
                    return
                j = qk_index[m]
                pe.wait_ge(squared, j + 1)
                if j == 4:
                    pe.wait_ge(sums_ready, 1)
                for half in range(2):
                    last = mm(ps[0:8, 4 + half, 0:HC], column(j % 4), sq[j % 2][:, half * HC:(half + 1) * HC], start=j % 4 == 0,
                              stop=j % 4 == 3)
                last.then_inc(sums_done, 1)

            def spread_norm(j):
                pe.wait_ge(norms_ready, j // 4 + 1)
                if j:
                    pe.wait_ge(qk_ready, j)
                else:
                    pe.wait_ge(ba_ready, 2)
                for half in range(2):
                    last = mm(ps[:, 6 + half, 0:HC], select(j % 4), rn[:, 1, half * HC:(half + 1) * HC], start=True, stop=True)
                last.then_inc(norms_spread, 1)

            for n in range(NZ + 4):
                if n < NZ:
                    project(n)
                if n == 1:
                    project_scalars()
                sum_squares(n - ZQ - 3)
                if n in SPREAD:
                    spread_norm(SPREAD.index(n))

            pe.wait_ge(g_ready, 2)
            pe.wait_ge(qk_ready, len(qk_index))
            mm(ps[:, 6, 0:TT * H], incl, gw[:, 7, 0:TT, :], start=True, stop=True).then_inc(g_summed, 1)

            def four_products(bank, left, right, **flags):
                for i in range(TT):
                    last = mm(ps[:, bank, i * P:(i + 1) * P], left(i), right(i), start=True, stop=True)
                return last

            for hp in range(2):
                pairs = [(z, 2 * hp + z, 4 * z) for z in range(2)]
                chunk = [lambda t, i: t[:, i * P:(i + 1) * P]][0]
                for z, h, B in pairs:
                    pe.wait_ge(rep_ready, both(z, 2 * hp + 2, 2))
                    if z == 1:
                        pe.wait_ge(g_cols, 2)
                    if hp:
                        pe.wait_ge(o_ready, both(z, hp))
                        pe.wait_ge(S_ready, both(z, TT * hp))
                    four_products(B, lambda i: grep[z][:, i, :], lambda i: incl).then_inc(spread, 1)
                    four_products(B + 1, lambda i: brep[z][:, i, :], lambda i: ident).then_inc(spread, 1)
                for z, h, B in pairs:
                    q, k, v = cv[h], cv[4 + h], cv[8 + h]
                    pe.wait_ge(kb_ready, both(z, hp + 1))
                    four_products(B + 2, lambda i: chunk(k, i), lambda i: kb[z][:, i, :])
                    four_products(B + 3, lambda i: chunk(k, i), lambda i: chunk(q, i)).then_inc(scored, 1)
                    pe.wait_ge(eG_ready, both(z, hp + 1))
                    pe.wait_ge(D_ready, both(z, 2 * hp + 2, 2))
                    for i in range(TT):
                        turn(ps[:, B, i * P:(i + 1) * P], chunk(k, i), ident)
                    for i in range(TT):
                        last = turn(ps[:, B + 1, i * P:(i + 1) * P], chunk(v, i), ident)
                    last.then_inc(rows_done, 1)
                for z, h, B in pairs:
                    pe.wait_ge(XT0_ready, both(z, hp + 1))
                    for i in range(TT):
                        last = turn(ps[:, B + 2, i * P:(i + 1) * P], XX[z][:, 1, i, :], ident)
                    last.then_inc(X0_done, 1)
                for n in range(1, LEVELS):
                    for z, h, B in pairs:
                        before = (LEVELS - 1) * hp + n
                        pe.wait_ge(BT_ready, both(z, before))
                        pe.wait_ge(X0_ready, both(z, hp + 1))
                        if n == 1:
                            pe.wait_ge(rows_scaled, both(z, 3 * hp + 3, 3))
                        else:
                            pe.wait_ge(X_ready, both(z, before - 1))
                        four_products(B + 2, lambda i: BT[z][n % 2][:, i, :], lambda i: XX[z][:, 0, i, :]).then_inc(T1_done, 1)
                    for z, h, B in pairs:
                        pe.wait_ge(T1_ready, both(z, before))
                        if n < LEVELS - 1:
                            four_products(B, lambda i: XX[z][:, 1, i, :], lambda i: t1[z][:, i, :])
                        four_products(B + 1, lambda i: t1[z][:, i, :], lambda i: XX[z][:, 1, i, :]).then_inc(T2_done, 1)
                for z, h, B in pairs:
                    pe.wait_ge(X_ready, both(z, (LEVELS - 1) * (hp + 1)))
                    four_products(B + 2, lambda i: kbG[z][:, i, :], lambda i: XX[z][:, 1, i, :]).then_inc(wT_done, 1)
                for i in range(TT):
                    for z, h, B in pairs:
                        pv = ps[:, B + 3, i * P:(i + 1) * P]
                        last = mm(pv, XX[z][:, 1, i, :], vb[z][:, i, :], start=True, stop=i == 0)
                        if i:
                            if i == 1:
                                pe.wait_ge(wT_ready, both(z, hp + 1))
                            pe.wait_ge(S_ready, both(z, TT * hp + i))
                            last = mm(pv, wT[z][:, i, :], S[z][(i - 1) % 2][:, :], start=False, stop=True)
                        last.then_inc(vn_done, 1)
                    for z, h, B in pairs:
                        pe.wait_ge(vn_ready, both(z, TT * hp + i + 1))
                        mm(ps[:, B, i * P:(i + 1) * P], kd[z][:, i, :], vn[z][:, i, :], start=True, stop=True).then_inc(S_done, 1)
                        po = ps[:, B + 1, i * P:(i + 1) * P]
                        if i:
                            mm(po, S[z][(i - 1) % 2][:, :], qG[z][:, i, :], start=True, stop=False)
                        last = mm(po, vn[z][:, i, :], att[z][:, i, :], start=i == 0, stop=True)
                        if i == TT - 1:
                            last.then_inc(o_done, 1)

            for z in range(2):
                pe.wait_ge(o_ready, both(z, 2))
                pe.wait_ge(S_ready, both(z, 2 * TT))
            for n in range(CQ):
                last = turn(ps[0:27, 5 + n // 4, n % 4 * P:(n % 4 + 1) * P], stq[:, n, :], ident)
            last.then_inc(rows_turned, 1)
            pe.wait_ge(states_ready, 1)
            for t in range(2):
                turn(ps[0:18, 7, t * P:(t + 1) * P], sta[:, t, :], ident)
                last = turn(ps[0:WB - 1, 7, DB + t * P:DB + (t + 1) * P], stp[:, t, :], ident)
            last.then_inc(rows_turned, 1)
            pe.wait_ge(small_saved, 2)
            pe.wait_ge(s0_in, H * 16)
            for h in range(H):
                for b in range(NS):
                    last = mm(ps[:, 0, 2 * (h * NS + b):2 * (h * NS + b) + 2], s0[:, h, b, :], kq[:, h, b, :], start=True, stop=True)
            last.then_inc(ds_prod, 1)
            pe.wait_ge(states_ready, 3)
            for a in range(2):
                for t in range(2):
                    last = turn(ps[0:120, 7, a * DB + t * P:a * DB + (t + 1) * P], stb[:, t, a * 120:(a + 1) * 120], ident)
            last.then_inc(rows_turned, 1)
            pe.wait_ge(ds_vec, 1)
            mm(ps[:, 1, 0:H * NS], ones, sb[:, 0, :], start=True, stop=True).then_inc(ds_prod, 1)
            pe.wait_ge(ds_vec, 3)
            mm(ps[:, 2, 0:2 * H * NS], ones[0:NS, :], dg[:, :, :, :].rearrange("p a b c -> p (a b c)"), start=True,
               stop=True).then_inc(ds_prod, 1)
            for h in range(H):
                turn(ps[0:NS, 4, h * P:(h + 1) * P], kq[:, h, :, 0], ident)
            pe.wait_ge(ds_vec, 4)
            for h in range(H):
                last = turn(ps[0:NS, 3, h * P:(h + 1) * P], sb[:, 5, h * NS:(h + 1) * NS], ident)
            last.then_inc(ds_row, 1)
            pe.wait_ge(b_conved, 2 * WB)
            for half in range(2):
                for t in range(2):
                    last = mm(ps[:, 5 + half, 0:HT], ones, yT[:, 2 + t, half * HT:(half + 1) * HT], start=t == 0, stop=t == 1)
            last.then_inc(mean_done, 1)
            for n in range(6):
                pe.wait_ge(osq_ready, n + 1)
                if n == 0:
                    pe.wait_ge(ds_act, 4)
                for half in range(2):
                    last = mm(ps[0:8, 1 + half, 0:HT], column(min(n, 4)), osq[n % 2][:, half * HT:(half + 1) * HT],
                              start=n == 0, stop=n == 5)
                last.then_inc(osum_done, 1)
            pe.wait_ge(onorm_ready, 1)
            pe.wait_ge(xc_ready, 2)
            for n in range(5):
                if n >= 2:
                    pe.wait_ge(oscaled, n - 1)
                b = (1, 5)[n % 2]
                for half in range(2):
                    last = mm(ps[:, b + half, 0:HT], select(n), rno[:, 1, half * HT:(half + 1) * HT], start=True, stop=True)
                last.then_inc(ospread, 1)
            pe.wait_ge(wout_in, 32)
            pe.wait_ge(a_mixed, 2)
            pe.wait_ge(yb_ready, 2)
            pe.wait_ge(oscaled, 5)
            pe.wait_ge(ds_rowed, 2)

            def outer(h, half):
                pe.wait_ge(ds_diag, h + 1)
                if 2 * h + half:
                    pe.wait_ge(s0_ready, 2 * h + half)
                mm(ps[:, 7, :], srow[:, 1, h * P:(h + 1) * P], vnd[:, 4 * half:4 * half + 4, :], start=True,
                   stop=True).then_inc(s0_outer, 1)

            def out_project(i):
                if i >= 2:
                    pe.wait_ge(x1_ready, i - 1)
                if i == TT:
                    for k in range(KT):
                        for g in range(4):
                            last = mm(ps[32 * g:32 * g + NS, 2 * (i % 2), 0:D // 4], yT[:, k, tokens(i)],
                                      wout[:, k, g * D // 4:(g + 1) * D // 4], start=k == 0, stop=k == KT - 1)
                    last.then_inc(wout_done, 1)
                    return
                n = P
                for half in range(2):
                    for k in range(KT):
                        last = mm(ps[0:n, 2 * (i % 2) + half, :], yT[:, k, tokens(i)], wout[:, k, half * 512:(half + 1) * 512],
                                  start=k == 0, stop=k == KT - 1)
                last.then_inc(wout_done, 1)

            def turn_h2(i):
                n = P if i < TT else NS
                pe.wait_ge(h2_ready, i + 1)
                if i >= 1:
                    pe.wait_ge(h2T_ready, i)
                for c in range(KT):
                    last = turn(ps[:, 4 + c // 4, c % 4 * P:c % 4 * P + n], h2row[i % 2][0:n, c, :], ident[0:n, 0:n])
                last.then_inc(h2_turned, 1)

            def logits(i):
                n = P if i < TT else NS
                pe.wait_ge(h2T_ready, i + 1)
                pe.wait_ge(wr_in, (1 + NG) * 16)
                for c in range(KT):
                    last = mm(ps[0:n, 6, i * (NG + NE):(i + 1) * (NG + NE)], h2T[:, c, 0:n], wr[:, c, :], start=c == 0,
                              stop=c == KT - 1)
                last.then_inc(logits_done, 1)

            for i in range(NT + 2):
                if i < NT:
                    out_project(i)
                if i < H:
                    outer(i, 0)
                if 1 <= i <= NT:
                    turn_h2(i - 1)
                    logits(i - 1)
                if i < H:
                    outer(i, 1)
            pe.wait_ge(routed, 1)
            mm(ps[:, 0, 0:NT * NE], cst[:, C_US:C_US + P], eight[4][:, :, :].rearrange("p a b -> p (a b)"), start=True, stop=True)
            mm(ps[:, 1, 0:NT * NE], ones, eight[4][:, :, :].rearrange("p a b -> p (a b)"), start=True, stop=True).then_inc(ranked, 1)
            count_groups(pe, "pe")
            slot_groups = [pe.alloc_register(f"slot_groups{s}") for s in range(2)]
            for r in slot_groups:
                pe.reg_mov(r, 0)
            pe.wait_ge(routed, 4)

            def halves(bank, left, right, steps, width):
                for c in range(steps):
                    for g in range(2):
                        last = mm(ps[g * CAP:(g + 1) * CAP, bank, 0:width], left(c), right(c, g), start=c == 0, stop=c == steps - 1)
                return last

            def up(u, bank, left):
                return halves(bank, left, lambda c, g: gu[u][:, :, c, g * P:(g + 1) * P], KT, 2 * P)

            def down(u, bank, a):
                return halves(bank, lambda c: a[:, c * CAP:(c + 1) * CAP], lambda c, g: wd[u][:, c, g * 512:(g + 1) * 512], 2, 512)

            def pe_up(it, u):
                e = ROUND * it + u
                s = u // 2
                pe.wait_ge(weights_in[u], tiles_in[u] + 3 * 16 * (it + 1))
                pe.wait_ge(xT_ready, 2 * it + s + 1)
                up(u, u % 2, lambda c: xT[s][:, c, u % 2 * CAP:(u % 2 + 1) * CAP]).then_inc(up_done, 1)

            def pe_round(it, first, last):
                for u in range(ROUND):
                    e = ROUND * it + u
                    if u == 0:
                        pe_up(it, 0)
                    if u < 3:
                        pe_up(it, u + 1)
                    if u == 0 or (u == 2 and not last):
                        j = 2 * it + u // 2 + 1
                        s = (u // 2 + 1) % 2
                        pe.wait_ge(xg_in[s], 16 * (it + 1) if s else 16 * (it + 2))
                        pe.wait_ge(xT_ready, j)
                        for c in range(KT):
                            ins = turn(ps[:, 6 + c // 4, c % 4 * P:(c % 4 + 1) * P], xg[s][:, c * P:(c + 1) * P], ident)
                        ins.then_inc(xg_turned, 1)
                    pe.wait_ge(act_ready, e + 1)
                    turn(ps[:, 2, 0:P], gact[u % 2][:, :], ident).then_inc(act_turned, 1)
                    pe.wait_ge(aT_ready, e + 1)
                    down(u, 4 + u % 2, aT[u % 2]).then_inc(down_done, 1)

                    def body(g, done, needed):
                        pe.wait_ge(m_rows[u % 2], pe.snap(slot_groups[u % 2]) * 16 + 16)
                        pe.reg_add(slot_groups[u % 2], slot_groups[u % 2], 1)
                        for c in range(KT):
                            ins = mm(ps[:, 3, c * CAP:(c + 1) * CAP], xo[u % 2][:, c * P:(c + 1) * P], ident[0:CAP, 0:CAP],
                                     start=True, stop=True)
                        ins.then_inc(m_pe, 1)
                        pe.wait_ge(m_act, done * 3 + 1)
                        up(u, 3, lambda c: xTo[:, c, :]).then_inc(m_pe, 1)
                        pe.wait_ge(m_vec, done * 3 + 2)
                        turn(ps[:, 3, 0:P], oact[:, :], ident).then_inc(m_pe, 1)
                        pe.wait_ge(m_act, done * 3 + 3)
                        down(u, 3, oaT).then_inc(m_pe, 1)

                    more_groups(pe, e, body)

            pe.wait_ge(xg_in[0], 16)
            for c in range(KT):
                last = turn(ps[:, 6 + c // 4, c % 4 * P:(c % 4 + 1) * P], xg[0][:, c * P:(c + 1) * P], ident)
            last.then_inc(xg_turned, 1)
            rounds(pe, pe_round)


OUTS = {
    "y_p": (1, SEQ, D), "y_s": (NS, 1, D),
    "ca_p": (1, 1, WA - 1, DA), "cb_p": (1, 1, WB - 1, DB), "cq_p": (1, 1, WC - 1, CQ * P), "d_p": (1, 1, H, P, P),
    "ca_s": (1, NS, WA - 1, DA), "cb_s": (1, NS, WB - 1, DB), "cq_s": (1, NS, WC - 1, CQ * P), "d_s": (1, NS, H, P, P),
}


def kernel(**inputs):
    import concourse.bacc as bacc
    from concourse.bass_utils import run_bass_kernel_spmd

    nc = bacc.Bacc("TRN2", target_bir_lowering=False, num_devices=1)
    arrays = {name: np.ascontiguousarray(a) for name, a in inputs.items()}
    arrays["consts"] = constants()
    A = {name: nc.dram_tensor(name, a.shape, mybir.dt.from_np(a.dtype), kind="ExternalInput").ap() for name, a in arrays.items()}
    R = {name: nc.dram_tensor(name + "_out", shape, F32, kind="ExternalOutput").ap() for name, shape in OUTS.items()}
    build(nc, A, R)
    got = run_bass_kernel_spmd(nc, [arrays], core_ids=[0]).results[0]
    return tuple(got[name + "_out"] for name in OUTS)
```

```python
from contextlib import ExitStack

import concourse.bass as bass
import numpy as np
from concourse import mybir

ALU = mybir.AluOpType
ACT = mybir.ActivationFunctionType
F32 = mybir.dt.float32
I32 = mybir.dt.int32
F32R = mybir.dt.float32r
AX_X = mybir.AxisListType.X

P = 128
D = 1024
KT = D // P
SEQ, NS = 512, 8
T = SEQ + NS
TT = SEQ // P
NT = TT + 1
ORDER = [TT] + list(range(TT))
HT = T // 2
DA = DB = 256
H = 4
WA, WB, WC = 3, 31, 4
CQ = 3 * H
RAW = (WC - 1) + SEQ + NS * WC
CV = RAW - (WC - 1)
SC = SEQ + WC - 1
HC = CV // 2
EPS = 1e-6
NG, EG = 4, 8
NE = NG * EG
F = 256
CAP = 64
MAXROWS = 9 * CAP
MORE = MAXROWS // CAP - 1
NOWHERE = 1 << 20
SPLIT = 3
LEVELS = 7

BLOCKS = [3, 4, 0, 1, 2, 5, 7, 6, 8, 9, 10, 11, 12]
NZ = 2 * len(BLOCKS)
ZA, ZQ, ZG = 4, 10, 22
QKV = [0, 1, 4, 5, 2, 3, 6, 7, 8, 9, 10, 11]
WSLOTS = 4
ROWS_AB = WB + 2 + WA + NS * (WA - 1)
LNG, LNB, CAW, STA = WB, WB + 1, WB + 2, WB + 2 + WA
ROWS_Q = WC + NS * (WC - 1)

C_ID, C_UI, C_US, C_MN, C_ONE, C_LM = 0, 128, 256, 384, 512, 640
C_COL = C_LM + 128 * LEVELS
C_IO = C_COL + 16
C_GI = C_IO + NE
C_HALF = C_GI + NE
C_ROWID = C_HALF + 1
C_TILE = C_ROWID + NT
C_PAD = C_TILE + NT
C_EC = C_PAD + NT
C_SEL = C_EC + NE
C_END = C_SEL + 8 * 128


def constants():
    c = np.zeros((P, C_END), np.float32)
    p = np.arange(P)
    c[:, C_ID:C_ID + P] = np.eye(P)
    c[:, C_UI:C_UI + P] = p[:, None] <= p[None, :]
    c[:, C_US:C_US + P] = p[:, None] < p[None, :]
    c[:, C_MN:C_MN + P] = np.where(p[:, None] <= p[None, :], 0.0, -1e30)
    c[:, C_ONE:C_ONE + P] = 1.0
    for n in range(LEVELS):
        m = 1 << n
        j, i = p[:, None] // m, p[None, :] // m
        c[:, C_LM + n * P:C_LM + (n + 1) * P] = (i // 2 == j // 2) & (i % 2 == 1) & (j % 2 == 0)
    c[:, C_COL + 7] = 1.0
    c[:, C_IO:C_IO + NE] = np.arange(NE)
    c[:, C_GI:C_GI + NE] = np.arange(NE) // EG
    c[:, C_HALF] = p // CAP
    c[:, C_EC:C_EC + NE] = np.arange(NE) % 2 * (NE // 2) + np.arange(NE) // 2
    for t, tile in enumerate(ORDER):
        real = tile * P + p < T
        c[:, C_ROWID + t] = np.where(real, tile * P + p, NOWHERE)
        c[:, C_TILE + t] = real
        c[:, C_PAD + t] = np.where(real, 0.0, NOWHERE)
    for m in range(8):
        c[m, C_SEL + m * P:C_SEL + (m + 1) * P] = 1.0
    return c


def bcast(ap, n):
    return ap.unsqueeze(2).broadcast_to([ap.shape[0], ap.shape[1], n])


def build(nc, A, R):
    with ExitStack() as ctx:
        base = (nc.sbuf_base + 31) // 32 * 32

        class Region:

            def __init__(self, start, end):
                self.at, self.end = (start + 31) // 32 * 32, end

            def __call__(self, name, shape, dt=F32):
                n = 2 if dt == mybir.dt.bfloat16 else 4
                for d in shape[1:]:
                    n *= d
                t = nc.alloc_sbuf_tensor_at(name, shape, dt, offset=base + self.at)
                self.at += (n + 31) // 32 * 32
                assert self.at <= self.end, (name, self.at, self.end)
                return t

        def sem(name):
            return ctx.enter_context(nc.semaphore(name))

        h2d = nc.dram_tensor("h2_rows", [T, D], F32, kind="Internal").ap()
        tab = nc.dram_tensor("slot_table", [MAXROWS * NE, 1], I32, kind="Internal").ap()
        yd = nc.dram_tensor("expert_rows", [2 * T * 2, D // 2], F32, kind="Internal").ap()

        ps = ctx.enter_context(nc.psum_tensor("ps", [P, 8, 512], F32))

        K1 = 44064 + 256
        K2 = K1 + 55328
        K3 = K2 + 26208
        K4 = K3 + 16672
        K5 = (nc.sbuf_usable_end - base) // 32 * 32
        keep = Region(0, K1)
        x = keep("x", [P, NT, D])
        cst = keep("cst", [P, C_END])
        gfb = keep("gfb", [P, D])
        sb = Region(keep.at, keep.at + 1024)("sb", [P, 8, H * NS])
        parq = keep("parq", [P, CQ, ROWS_Q])
        parab = keep("parab", [P, 2, ROWS_AB])
        g1c = keep("g1c", [P, KT])
        wgt = keep("wgt", [P, 2, NT])
        pid = keep("pid", [P, 2, NT], I32)
        where = keep("where", [P, 2, NT], I32)
        graw = keep("graw", [P, NE // 2], I32)
        sraw = keep("sraw", [P, NE], I32)
        gidx = keep("gidx", [P, NE // 2], I32)
        sidx = keep("sidx", [P, NE], I32)
        idf = keep("idf", [P, 2, NE])
        more = keep("more", [1, NE], I32)
        moref = keep("moref", [1, 2, NE])
        ogc = keep("ogc", [P, 1])
        ogh = keep("ogh", [P, 1])
        epsc = keep("epsc", [P, 1])
        lnh = keep("lnh", [P, 2, 2])
        alog = keep("alog", [P, H])
        dtb = keep("dtb", [P, H])
        ss = keep("ss", [P, NT])
        rstd = keep("rstd", [P, NT])
        ba = keep("ba", [P, NT, 8])
        gw = keep("gw", [P, 10, NT, H])
        stq = keep("stq", [P, CQ, 27])
        sta = keep("sta", [P, 2, 2 + NS * 2])
        stp = keep("stp", [P, 2, WB - 1])
        small = keep("small", [P, CQ, NS])
        kq = keep("kq", [P, H, NS, 2])
        wr = keep("wr", [P, KT, NG + NE])
        nowhere = keep("nowhere", [P, MAXROWS * NE // P], I32)

        proj = Region(K1, K2)
        hhi = proj("hhi", [P, KT, T], F32R)
        hlo = proj("hlo", [P, KT, T], F32R)
        whi = [proj(f"whi{s}", [P, KT, P], F32R) for s in range(WSLOTS)]
        at = [proj.at]
        wraw = [proj("wraw0", [P, KT, P])]
        late = Region(K1, K2)
        wout = late("wout", [P, KT, D])
        s0 = late("s0", [P, H, NS, P])
        g2b = late("g2b", [P, D])
        stb = Region(K5 - 1920, K5)("stb", [P, 2, NS * (WB - 1)])

        hT = Region(K2, K3)("hT", [P, KT, T])
        convd = Region(K2, K3)
        cv = [convd(f"cv{n}", [P, CV]) for n in range(CQ)]
        mixed = Region(K3, K4)
        yT = mixed("yT", [P, 8, T])

        first = Region(K4, K5 - 1920)
        at += [first.at + n * 4096 for n in range(WSLOTS - 1)]
        wraw += [first(f"wraw{s}", [P, KT, P]) for s in range(1, WSLOTS)]
        wlo = [Region(a, a + 4096)(f"wlo{s}", [P, KT, P], F32R) for s, a in enumerate(at)]
        raw = [first(f"raw{s}", [P, RAW]) for s in range(3)]
        begin = Region(first.at, first.at + 8704)
        hrow = [begin(f"hrow{s}", [P, KT, P]) for s in range(2)]
        silu = Region(first.at, first.at + 8704)
        th = [silu(f"th{s}", [P, CV]) for s in range(2)]
        sq = [silu(f"sq{s}", [P, CV]) for s in range(2)]
        first.at += 8704
        rowq = first("rowq", [ROWS_Q, CQ * P])
        rowab = first("rowab", [ROWS_AB, DB])
        rowsb = first("rowsb", [120, 2, DB])
        wba = first("wba", [P, KT, 8])
        convolved = Region(first.at, first.at + 6528)
        acc = [convolved(f"acc{s}", [P, CV]) for s in range(3)]
        bval = [first(f"bval{t}", [P, T]) for t in range(2)]
        bth = [first(f"bth{t}", [P, T]) for t in range(2)]
        gates = Region(K3 + 16 * T, K4)
        mab = [gates(f"mab{t}", [P, T]) for t in range(2)]
        mac = [gates(f"mac{t}", [P, T]) for t in range(2)]
        mah = [first(f"mah{t}", [P, T]) for t in range(2)]
        ub = [first(f"ub{t}", [P, WB - 1 + SEQ]) for t in range(2)]
        usb = first("usb", [P, 2, NS, WB])
        sprod = first("sprod", [P, NS, WB])
        ua = [first(f"ua{t}", [P, WA - 1 + SEQ]) for t in range(2)]
        uas = first("uas", [P, 2, NS, WA])
        rn = first("rn", [8, 2, CV])

        delta = Region(K4, K5 - 1920)
        four = [P, TT, P]
        wT = [delta(f"wT{z}", four) for z in range(2)]
        t1 = [delta(f"t1{z}", four) for z in range(2)]
        vn = [delta(f"vn{z}", four) for z in range(2)]
        S = [[delta(f"S{z}{s}", [P, P]) for s in range(2)] for z in range(2)]
        grep = [delta(f"grep{z}", four) for z in range(2)]
        brep = [delta(f"brep{z}", four) for z in range(2)]
        kbG, kd = grep, brep
        eG = [delta(f"eG{z}", four) for z in range(2)]
        qG = [delta(f"qG{z}", four) for z in range(2)]
        kb = [delta(f"kb{z}", four) for z in range(2)]
        DT = [delta(f"DT{z}", four) for z in range(2)]
        AT = [delta(f"AT{z}", four) for z in range(2)]
        att = [delta(f"att{z}", four) for z in range(2)]
        BT = [[delta(f"BT{z}{s}", four) for s in range(2)] for z in range(2)]
        XX = [delta(f"XX{z}", [P, 2, TT, P]) for z in range(2)]
        vb = kb
        bsq = [delta(f"bsq{t}", [P, T]) for t in range(2)]
        dg = delta("dg", [NS, 2, H, NS])
        kqs = delta("kqs", [P, H * NS, 2])
        mix = Region(K4, K5 - 49152)
        samples = Region(K5 - 24576, K5)
        srow = samples("srow", [NS, 2, H * P])
        vnd = samples("vnd", [NS, NS, P])
        osq = [mix(f"osq{s}", [P, T]) for s in range(2)]
        rno = mix("rno", [8, 2, T])
        rowq2 = mix("rowq2", [27, CQ * P])
        rowab2 = mix("rowab2", [18, DB])
        rowsb2 = mix("rowsb2", [120, 2, DB])
        rowb = mix("rowb", [WB - 1, DB])
        route = Region(K4, K5 - 49152)
        h2row = [route(f"h2row{s}", [P, KT, P]) for s in range(2)]
        h2T = route("h2T", [P, KT, P])
        tail = Region(K2 + 24576, K3)
        L = tail("L", [P, NT, NG + NE])
        ns = tail("ns", [P, 12, NT])
        g4 = tail("g4", [P, 3, NT, NG])
        sqj = route("sqj", [P, D], mybir.dt.bfloat16)
        eight = [route(f"eight{n}", [P, NT, NE]) for n in range(7)]
        wslots = [Region(a, a + 24576) for a in (K2, K5 - 49152, K5 - 24576, K1)]
        gu = [r(f"gu{n}", [P, 2, KT, F]) for n, r in enumerate(wslots)]
        wd = [r(f"wd{n}", [P, 2, D]) for n, r in enumerate(wslots)]
        moe = Region(K1 + 24576, K2)
        xg = [moe(f"xg{s}", [P, D]) for s in range(2)]
        xT = [moe(f"xT{s}", [P, KT, P]) for s in range(2)]
        ysb = [moe(f"ysb{s}", [P, D // 2]) for s in range(4)]
        yk = [Region(a, a + 8192)(f"yk{i}", [P, 2, D]) for i, a in enumerate(
            (K2, K2 + 8192, K5 - 49152, K5 - 49152 + 8192, K5 - 24576))]
        fsq = Region(K2 + 16384, K3)("fsq", [P, D])
        moe2 = Region(K3, K4)
        gth = [moe2(f"gth{s}", [P, P]) for s in range(2)]
        gact = [moe2(f"gact{s}", [P, P]) for s in range(2)]
        aT = [moe2(f"aT{s}", [P, P]) for s in range(2)]
        gcur = [moe2(f"gcur{s}", [P, 1], I32) for s in range(2)]
        zero = moe2("zero", [P, 1], I32)
        scur = [moe2(f"scur{s}", [P, 1], I32) for s in range(4)]
        xTo = moe2("xTo", [P, KT, CAP])
        oth, oact, oaT = (moe2(n, [P, P]) for n in ("oth", "oact", "oaT"))
        yo = moe2("yo", [P, D // 2])
        otok = [moe2(f"otok{s}", [P, 1], I32) for s in range(2)]
        osid = moe2("osid", [P, 1], I32)
        further = Region(K4, K5 - 49152)
        oraw = further("oraw", [P, MORE, NE], I32)
        oidf = [further(f"oidf{n}", [P, MORE, NE]) for n in range(2)]
        otoks = further("otoks", [P, (MORE + 1) * NE], I32)
        osids = further("osids", [P, MORE * NE], I32)
        xo = [further(f"xo{s}", [CAP, D]) for s in range(2)]
        sfin = late("sfin", [P, H, P])
        nG, eGc, sc1, sc3, gdif, kds = (gw[:, n] for n in (2, 3, 4, 5, 6, 8))

        ident = cst[:, C_ID:C_ID + P]
        incl = cst[:, C_UI:C_UI + P]
        ones = cst[:, C_ONE:C_ONE + P]

        def column(m):
            return cst[:, C_COL + 7 - m:C_COL + 15 - m]

        def select(m):
            return cst[0:8, C_SEL + m * P:C_SEL + (m + 1) * P]

        def rows(i):
            return NS if ORDER[i] == TT else P

        def tokens(i):
            return slice(i * P, min((i + 1) * P, T))

        x_in = [sem(f"x_in{i}") for i in range(NT)]
        g1_in = sem("g1_in")
        consts_in, rows_in, small_in = sem("consts_in"), sem("rows_in"), sem("small_in")
        weights_in = [sem(f"weights_in{s}") for s in range(WSLOTS)]
        tiles_in = [16 * len(range(s, NZ, WSLOTS)) for s in range(WSLOTS)]
        w_hi, w_lo, h_hi, h_lo = sem("w_hi"), sem("w_lo"), sem("h_hi"), sem("h_lo")
        x_squared, rstd_ready = sem("x_squared"), sem("rstd_ready")
        hrow_ready, h_turned, hT_ready = sem("hrow_ready"), sem("h_turned"), sem("hT_ready")
        rows_turned, params_ready = sem("rows_turned"), sem("params_ready")
        ba_done, ba_ready = sem("ba_done"), sem("ba_ready")
        z_done, z_evac = sem("z_done"), sem("z_evac")
        glu_ready = sem("glu_ready")
        first_tap, qG_ready = sem("first_tap"), sem("qG_ready")
        conv_done, tanh_done, cv_done, squared, sums_done = (
            sem("conv_done"), sem("tanh_done"), sem("cv_done"), sem("squared"), sem("sums_done"))
        raw_saved = sem("raw_saved")
        sums_ready, norms_ready, norms_spread, qk_ready = (
            sem("sums_ready"), sem("norms_ready"), sem("norms_spread"), sem("qk_ready"))
        gate_tanh, a_mixed, b_conved = sem("gate_tanh"), sem("a_mixed"), sem("b_conved")
        states_ready, states_out = sem("states_ready"), sem("states_out")
        g_scalar, g_vector, g_ready, g_summed = sem("g_scalar"), sem("g_vector"), sem("g_ready"), sem("g_summed")
        s_act, s_vec, s_pool = sem("act_step"), sem("vec_step"), sem("pool_step")
        g_cols, col_scales = sem("g_cols"), sem("col_scales")
        small_saved = sem("small_saved")

        def both(z, n, each=1):
            turns, rest = divmod(n - 1, each)
            return (2 * turns + z) * each + rest + 1

        def pair(name):
            return [sem(f"{name}{z}") for z in range(2)]

        rep_ready, spread, eG_ready, D_ready, DT_ready = sem("rep_ready"), sem("spread"), sem("eG_ready"), sem("D_ready"), sem("DT_ready")
        kb_ready, scored, rows_done, A_ready, rows_scaled = (
            sem("kb_ready"), sem("scored"), sem("rows_done"), sem("A_ready"), sem("rows_scaled"))
        XT0_ready, X0_done, X0_ready, BT_ready, T1_done, T1_ready, T2_done, X_ready = (
            sem("XT0_ready"), sem("X0_done"), sem("X0_ready"), sem("BT_ready"), sem("T1_done"), sem("T1_ready"),
            sem("T2_done"), sem("X_ready"))
        wT_done, wT_ready, vn_done, vn_ready, S_done, S_ready, o_done, o_ready = (
            sem("wT_done"), sem("wT_ready"), sem("vn_done"), sem("vn_ready"), sem("S_done"), sem("S_ready"),
            sem("o_done"), sem("o_ready"))
        finals_out = sem("finals_out")
        s0_in, wout_in = sem("s0_in"), sem("wout_in")
        ds_vec, ds_prod, ds_act, ds_row, ds_rowed, ds_diag = (
            sem("ds_vec"), sem("ds_prod"), sem("ds_act"), sem("ds_row"), sem("ds_rowed"), sem("ds_diag"))
        s0_decayed, s0_outer, s0_ready = sem("s0_decayed"), sem("s0_outer"), sem("s0_ready")
        osq_ready, osum_done, oroot_ready, onorm_ready, ospread, oscaled = (
            sem("osq_ready"), sem("osum_done"), sem("oroot_ready"), sem("onorm_ready"), sem("ospread"), sem("oscaled"))
        b_pe, b_vec, b_act, yb_ready = sem("b_pe"), sem("b_vec"), sem("b_act"), sem("yb_ready")
        wout_done, x1_ready, x1_squared, r2_ready = sem("wout_done"), sem("x1_ready"), sem("x1_squared"), sem("r2_ready")
        h2_ready, h2_turned, h2T_ready, logits_done, logits_ready, h2_stored = (
            sem("h2_ready"), sem("h2_turned"), sem("h2T_ready"), sem("logits_done"), sem("logits_ready"), pair("h2_stored"))
        rt_vec, rt_act, routed, ranked = sem("rt_vec"), sem("rt_act"), sem("routed"), sem("ranked")
        tab_written, slots_in, idx_ready = sem("tab_written"), sem("slots_in"), sem("idx_ready")
        xg_in = pair("xg_in")
        y_out = [sem(f"y_out{n}") for n in range(4)]
        gidx_set, sidx_set, xg_turned, xT_ready = sem("gidx_set"), sem("sidx_set"), sem("xg_turned"), sem("xT_ready")
        up_done, up_tanh, act_half, act_ready, act_turned, aT_ready, down_done, y_ready = (
            sem("up_done"), sem("up_tanh"), sem("act_half"), sem("act_ready"), sem("act_turned"), sem("aT_ready"),
            sem("down_done"), sem("y_ready"))
        expert_done, moe_done = sem("expert_done"), sem("moe_done")
        m_rows = pair("more_rows")
        m_otok, m_osid, m_pe, m_act, m_vec, m_out, m_saved = (
            sem("more_" + n) for n in ("otok", "osid", "pe", "act", "vec", "out", "saved"))
        fin_added, fin_ready = sem("fin_added"), sem("fin_ready")
        wr_in, pool_passed = sem("wr_in"), sem("pool_passed")
        cleared = sem("cleared")

        block = ctx.enter_context(nc.Block())

        def linker(eng, semaphore):
            n = [0]

            def link(ins):
                n[0] += 1
                ins.then_inc(semaphore, 1)
                eng.wait_ge(semaphore, n[0])
            return link

        qk_index = {}
        for m, tile in enumerate(QKV):
            if tile < 8:
                qk_index[m] = len(qk_index)

        LAST_SUM = [ZQ + 3 + m for m, j in qk_index.items() if j % 4 == 3]
        SPREAD = [LAST_SUM[j // 4] + 2 + j % 4 for j in range(8)]

        def more_groups(eng, e, body):
            n = eng.value_load(more[0:1, bass.ds(e, 1)], min_val=0, max_val=MORE)
            with eng.If(n > 0):
                body(0, eng.snap(groups_done[eng]), n)
                eng.reg_add(groups_done[eng], groups_done[eng], 1)
                with eng.If(n > 1):
                    with eng.Fori(1, MORE) as g:
                        with eng.If(n > g):
                            body(g, eng.snap(groups_done[eng]), n)
                            eng.reg_add(groups_done[eng], groups_done[eng], 1)

        groups_done = {}

        def count_groups(eng, name):
            groups_done[eng] = eng.alloc_register(f"groups_done_{name}")
            eng.reg_mov(groups_done[eng], 0)

        ROUND = 4
        ROUNDS = NE // ROUND

        def rounds(eng, body):
            body(0, True, False)
            with eng.Fori(1, ROUNDS - 1) as it:
                body(it, False, False)
            body(ROUNDS - 1, False, True)

        def rest_of_tokens(eng, i):
            eng.wait_ge(h_hi, i + 1)
            eng.tensor_tensor(hlo[:, :, tokens(i)], hT[:, :, tokens(i)], hhi[:, :, tokens(i)], ALU.subtract).then_inc(h_lo, 1)

        @block.sync
        def _(sp):
            xp = A["x_prompt"].rearrange("o (i p) d -> (o i) p d", p=P)
            w_in_cols = A["w_in"].rearrange("o (p c) e -> (o p) c e", c=KT)

            def load_tile(n):
                if n >= WSLOTS:
                    sp.wait_ge(z_done, n - WSLOTS + 1)
                column = BLOCKS[n // 2] * 256 + n % 2 * P
                sp.dma_start(wraw[n % WSLOTS][:, :, :], w_in_cols[:, :, column:column + P]).then_inc(weights_in[n % WSLOTS], 16)

            for i in range(TT):
                sp.dma_start(x[:, i, :], xp[i]).then_inc(x_in[i], 16)
            sp.dma_start(x[0:NS, TT, :], A["x_sample"].rearrange("b o d -> (b o) d")).then_inc(x_in[TT], 16)
            sp.dma_start(g1c[:, :], A["norm1_g"].rearrange("o (p c) -> (o p) c", c=KT)).then_inc(g1_in, 16)
            sp.dma_start(cst[:, :], A["consts"]).then_inc(consts_in, 16)
            for n in range(WSLOTS):
                load_tile(n)
            for dst, src in (
                (rowq[0:WC, :], A["conv_c_w"][0]),
                (rowq[WC:ROWS_Q, :], A["state_conv_qkv"].rearrange("o b j e -> (o b j) e")),
                (rowab[0:WB, :], A["conv_b_w"][0]),
                (rowab[LNG:LNG + 1, :], A["ln_b_g"]),
                (rowab[LNB:LNB + 1, :], A["ln_b_b"]),
                (rowab[CAW:STA, :], A["conv_a_w"][0]),
                (rowab[STA:ROWS_AB, :], A["state_conv_a"].rearrange("o b j e -> (o b j) e")),
                (rowsb[:, :, :], A["state_conv_b"].rearrange("o (a b) j e -> (o b j) a e", a=2)),
            ):
                sp.dma_start(dst, src).then_inc(rows_in, 16)
            for dst, src in (
                (wba[:, :, :], w_in_cols[:, :, 3328:3336]),
                (ogc[:, :], A["o_norm_g"].rearrange("o p -> p o")),
                (alog[:, :], A["a_log"].broadcast_to([P, H])),
                (dtb[:, :], A["dt_bias"].broadcast_to([P, H])),
                (gfb[:, :], A["final_g"].unsqueeze(0).broadcast_to([P, D])),
            ):
                sp.dma_start(dst, src).then_inc(small_in, 16)
            for n in range(WSLOTS, NZ):
                load_tile(n)
            w_router = A["w_router"][0]
            sp.dma_start(wr[:, :, 0:NG], A["w_group"].rearrange("o (p c) g -> (o p) c g", c=KT)).then_inc(wr_in, 16)
            for g in range(NG):
                sp.dma_start(wr[:, :, NG + g * EG:NG + (g + 1) * EG], w_router[g].rearrange("(p c) e -> p c e", c=KT)).then_inc(
                    wr_in, 16)
            sp.wait_ge(cleared, 3)
            sp.dma_start(tab.rearrange("(p n) o -> p (n o)", p=P), nowhere[:, :]).then_inc(slots_in, 16)
            sp.wait_ge(z_done, NZ)
            sp.wait_ge(cv_done, CQ)
            sp.wait_ge(raw_saved, 3 + 2 * CQ)
            for h in range(H):
                sp.dma_start(s0[:, h], A["state_delta"][0, :, h].rearrange("b k v -> k b v")).then_inc(s0_in, 16)
            sp.dma_start(wout[:, :, :], A["w_out"].rearrange("o (k p) d -> (o p) k d", p=P)).then_inc(wout_in, 16)
            sp.dma_start(g2b[:, :], A["norm2_g"].broadcast_to([P, D])).then_inc(wout_in, 16)
            w_gu = [A[n].rearrange("o e (p c) f -> (o e) p c f", c=KT) for n in ("w_gate", "w_up")]
            w_down = A["w_down"].rearrange("o e (c p) d -> (o e) p c d", c=2)

            def load_expert(e, u):
                for n in range(2):
                    sp.dma_start(gu[u][:, n], w_gu[n][bass.ds(e, 1)].rearrange("o p c f -> (o p) c f")).then_inc(weights_in[u], 16)
                sp.dma_start(wd[u][:, :, :], w_down[bass.ds(e, 1)].rearrange("o p c d -> (o p) c d")).then_inc(weights_in[u], 16)

            for z in range(2):
                sp.wait_ge(S_ready, both(z, 2 * TT))
                sp.wait_ge(o_ready, both(z, 2))
            load_expert(1, 1)
            sp.dma_start(R["d_p"][0, 0].rearrange("h k v -> k h v"), sfin[:, :, :]).then_inc(finals_out, 16)
            sp.wait_ge(finals_out, 16)
            sp.wait_ge(states_ready, 5)
            for dst, src in (
                (R["cq_p"][0, 0], rowq2[0:3, :]),
                (R["cq_s"].rearrange("o b j e -> (o b j) e"), rowq2[3:27, :]),
                (R["ca_p"][0, 0], rowab2[0:2, :]),
                (R["ca_s"].rearrange("o b j e -> (o b j) e"), rowab2[2:18, :]),
                (R["cb_p"][0, 0], rowb[:, :]),
                (R["cb_s"].rearrange("o (a b) j e -> (o b j) a e", a=2), rowsb2[:, :, :]),
            ):
                sp.dma_start(dst, src).then_inc(states_out, 16)
            sp.wait_ge(oscaled, 4)
            load_expert(0, 0)
            for i in range(NT):
                n = rows(i)
                if 1 <= i <= H:
                    sp.wait_ge(s0_ready, 2 * i)
                    sp.dma_start(R["d_s"][0, :, i - 1].rearrange("b k v -> k b v"), s0[:, i - 1]).then_inc(finals_out, 16)
                if i == H:
                    load_expert(2, 2)
                sp.wait_ge(h2_ready, i + 1)
                sp.dma_start(h2d[ORDER[i] * P:ORDER[i] * P + n, :], h2row[i % 2][0:n].rearrange("t c p -> t (c p)")).then_inc(
                    h2_stored[i % 2], 16)
            sp.wait_ge(finals_out, (H + 1) * 16)
            sp.wait_ge(wout_done, NT)
            load_expert(3, 3)
            sp.wait_ge(tab_written, 2 * NT * 16)
            slots = tab.rearrange("(r e) o -> r (e o)", e=NE)[0:CAP]
            sp.dma_start(graw[0:CAP, :], slots[:, 0:NE // 2]).then_inc(slots_in, 16)
            sp.dma_start(graw[CAP:P, :], slots[:, NE // 2:NE]).then_inc(slots_in, 16)
            for half in range(2):
                sp.dma_start(sraw[half * CAP:(half + 1) * CAP, :], slots[:, :]).then_inc(slots_in, 16)
            for s in range(2):
                sp.wait_ge(h2_stored[s], 16 * ((NT + 1 - s) // 2))
            sp.wait_ge(logits_done, NT)
            for half in range(2):
                sp.dma_start(oraw[half * CAP:(half + 1) * CAP], tab.rearrange("(g r e) o -> r g (e o)", r=CAP, e=NE)[:, 1:]).then_inc(
                    slots_in, 16)
            with sp.Fori(1, ROUNDS) as it:
                for u in range(ROUND):
                    sp.wait_ge(expert_done, ROUND * (it - 1) + u + 1)
                    load_expert(ROUND * it + u, u)
            sp.wait_ge(moe_done, 1)
            yrows = yd.rearrange("(r b) d -> r (b d)", b=2)
            for i in range(NT):
                n = rows(i)
                for k in range(2):
                    sp.dma_start(yk[i][0:n, k, :], yrows[k * T + ORDER[i] * P:k * T + ORDER[i] * P + n]).then_inc(x_in[i], 16)
            for i in range(NT):
                n = rows(i)
                sp.wait_ge(fin_ready, i + 1)
                dst = R["y_p"][0, tokens(ORDER[i]), :] if n == P else R["y_s"].rearrange("b o d -> (b o) d")
                sp.dma_start(dst, x[0:n, ORDER[i], :]).then_inc(finals_out, 16)
            sp.wait_ge(finals_out, (H + 1 + NT) * 16)

        @block.scalar
        def _(act):
            link = linker(act, s_act)
            copy = nc.scalar.activation

            for i in range(NT):
                act.wait_ge(x_in[i], 16)
                n = P if i < TT else NS
                if i == 0:
                    act.wait_ge(cleared, 1)
                if i >= 2:
                    act.wait_ge(x_squared, i - 1)
                copy(yT[0:n, 2 * (i % 2):2 * (i % 2) + 2, 0:512], x[0:n, i, :].rearrange("p (a b) -> p a b", a=2), ACT.Square,
                     accum_out=ss[0:n, i:i + 1]).then_inc(x_squared, 1)
            act.wait_ge(x_squared, NT)
            act.wait_ge(cleared, 2)
            copy(ss[:, :], ss[:, :], ACT.Sqrt, scale=1.0 / D, bias=epsc[:, :]).then_inc(x_squared, 1)
            def round_tokens(i):
                act.wait_ge(hT_ready, i + 1)
                copy(hhi[:, :, tokens(i)], hT[:, :, tokens(i)], ACT.Copy).then_inc(h_hi, 1)

            def round_weights(n):
                act.wait_ge(weights_in[n % WSLOTS], 16 * (n // WSLOTS + 1))
                copy(whi[n % WSLOTS][:, :, :], wraw[n % WSLOTS][:, :, :], ACT.Copy).then_inc(w_hi, 1)

            for i in range(NT):
                round_tokens(i)
                if i < WSLOTS - 1:
                    round_weights(i)
            def decays():
                act.wait_ge(ba_done, 1)
                act.wait_ge(cleared, 4)
                copy(ba[:, 0:TT, :], ps[:, 7, 0:TT * 8].rearrange("p (i e) -> p i e", e=8), ACT.Copy).then_inc(ba_ready, 1)
                copy(ba[0:NS, TT, :], ps[0:NS, 7, TT * 8:NT * 8], ACT.Copy).then_inc(ba_ready, 1)
                act.wait_ge(ba_ready, 2)
                act.wait_ge(small_in, 5 * 16)
                copy(gw[:, 0, :, :], ba[:, :, 0:4], ACT.Exp, scale=-1.0).then_inc(g_scalar, 1)
                copy(gw[:, 9, 0, :], alog[:, :], ACT.Exp).then_inc(g_scalar, 1)
                act.wait_ge(g_vector, 1)
                copy(gw[:, 3, :, :], gw[:, 2, :, :], ACT.Exp, scale=-1.0).then_inc(g_scalar, 1)
                act.wait_ge(g_vector, 2)
                copy(gw[:, 5, :, :], gw[:, 4, :, :], ACT.Ln).then_inc(g_scalar, 1)

            def cumulated():
                act.wait_ge(g_summed, 1)
                act.wait_ge(g_ready, 2)
                copy(nG[:, 0:TT], ps[:, 7, 0:TT * H].rearrange("p (i h) -> p i h", h=H), ACT.Copy, scale=-1.0).then_inc(g_cols, 1)
                copy(eGc[:, 0:TT], ps[:, 7, 0:TT * H].rearrange("p (i h) -> p i h", h=H), ACT.Exp).then_inc(g_cols, 1)

            def evacuate(n):
                act.wait_ge(z_done, n + 1)
                b = 2 * (n % 2)
                prompt, sample = ps[:, b:b + 2, 0:256], ps[:, b + 1, 256:264]
                f, scale = ACT.Copy, 1.0
                if n < 2:
                    dst, scale = bval[n], 0.5
                elif n < 4:
                    dst, f, scale = bth[n - 2], ACT.Tanh, 0.5
                elif n < ZQ:
                    dst = (mab, mac, mah)[(n - ZA) // 2][n % 2]
                elif n < ZG:
                    m = n - ZQ
                    if m == 0:
                        act.wait_ge(h_turned, NT)
                    dst = raw[m % 3]
                    if m >= 3:
                        act.wait_ge(conv_done, m - 2)
                        act.wait_ge(raw_saved, 3 + 2 * (m - 2))
                    else:
                        act.wait_ge(raw_saved, 3)
                    act.wait_ge(params_ready, 3)
                    link(copy(dst[:, WC - 1 + SEQ:RAW].rearrange("p (b j) -> p b j", j=WC)[:, :, 0:WC - 1],
                              parq[:, QKV[m], WC:ROWS_Q].rearrange("p (b j) -> p b j", j=WC - 1), ACT.Copy))
                    copy(dst[:, WC - 1:WC - 1 + SEQ].rearrange("p (a b) -> p a b", a=2), prompt, ACT.Copy)
                    copy(dst[:, WC - 1 + SEQ:RAW].rearrange("p (b j) -> p b j", j=WC)[:, :, WC - 1:WC],
                         sample.unsqueeze(2), ACT.Copy).then_inc(z_evac, 1)
                    return
                else:
                    g = n - ZG
                    if g == 0:
                        act.wait_ge(a_mixed, 2)
                    yg = yT[:, 4 + g, :]
                    link(copy(yg[:, 0:SEQ].rearrange("p (a b) -> p a b", a=2), prompt, ACT.Copy))
                    link(copy(yg[:, SEQ:T], sample, ACT.Copy))
                    dst, f, scale = th[g % 2], ACT.Tanh, 0.5
                    if g < 2:
                        act.wait_ge(cv_done, CQ)
                    else:
                        act.wait_ge(gate_tanh, g - 1)
                copy(dst[:, 0:SEQ].rearrange("p (a b) -> p a b", a=2), prompt, f, scale=scale)
                copy(dst[:, SEQ:T], sample, f, scale=scale).then_inc(z_evac, 1)

            def tanh(m):
                act.wait_ge(conv_done, m + 1)
                if m >= 2:
                    act.wait_ge(cv_done, m - 1)
                copy(th[m % 2][:, :], acc[m % 3][:, :], ACT.Tanh, scale=0.5).then_inc(tanh_done, 1)

            def square(m):
                if QKV[m] >= 8:
                    return
                j = qk_index[m]
                act.wait_ge(cv_done, m + 1)
                if j >= 2:
                    act.wait_ge(sums_done, j - 1)
                copy(sq[j % 2][:, :], cv[QKV[m]][:, :], ACT.Square).then_inc(squared, 1)

            def start_conv(m):
                act.wait_ge(z_evac, ZQ + m + 1)
                if m == 0:
                    act.wait_ge(glu_ready, 4)
                if m >= 3:
                    act.wait_ge(cv_done, m - 2)
                copy(acc[m % 3][:, :], raw[m % 3][:, 0:CV], ACT.Copy, scale=parq[:, QKV[m], 0:1]).then_inc(first_tap, 1)

            def root(g):
                act.wait_ge(sums_done, 4 * g + 4)
                if g:
                    act.wait_ge(norms_ready, g)
                copy(rn[:, 0, :].rearrange("p (a b) -> p a b", a=2), ps[0:8, 4:6, 0:HC], ACT.Sqrt, scale=0.25,
                     bias=epsc[0:8, :]).then_inc(sums_ready, 1)

            for n in range(NZ + 3):
                for g in range(2):
                    if n == LAST_SUM[g] + 1:
                        root(g)
                if 0 <= n - ZQ - 1 < CQ:
                    tanh(n - ZQ - 1)
                if 0 <= n - ZQ - 2 < CQ:
                    square(n - ZQ - 2)
                if n < NZ:
                    evacuate(n)
                if 0 <= n - ZQ < CQ:
                    start_conv(n - ZQ)
                if n + WSLOTS - 1 < NZ:
                    round_weights(n + WSLOTS - 1)
                if n == 3:
                    decays()
                if n == ZQ - 1:
                    cumulated()

            act.wait_ge(g_cols, 2)
            act.wait_ge(qk_ready, len(qk_index))

            def beside_level(hp, n):
                if hp == 0 and n == 2:
                    for t in range(2):
                        act.wait_ge(b_vec, t + 1)
                        copy(bsq[t][:, :], yT[:, 2 + t, :], ACT.Square).then_inc(b_act, 1)
                if hp == 0 and n == 4:
                    act.wait_ge(b_pe, 2)
                    for half in range(2):
                        ins = copy(bsq[0][:, half * HT:(half + 1) * HT], ps[:, 3 + 4 * half, 0:HT], ACT.Sqrt, scale=1.0 / DB,
                                   bias=epsc[:, :])
                    ins.then_inc(b_act, 1)
                if hp == 1 and n == 3:
                    act.wait_ge(ds_prod, 2)
                    copy(sb[:, 1, :], ps[:, 7, 0:H * NS], ACT.Copy).then_inc(ds_act, 1)
                    copy(sb[:, 2, :], ps[:, 7, 2 * H * NS:3 * H * NS], ACT.Exp).then_inc(ds_act, 1)
                    copy(sb[:, 3, :], ps[:, 7, 3 * H * NS:4 * H * NS], ACT.Copy).then_inc(ds_act, 1)
                if hp == 1 and n == 4:
                    for t in range(2):
                        act.wait_ge(b_vec, 5 + t)
                        copy(bsq[t][:, :], yT[:, 2 + t, :], ACT.Tanh).then_inc(b_act, 1)
                if hp == 1 and n == LEVELS - 1:
                    act.wait_ge(ds_prod, 3)
                    copy(kqs[:, :, :].rearrange("p a b -> p (a b)"), ps[:, 3, 0:2 * H * NS], ACT.Copy).then_inc(ds_act, 1)

            for hp in range(2):
                pairs = [(z, 2 * hp + z, 4 * z) for z in range(2)]
                for z, h, B in pairs:
                    act.wait_ge(spread, both(z, 2 * hp + 1, 2))
                    act.wait_ge(rep_ready, both(z, 2 * hp + 2, 2))
                    copy(eG[z][:, :, :].rearrange("p a b -> p (a b)"), ps[:, B, :], ACT.Exp).then_inc(eG_ready, 1)
                for z, h, B in pairs:
                    act.wait_ge(D_ready, both(z, 2 * hp + 2, 2))
                    for i in range(TT):
                        copy(DT[z][:, i, :], DT[z][:, i, :], ACT.Exp, bias=nG[:, i, h:h + 1]).then_inc(DT_ready, 1)
                    copy(kds[:, 0:TT, h], gdif[:, 0:TT, h], ACT.Exp).then_inc(DT_ready, 1)
                for z, h, B in pairs:
                    act.wait_ge(X0_done, both(z, hp + 1))
                    copy(XX[z][:, 0].rearrange("p a b -> p (a b)"), ps[:, B + 2, :], ACT.Copy).then_inc(X0_ready, 1)
                for n in range(1, LEVELS):
                    for z, h, B in pairs:
                        act.wait_ge(T1_done, both(z, (LEVELS - 1) * hp + n))
                        copy(t1[z][:, :, :].rearrange("p a b -> p (a b)"), ps[:, B + 2, :], ACT.Copy).then_inc(T1_ready, 1)
                    beside_level(hp, n)
                for z, h, B in pairs:
                    act.wait_ge(wT_done, both(z, hp + 1))
                    copy(wT[z][:, :, :].rearrange("p a b -> p (a b)"), ps[:, B + 2, :], ACT.Copy).then_inc(wT_ready, 1)
                for i in range(TT):
                    for z, h, B in pairs:
                        act.wait_ge(vn_done, both(z, TT * hp + i + 1))
                        copy(vn[z][:, i, :], ps[:, B + 3, i * P:(i + 1) * P], ACT.Copy).then_inc(vn_ready, 1)
                for z, h, B in pairs:
                    act.wait_ge(o_done, both(z, hp + 1))
                    act.wait_ge(small_saved, 2)
                    copy(cv[8 + h][:, 0:SEQ], ps[:, B + 1, :], ACT.Copy).then_inc(o_ready, 1)

            def square_output(h):
                if h == 0:
                    act.wait_ge(ds_vec, 8)
                if h >= 2:
                    act.wait_ge(osum_done, h - 1)
                copy(osq[h % 2][:, :], cv[8 + h][:, 0:T], ACT.Square).then_inc(osq_ready, 1)

            square_output(0)
            square_output(1)
            act.wait_ge(ds_row, 1)
            copy(srow[:, 0, :], ps[0:NS, 4, :], ACT.Copy).then_inc(ds_rowed, 1)
            copy(srow[:, 1, :], ps[0:NS, 5, :], ACT.Copy).then_inc(ds_rowed, 1)
            square_output(2)
            square_output(3)
            act.wait_ge(osum_done, H)
            copy(rno[:, 0, :].rearrange("p (a b) -> p a b", a=2), ps[0:8, 2:4, 0:HT], ACT.Sqrt, scale=1.0 / P,
                 bias=epsc[0:8, :]).then_inc(oroot_ready, 1)
            act.wait_ge(rows_turned, 4)
            copy(rowq2[:, 0:8 * P].rearrange("p (a b) -> p a b", a=2), ps[0:27, 6:8, :], ACT.Copy).then_inc(states_ready, 1)
            act.wait_ge(rows_turned, 5)
            copy(rowq2[:, 8 * P:], ps[0:27, 6, :], ACT.Copy).then_inc(states_ready, 1)
            copy(rowab2[:, :], ps[0:18, 7, 0:DB], ACT.Copy).then_inc(states_ready, 1)
            copy(rowb[:, :], ps[0:WB - 1, 7, DB:2 * DB], ACT.Copy).then_inc(states_ready, 1)
            act.wait_ge(rows_turned, 6)
            copy(rowsb2[:, :, :].rearrange("p a b -> p (a b)"), ps[0:120, 6, :], ACT.Copy).then_inc(states_ready, 1)

            def square_x1(i):
                n = rows(i)
                act.wait_ge(x1_ready, i + 1)
                if i == 0:
                    act.wait_ge(yb_ready, 2)
                    act.wait_ge(x_squared, NT)
                if i >= 1:
                    act.wait_ge(h2T_ready, i)
                copy(sqj[0:n, :], x[0:n, ORDER[i], :], ACT.Square, accum_out=ss[0:n, i:i + 1]).then_inc(x1_squared, 1)
                act.wait_ge(x1_squared, 2 * i + 1)
                copy(ss[0:n, i:i + 1], ss[0:n, i:i + 1], ACT.Sqrt, scale=1.0 / D, bias=epsc[0:n, :]).then_inc(x1_squared, 1)

            def evacuate_h2(i):
                n = rows(i)
                act.wait_ge(h2_turned, i + 1)
                if i >= 1:
                    act.wait_ge(logits_done, i)
                copy(h2T[:, :, 0:n], ps[:, 4:6, :].rearrange("p b (c t) -> p (b c) t", t=P)[:, :, 0:n], ACT.Copy).then_inc(
                    h2T_ready, 1)

            def evacuate_logits(start, end):
                act.wait_ge(logits_done, end)
                act.wait_ge(cleared, 5)
                if start == 0:
                    copy(L[0:NS, 0, :], ps[0:NS, 6, 0:NG + NE], ACT.Copy).then_inc(logits_ready, 1)
                    start = 1
                copy(L[:, start:end, :], ps[:, 6, start * (NG + NE):end * (NG + NE)].rearrange("p (i e) -> p i e", e=NG + NE),
                     ACT.Copy).then_inc(logits_ready, 1)

            for i in range(NT):
                square_x1(i)
                if i == SPLIT:
                    evacuate_logits(0, SPLIT)
                evacuate_h2(i)
            evacuate_logits(SPLIT, NT)
            act.wait_ge(rt_vec, 2)
            copy(g4[:, 1], g4[:, 0], ACT.Exp).then_inc(rt_act, 1)
            copy(ns[:, 5], ns[:, 4], ACT.Exp).then_inc(rt_act, 1)
            count_groups(act, "act")
            act.wait_ge(routed, 7)

            def act_round(it, first, last):
                for u in range(ROUND):
                    e = ROUND * it + u
                    if u == 1 or (u == 3 and not last):
                        xT_out(2 * it + (u + 1) // 2, (u + 1) // 2 % 2)
                    if u < 3:
                        if u == 0:
                            tanh_gate(e, 0)
                        tanh_gate(e + 1, (u + 1) % 2)
                    act_T(e, u % 2)

                    def body(g, done, needed):
                        act.wait_ge(m_pe, done * 4 + 1)
                        copy(xTo[:, :, :].rearrange("p a b -> p (a b)"), ps[:, 3, :], ACT.Copy).then_inc(m_act, 1)
                        act.wait_ge(m_pe, done * 4 + 2)
                        copy(oth[:, :], ps[:, 3, 0:P], ACT.Tanh, scale=0.5).then_inc(m_act, 1)
                        act.wait_ge(m_pe, done * 4 + 3)
                        copy(oaT[:, :], ps[:, 3, 0:P], ACT.Copy).then_inc(m_act, 1)

                    more_groups(act, e, body)

            def xT_out(j, s):
                act.wait_ge(xg_turned, j + 1)
                copy(xT[s][:, :, :], ps[:, 6:8, :].rearrange("p b (c t) -> p (b c) t", t=P), ACT.Copy).then_inc(xT_ready, 1)

            def tanh_gate(e, s):
                act.wait_ge(up_done, e + 1)
                copy(gth[s][:, :], ps[:, s, 0:P], ACT.Tanh, scale=0.5).then_inc(up_tanh, 1)

            def act_T(e, s):
                act.wait_ge(act_turned, e + 1)
                copy(aT[s][:, :], ps[:, 2, 0:P], ACT.Copy).then_inc(aT_ready, 1)

            xT_out(0, 0)
            rounds(act, act_round)
            for i in range(NT):
                n = rows(i)
                act.wait_ge(fin_added, 2 * i + 2)
                if i:
                    act.wait_ge(x1_squared, 2 * (NT + i))
                copy(fsq[0:n, :], x[0:n, ORDER[i], :], ACT.Square, accum_out=ss[0:n, i:i + 1]).then_inc(x1_squared, 1)
                act.wait_ge(x1_squared, 2 * (NT + i) + 1)
                copy(ss[0:n, i:i + 1], ss[0:n, i:i + 1], ACT.Sqrt, scale=1.0 / D, bias=epsc[0:n, :]).then_inc(x1_squared, 1)

        @block.gpsimd
        def _(pool):
            link = linker(pool, s_pool)
            nc.gpsimd.memset(ss[:, :], 1.0).then_inc(cleared, 1)
            nc.gpsimd.memset(epsc[:, :], EPS).then_inc(cleared, 1)
            nc.gpsimd.memset(nowhere[:, :], NOWHERE).then_inc(cleared, 1)
            nc.gpsimd.memset(ba[:, :, :], 0.0).then_inc(cleared, 1)
            for r in raw:
                nc.gpsimd.memset(r[:, 0:WC - 1], 0.0).then_inc(raw_saved, 1)
            for t in range(2):
                link(nc.gpsimd.memset(ub[t][:, 0:WB - 1], 0.0))
                link(nc.gpsimd.memset(ua[t][:, 0:WA - 1], 0.0))
            for i in range(2):
                rest_of_tokens(pool, i)

            def rest_of_weights(n):
                pool.wait_ge(w_hi, n + 1)
                s = n % WSLOTS
                nc.gpsimd.tensor_tensor(wlo[s][:, :, :], wraw[s][:, :, :], whi[s][:, :, :], ALU.subtract).then_inc(w_lo, 1)

            def glu():
                pool.wait_ge(z_evac, ZA)
                for t in range(2):
                    for out, c in ((ub[t][:, WB - 1:], slice(0, SEQ)), (usb[:, t, :, WB - 1], slice(SEQ, T))):
                        link(nc.gpsimd.tensor_tensor(bth[t][:, c], bth[t][:, c], bval[t][:, c], ALU.mult))
                        nc.gpsimd.tensor_tensor(out, bth[t][:, c], bval[t][:, c], ALU.add).then_inc(glu_ready, 1)
                pool.wait_ge(glu_ready, 4)
                pool.wait_ge(params_ready, 3)
                nc.gpsimd.tensor_copy(stp[:, 0, :], ub[0][:, SEQ:]).then_inc(glu_ready, 1)
                nc.gpsimd.tensor_copy(stp[:, 1, :], ub[1][:, SEQ:]).then_inc(glu_ready, 1)
                for t in range(2):
                    nc.gpsimd.tensor_copy(stb[:, t, :].rearrange("p (b j) -> p b j", j=WB - 1), usb[:, t, :, 1:WB]).then_inc(
                        glu_ready, 1)

            def mix_a(t, step):
                parts = ((slice(0, SEQ), lambda j: ua[t][:, j:j + SEQ]), (slice(SEQ, T), lambda j: uas[:, t, :, j]))
                if step == 0:
                    pool.wait_ge(z_evac, ZA + 5 + t)
                    link(nc.gpsimd.tensor_copy(uas[:, t, :, 0:WA - 1],
                                               parab[:, t, STA:ROWS_AB].rearrange("p (b j) -> p b j", j=WA - 1)))
                    link(nc.gpsimd.tensor_tensor(ua[t][:, WA - 1:], mac[t][:, 0:SEQ], mah[t][:, 0:SEQ], ALU.mult))
                    link(nc.gpsimd.tensor_tensor(uas[:, t, :, WA - 1], mac[t][:, SEQ:T], mah[t][:, SEQ:T], ALU.mult))
                    link(nc.gpsimd.tensor_copy(sta[:, t, 0:WA - 1], ua[t][:, SEQ:SEQ + WA - 1]))
                    link(nc.gpsimd.tensor_copy(sta[:, t, WA - 1:].rearrange("p (b j) -> p b j", j=WA - 1), uas[:, t, :, 1:WA]))
                    for c, u in parts:
                        link(nc.gpsimd.tensor_scalar(yT[:, t, c], u(0), parab[:, t, CAW:CAW + 1], None, ALU.mult))
                    return
                for c, u in parts:
                    link(nc.gpsimd.tensor_scalar(mac[t][:, c], u(step), parab[:, t, CAW + step:CAW + step + 1], None, ALU.mult))
                    link(nc.gpsimd.tensor_tensor(yT[:, t, c], yT[:, t, c], mac[t][:, c], ALU.add))
                if step == WA - 1:
                    nc.gpsimd.tensor_tensor(yT[:, t, :], yT[:, t, :], mab[t][:, :], ALU.mult).then_inc(a_mixed, 1)

            def save_columns(m):
                pool.wait_ge(z_evac, ZQ + m + 1)
                r, s = raw[m % 3], stq[:, QKV[m], :]
                nc.gpsimd.tensor_copy(s[:, 0:WC - 1], r[:, SEQ:SEQ + WC - 1]).then_inc(raw_saved, 1)
                nc.gpsimd.tensor_copy(s[:, WC - 1:].rearrange("p (b j) -> p b j", j=WC - 1),
                                      r[:, WC - 1 + SEQ:].rearrange("p (b j) -> p b j", j=WC)[:, :, 1:]).then_inc(raw_saved, 1)

            for n in range(NZ):
                rest_of_weights(n)
                done = n - WSLOTS + 1
                if done == ZA - 1:
                    glu()
                if 0 <= done - ZQ + 1 < 2 * WA:
                    mix_a(*divmod(done - ZQ + 1, WA))
                if 0 <= done - ZQ < CQ:
                    save_columns(done - ZQ)
            pool.wait_ge(qk_ready, len(qk_index))
            pool.wait_ge(cv_done, CQ)
            for h in range(H):
                for j, tile in enumerate((4 + h, h)):
                    link(nc.gpsimd.tensor_copy(kq[:, h, :, j], cv[tile][:, SC:CV:WC]))
            for n in range(CQ):
                ins = nc.gpsimd.tensor_copy(small[:, n, :], cv[n][:, SC:CV:WC])
                if n < CQ - 1:
                    link(ins)
            ins.then_inc(small_saved, 2)
            for hp in range(2):
                for z in range(2):
                    pool.wait_ge(eG_ready, both(z, hp + 1))
                    if hp:
                        pool.wait_ge(o_done, both(z, hp))
                    nc.gpsimd.tensor_tensor(qG[z][:, :, :], cv[2 * hp + z][:, 0:SEQ].rearrange("p (a b) -> p a b", b=P),
                                            eG[z][:, :, :], ALU.mult).then_inc(qG_ready, 1)
            pool.wait_ge(ds_act, 4)
            for h in range(H):
                nc.gpsimd.tensor_tensor(s0[:, h], s0[:, h], bcast(sb[:, 2, h * NS:(h + 1) * NS], P), ALU.mult).then_inc(s0_decayed, 1)
            pool.wait_ge(oscaled, H)
            nc.gpsimd.memset(L[:, :, :], 0.0).then_inc(cleared, 1)
            pool.wait_ge(slots_in, 16)
            for i in range(NT):
                pool.wait_ge(routed, 3 if i < SPLIT else 6)
                for n in range(2):
                    nc.gpsimd.indirect_dma_start(out=tab, out_offset=bass.IndirectOffsetOnAxis(ap=where[:, n, i:i + 1], axis=0),
                                                 in_=pid[:, n, i:i + 1], in_offset=None, bounds_check=MAXROWS * NE - 1,
                                                 oob_is_err=False).then_inc(tab_written, 16)
            count_groups(pool, "pool")
            otok_set = pool.alloc_register("otok_set")
            pool.reg_mov(otok_set, 0)
            pool.sem_inc(m_saved, 1)
            pool.wait_ge(routed, 7)
            for s in range(2):
                pool.wait_ge(h2_stored[s], 16 * ((NT + 1 - s) // 2))
            for t in (*xg, *xo, zero):
                nc.gpsimd.memset(t[:, :], 0).then_inc(cleared, 1)
            pool.wait_ge(cleared, 10)
            pool.wait_ge(idx_ready, 2)

            def gather(j, s):
                nc.gpsimd.tensor_tensor(gcur[s][:, :], gidx[:, bass.ds(j, 1)], zero[:, :], ALU.add).then_inc(gidx_set, 1)
                pool.wait_ge(gidx_set, j + 1)
                pool.sem_inc(pool_passed, 1)
                nc.gpsimd.indirect_dma_start(out=xg[s][:, :], out_offset=None, in_=h2d,
                                             in_offset=bass.IndirectOffsetOnAxis(ap=gcur[s][:, 0:1], axis=0),
                                             bounds_check=T - 1, oob_is_err=False).then_inc(xg_in[s], 16)

            def pool_round(it, first, last):
                for u in range(ROUND):
                    e = ROUND * it + u
                    if u % 2 == 0 and not last:
                        j = 2 * it + u // 2 + 2
                        pool.wait_ge(xg_turned, j - 1)
                        gather(j, u // 2)
                    column = 2 * it + u // 2 + u % 2 * (NE // 2)
                    if not first:
                        pool.wait_ge(y_out[u], 16 * it)
                    nc.gpsimd.tensor_tensor(scur[u][:, :], sidx[:, bass.ds(column, 1)], zero[:, :], ALU.add).then_inc(sidx_set, 1)
                    pool.wait_ge(sidx_set, e + 1)
                    pool.wait_ge(y_ready, e + 1)
                    pool.sem_inc(pool_passed, 1)
                    nc.gpsimd.indirect_dma_start(out=yd, out_offset=bass.IndirectOffsetOnAxis(ap=scur[u][:, 0:1], axis=0),
                                                 in_=ysb[u][:, :], in_offset=None, bounds_check=4 * T - 1,
                                                 oob_is_err=False).then_inc(y_out[u], 16)

                    def body(g, done, needed):
                        nc.gpsimd.tensor_tensor(osid[:, :], osids[:, bass.ds(g * NE + column, 1)], zero[:, :], ALU.add).then_inc(
                            m_osid, 1)
                        with pool.If(needed - 1 > g):
                            pool.wait_ge(m_pe, done * 4 + 1)
                            gather_more(g + 1, column, u % 2)
                        pool.wait_ge(m_osid, done + 1)
                        pool.wait_ge(m_vec, done * 3 + 3)
                        pool.sem_inc(pool_passed, 1)
                        nc.gpsimd.indirect_dma_start(out=yd, out_offset=bass.IndirectOffsetOnAxis(ap=osid[:, 0:1], axis=0),
                                                     in_=yo[:, :], in_offset=None, bounds_check=4 * T - 1,
                                                     oob_is_err=False).then_inc(m_out, 16)
                        pool.wait_ge(m_out, done * 16 + 16)
                        pool.sem_inc(m_saved, 1)

                    more_groups(pool, e, body)
                    if not (last and u >= 2):
                        first_further(e + 2, column + 1, u % 2)

            def gather_more(g, column, s):
                nc.gpsimd.tensor_tensor(otok[s][:, :], otoks[:, bass.ds(g * NE + column, 1)], zero[:, :], ALU.add).then_inc(
                    m_otok, 1)
                pool.reg_add(otok_set, otok_set, 1)
                pool.wait_ge(m_otok, pool.snap(otok_set))
                pool.sem_inc(pool_passed, 1)
                nc.gpsimd.indirect_dma_start(out=xo[s][:, :], out_offset=None, in_=h2d,
                                             in_offset=bass.IndirectOffsetOnAxis(ap=otok[s][0:CAP, 0:1], axis=0),
                                             bounds_check=T - 1, oob_is_err=False).then_inc(m_rows[s], 16)

            def first_further(e, column, s):
                with pool.If(pool.value_load(more[0:1, bass.ds(e, 1)], min_val=0, max_val=MORE) > 0):
                    gather_more(0, column, s)

            for s in range(2):
                gather(s, s)
            pool.wait_ge(idx_ready, 4)
            for s in range(2):
                first_further(s, s * (NE // 2), s)
            rounds(pool, pool_round)
            for u in range(ROUND):
                pool.wait_ge(y_out[u], 16 * ROUNDS)
            pool.sem_inc(moe_done, 1)

        @block.vector
        def _(vec):
            link = linker(vec, s_vec)
            stt = nc.vector.scalar_tensor_tensor
            def scale_rows(i):
                n = P if i < TT else NS
                if i >= 2:
                    vec.wait_ge(h_turned, i - 1)
                nc.vector.tensor_scalar(hrow[i % 2][0:n].rearrange("t c p -> t p c"), x[0:n, i, :].rearrange("t (p c) -> t p c", c=KT),
                                        rstd[0:n, i:i + 1], None, ALU.mult).then_inc(hrow_ready, 1)

            def evacuate_h(i):
                n = P if i < TT else NS
                vec.wait_ge(h_turned, i + 1)
                b = 2 * (i % 2)
                nc.vector.tensor_tensor(hT[:, :, tokens(i)], ps[:, b:b + 2, :].rearrange("p b (c t) -> p (b c) t", t=P)[:, :, 0:n],
                                        bcast(g1c[:, :], n), ALU.mult).then_inc(hT_ready, 1)

            vec.wait_ge(g1_in, 16)
            vec.wait_ge(x_squared, NT + 1)
            nc.vector.reciprocal(rstd[:, :], ss[:, :]).then_inc(rstd_ready, 1)
            vec.wait_ge(rstd_ready, 1)
            for i in range(NT + 1):
                if i < NT:
                    scale_rows(i)
                if i >= 1:
                    evacuate_h(i - 1)
            for i in range(2, NT):
                rest_of_tokens(vec, i)

            for n, (dst, src) in enumerate((
                (parq[:, :, :], ps[:, 4, 0:CQ * ROWS_Q].rearrange("p (n r) -> p n r", n=CQ)),
                (parab[:, :, :], ps[:, 5, 0:2 * ROWS_AB].rearrange("p (n r) -> p n r", n=2)),
                (usb[:, :, :, 0:WB - 1], ps[:, 6, 0:480].rearrange("p (t b j) -> p t b j", t=2, b=NS)),
            )):
                vec.wait_ge(rows_turned, n + 1)
                if n == 2:
                    for t in range(2):
                        link(nc.vector.tensor_copy(dst[:, t], src[:, t]))
                    nc.vector.tensor_scalar(lnh[:, :, :], parab[:, :, LNG:LNB + 1], 0.5, None, ALU.mult).then_inc(params_ready, 1)
                else:
                    nc.vector.tensor_copy(dst, src).then_inc(params_ready, 1)
                vec.wait_ge(params_ready, n + 1)
            vec.wait_ge(small_in, 5 * 16)
            link(nc.vector.tensor_scalar(ogh[:, :], ogc[:, :], 0.5, None, ALU.mult))

            def rows_of(ap):
                return ap.unsqueeze(1).broadcast_to([P, NT, H])

            vec.wait_ge(ba_ready, 2)
            link(nc.vector.tensor_tensor(gw[:, 6], ba[:, :, 4:8], rows_of(dtb[:, :]), ALU.add))
            stt(out=gw[:, 2], in0=gw[:, 6], scalar=-1.0, in1=gw[:, 6], op0=ALU.mult, op1=ALU.max).then_inc(g_vector, 1)
            vec.wait_ge(g_scalar, 3)
            nc.vector.tensor_scalar(gw[:, 4], gw[:, 3], 1.0, None, ALU.add).then_inc(g_vector, 1)
            link(nc.vector.tensor_scalar(gw[:, 8], gw[:, 0], 1.0, None, ALU.add))
            nc.vector.reciprocal(gw[:, 1], gw[:, 8]).then_inc(g_ready, 1)
            vec.wait_ge(g_scalar, 4)
            vec.wait_ge(g_ready, 1)
            link(stt(out=gw[:, 8], in0=gw[:, 6], scalar=0.0, in1=gw[:, 5], op0=ALU.max, op1=ALU.add))
            stt(out=gw[:, 7], in0=gw[:, 8], scalar=-1.0, in1=rows_of(gw[:, 9, 0, :]), op0=ALU.mult,
                op1=ALU.mult).then_inc(g_ready, 1)

            vec.wait_ge(glu_ready, 4)
            for t in range(2):
                link(nc.vector.tensor_tensor(sprod[:, :, :], usb[:, t, :, :],
                                             parab[:, t, 0:WB].unsqueeze(1).broadcast_to([P, NS, WB]), ALU.mult))
                link(nc.vector.tensor_reduce(yT[:, 2 + t, SEQ:T], sprod[:, :, :], AX_X, ALU.add))
            def taps(start, end):
                for k in range(start, min(end, 2 * WB)):
                    j, t = divmod(k, 2)
                    y, tap = yT[:, 2 + t, 0:SEQ], ub[t][:, j:j + SEQ]
                    if j >= 1:
                        vec.wait_ge(b_conved, 2 * j + t - 1)
                    if j == 0:
                        ins = nc.vector.tensor_scalar(y, tap, parab[:, t, 0:1], None, ALU.mult)
                    else:
                        ins = stt(out=y, in0=tap, scalar=parab[:, t, j:j + 1], in1=y, op0=ALU.mult, op1=ALU.add)
                    ins.then_inc(b_conved, 1)

            taps(0, 36)

            def convolve(m):
                vec.wait_ge(first_tap, m + 1)
                a, r = acc[m % 3], raw[m % 3]
                for j in range(1, WC):
                    ins = stt(out=a[:, :], in0=r[:, j:j + CV], scalar=parq[:, QKV[m], j:j + 1], in1=a[:, :],
                              op0=ALU.mult, op1=ALU.add)
                    if j < WC - 1:
                        link(ins)
                ins.then_inc(conv_done, 1)

            def gate(m):
                vec.wait_ge(tanh_done, m + 1)
                stt(out=cv[QKV[m]][:, :], in0=th[m % 2][:, :], scalar=1.0, in1=acc[m % 3][:, :], op0=ALU.add,
                    op1=ALU.mult).then_inc(cv_done, 1)

            def invert(g):
                vec.wait_ge(sums_ready, g + 1)
                if g:
                    vec.wait_ge(norms_spread, 4 * g)
                nc.vector.reciprocal(rn[:, 1, :], rn[:, 0, :]).then_inc(norms_ready, 1)

            def normalize(j):
                tile = [QKV[m] for m in qk_index][j]
                vec.wait_ge(norms_spread, j + 1)
                t = cv[tile][:, :].rearrange("p (a b) -> p a b", a=2)
                stt(out=t, in0=t, scalar=0.5 * P ** -0.5 if tile < 4 else 0.5, in1=ps[:, 6:8, 0:HC], op0=ALU.mult,
                    op1=ALU.mult).then_inc(qk_ready, 1)

            def gate_output(g):
                vec.wait_ge(z_evac, ZG + g + 1)
                stt(out=yT[:, 4 + g, :], in0=th[g % 2][:, 0:T], scalar=1.0, in1=yT[:, 4 + g, :], op0=ALU.add,
                    op1=ALU.mult).then_inc(gate_tanh, 1)

            vec.wait_ge(ba_done, 1)
            vec.wait_ge(h_lo, NT)
            for n in range(ZQ, NZ + 4):
                m = n - ZQ
                if n - 1 in LAST_SUM:
                    invert(LAST_SUM.index(n - 1))
                if m < CQ:
                    convolve(m)
                if 1 <= m <= CQ:
                    gate(m - 1)
                if 0 <= n - ZG < H:
                    gate_output(n - ZG)
                if n in SPREAD:
                    normalize(SPREAD.index(n))
                taps(36 + 3 * m, 36 + 3 * m + 3)

            vec.wait_ge(g_cols, 2)
            vec.wait_ge(a_mixed, 2)
            vec.wait_ge(qk_ready, len(qk_index))
            stt(out=sc1[:, 0:TT], in0=gw[:, 1, 0:TT], scalar=-1.0, in1=eGc[:, 0:TT], op0=ALU.mult, op1=ALU.mult).then_inc(col_scales, 1)
            nc.vector.tensor_scalar(sc3[:, 0:TT], gw[:, 1, 0:TT], 0.5, None, ALU.mult).then_inc(col_scales, 1)
            vec.wait_ge(col_scales, 2)

            def flat(t):
                return t[:, :, :].rearrange("p a b -> p (a b)")

            def bank(b):
                return ps[:, b, :].rearrange("p (a b) -> p a b", b=P)

            def mask(n):
                return cst[:, C_LM + n * P:C_LM + (n + 1) * P].unsqueeze(1).broadcast_to([P, TT, P])

            def over_chunks(ap):
                return ap.unsqueeze(1).broadcast_to([P, TT, P])

            tt = nc.vector.tensor_tensor

            def beside_level(hp, n):
                if hp == 0 and n == 2:
                    vec.wait_ge(b_pe, 1)
                    vec.wait_ge(b_conved, 2 * WB)
                    for t in range(2):
                        for half in range(2):
                            y = yT[:, 2 + t, half * HT:(half + 1) * HT]
                            ins = stt(out=y, in0=ps[:, 3 + 4 * half, 0:HT], scalar=-1.0 / DB, in1=y, op0=ALU.mult, op1=ALU.add)
                        ins.then_inc(b_vec, 1)
                if hp == 0 and n >= 5:
                    vec.wait_ge(b_act, 3)
                    half = slice((n - 5) * HT, (n - 4) * HT)
                    nc.vector.reciprocal(bsq[1][:, half], bsq[0][:, half]).then_inc(b_vec, 1)
                if hp == 1 and n == 1:
                    vec.wait_ge(small_saved, 2)
                    vec.wait_ge(z_evac, NZ)
                    tt(sb[:, 0, :].rearrange("p (h b) -> p h b", h=H), kq[:, :, :, 0], kq[:, :, :, 1], ALU.mult).then_inc(ds_vec, 1)
                    for j, slot in enumerate((7, 1)):
                        tt(dg[:, j], bcast(gw[0:NS, slot, TT, :], NS), ident[0:NS, 0:NS].unsqueeze(1).broadcast_to([NS, H, NS]),
                           ALU.mult).then_inc(ds_vec, 1)
                if hp == 1 and n == 2:
                    vec.wait_ge(b_vec, 4)
                    for t in range(2):
                        link(tt(yT[:, 2 + t, :], yT[:, 2 + t, :], bsq[1][:, :], ALU.mult))
                if hp == 1 and n == 3:
                    for t in range(2):
                        nc.vector.tensor_scalar(yT[:, 2 + t, :], yT[:, 2 + t, :], lnh[:, t, 0:1], lnh[:, t, 1:2], ALU.mult,
                                                ALU.add).then_inc(b_vec, 1)
                if hp == 1 and n == 5:
                    for t in range(2):
                        vec.wait_ge(b_act, 4 + t)
                        stt(out=yT[:, 2 + t, :], in0=bsq[t][:, :], scalar=1.0, in1=yT[:, 2 + t, :], op0=ALU.add,
                            op1=ALU.mult).then_inc(yb_ready, 1)

            def step_samples():
                vec.wait_ge(ds_act, 4)
                link(tt(sb[:, 4, :], kqs[:, :, 0], sb[:, 2, :], ALU.mult))
                link(stt(out=sb[:, 6, :], in0=small[:, 8:12, :].rearrange("p a b -> p (a b)"), scalar=0.5, in1=sb[:, 4, :],
                         op0=ALU.mult, op1=ALU.subtract))
                tt(sb[:, 5, :], sb[:, 6, :], sb[:, 3, :], ALU.mult).then_inc(ds_vec, 1)
                vec.wait_ge(ds_vec, 4)
                link(tt(sb[:, 7, :], kqs[:, :, 1], sb[:, 2, :], ALU.mult))
                link(tt(sb[:, 4, :], sb[:, 1, :], sb[:, 5, :], ALU.mult))
                for h in range(H):
                    tt(cv[8 + h][:, SEQ:T], sb[:, 7, h * NS:(h + 1) * NS], sb[:, 4, h * NS:(h + 1) * NS], ALU.add).then_inc(ds_vec, 1)

            for hp in range(2):
                pairs = [(z, 2 * hp + z, 4 * z) for z in range(2)]
                for z, h, B in pairs:
                    if hp:
                        vec.wait_ge(o_done, both(z, hp))
                    nc.vector.tensor_copy(grep[z][:, :, :], bcast(gw[:, 7, 0:TT, h], P)).then_inc(rep_ready, 1)
                    nc.vector.tensor_copy(brep[z][:, :, :], bcast(gw[:, 1, 0:TT, h], P)).then_inc(rep_ready, 1)
                for z, h, B in pairs:
                    vec.wait_ge(spread, both(z, 2 * hp + 2, 2))
                    tt(kb[z][:, :, :], cv[4 + h][:, 0:SEQ].rearrange("p (a b) -> p a b", b=P), bank(B + 1), ALU.mult).then_inc(kb_ready, 1)
                    vec.wait_ge(eG_ready, both(z, hp + 1))
                    tt(DT[z][:, :, :], bank(B), over_chunks(cst[:, C_MN:C_MN + P]), ALU.add).then_inc(D_ready, 1)
                    tt(gdif[:, 0:TT, h], ps[:, B, P - 1:SEQ:P], nG[:, 0:TT, h], ALU.add).then_inc(D_ready, 1)
                for z, h, B in pairs:
                    vec.wait_ge(scored, both(z, hp + 1))
                    vec.wait_ge(DT_ready, both(z, (TT + 1) * (hp + 1), 5))
                    tt(AT[z][:, :, :], bank(B + 2), DT[z][:, :, :], ALU.mult).then_inc(A_ready, 1)
                    vec.wait_ge(A_ready, both(z, 2 * hp + 1))
                    link(tt(BT[z][0][:, :, :], AT[z][:, :, :], mask(0), ALU.mult))
                    tt(XX[z][:, 1], over_chunks(ident), BT[z][0][:, :, :], ALU.subtract).then_inc(XT0_ready, 1)

                def mask_level(z, n):
                    if n >= 3:
                        vec.wait_ge(T1_done, both(z, (LEVELS - 1) * hp + n - 2))
                    if n == 2:
                        vec.wait_ge(XT0_ready, both(z, hp + 1))
                    tt(BT[z][n % 2][:, :, :], AT[z][:, :, :], mask(n), ALU.mult).then_inc(BT_ready, 1)

                for z in range(2):
                    mask_level(z, 1)
                for z, h, B in pairs:
                    tt(att[z][:, :, :], bank(B + 3), DT[z][:, :, :], ALU.mult).then_inc(A_ready, 1)
                for z, h, B in pairs:
                    vec.wait_ge(rows_done, both(z, hp + 1))
                    tt(kbG[z][:, :, :], bank(B), bcast(sc1[:, 0:TT, h], P), ALU.mult).then_inc(rows_scaled, 1)
                    tt(kd[z][:, :, :], bank(B), bcast(kds[:, 0:TT, h], P), ALU.mult).then_inc(rows_scaled, 1)
                    tt(vb[z][:, :, :], bank(B + 1), bcast(sc3[:, 0:TT, h], P), ALU.mult).then_inc(rows_scaled, 1)
                for n in range(1, LEVELS):
                    for z, h, B in pairs:
                        if n < LEVELS - 1:
                            mask_level(z, n + 1)
                    beside_level(hp, n)
                    for z, h, B in pairs:
                        vec.wait_ge(T2_done, both(z, (LEVELS - 1) * hp + n))
                        if n < LEVELS - 1:
                            xx, new = XX[z][:, :, :, :].rearrange("p x a b -> p x (a b)"), ps[:, B:B + 2, :]
                        else:
                            xx, new = XX[z][:, 1].rearrange("p a b -> p (a b)"), ps[:, B + 1, :]
                        tt(xx, xx, new, ALU.subtract).then_inc(X_ready, 1)
                if hp == 1:
                    step_samples()
                for i in range(TT):
                    for z, h, B in pairs:
                        vec.wait_ge(S_done, both(z, TT * hp + i + 1))
                        dst = S[z][i % 2][:, :] if i < TT - 1 else sfin[:, h, :]
                        new = ps[:, B, i * P:(i + 1) * P]
                        if i == 0:
                            ins = nc.vector.tensor_copy(dst, new)
                        else:
                            vec.wait_ge(S_ready, both(z, TT * hp + i))
                            ins = stt(out=dst, in0=S[z][(i - 1) % 2][:, :], scalar=eG[z][:, i, P - 1:P], in1=new,
                                      op0=ALU.mult, op1=ALU.add)
                        ins.then_inc(S_ready, 1)

            vec.wait_ge(oroot_ready, 1)
            nc.vector.reciprocal(rno[:, 1, :], rno[:, 0, :]).then_inc(onorm_ready, 1)
            vec.wait_ge(ds_vec, 8)
            for n in range(H):
                vec.wait_ge(ospread, n + 1)
                o = cv[8 + n][:, 0:T].rearrange("p (a b) -> p a b", a=2)
                b = (2, 4)[n % 2]
                link(stt(out=o, in0=o, scalar=ogh[:, :], in1=ps[:, b:b + 2, 0:HT], op0=ALU.mult, op1=ALU.mult))
                tt(yT[:, 4 + n, :], yT[:, 4 + n, :], cv[8 + n][:, 0:T], ALU.mult).then_inc(oscaled, 1)
            vec.wait_ge(ds_rowed, 2)

            def spread_values(h):
                if h >= 1:
                    vec.wait_ge(s0_outer, 2 * h)
                tt(vnd[:, :, :], srow[:, 0, h * P:(h + 1) * P].unsqueeze(1).broadcast_to([NS, NS, P]), bcast(ident[0:NS, 0:NS], P),
                   ALU.mult).then_inc(ds_diag, 1)

            def add_outer(h, half):
                vec.wait_ge(s0_outer, 2 * h + half + 1)
                vec.wait_ge(s0_decayed, h + 1)
                s = s0[:, h, 4 * half:4 * half + 4].rearrange("p b v -> p (b v)")
                tt(s, s, ps[:, 7, :], ALU.add).then_inc(s0_ready, 1)

            spread_values(0)
            vec.wait_ge(wout_in, 32)
            vec.wait_ge(states_out, 6 * 16)

            def add_mixers(i):
                n = rows(i)
                vec.wait_ge(wout_done, i + 1)
                if n == P:
                    xi = x[0:n, ORDER[i], :].rearrange("p (a b) -> p a b", a=2)
                    ins = tt(xi, xi, ps[0:n, 2 * (i % 2):2 * (i % 2) + 2, :], ALU.add)
                else:
                    for g in range(4):
                        xi = x[0:n, ORDER[i], g * D // 4:(g + 1) * D // 4]
                        ins = tt(xi, xi, ps[32 * g:32 * g + n, 2 * (i % 2), 0:D // 4], ALU.add)
                ins.then_inc(x1_ready, 1)
                if i < H:
                    add_outer(i, 0)
                vec.wait_ge(x1_squared, 2 * i + 2)
                nc.vector.reciprocal(rstd[0:n, i:i + 1], ss[0:n, i:i + 1]).then_inc(r2_ready, 1)
                vec.wait_ge(r2_ready, i + 1)
                if i >= 2:
                    vec.wait_ge(h2_turned, i - 1)
                    vec.wait_ge(h2_stored[i % 2], 16 * (i // 2))
                stt(out=h2row[i % 2][0:n].rearrange("t c p -> t p c"), in0=x[0:n, ORDER[i], :].rearrange("t (p c) -> t p c", c=KT),
                    scalar=rstd[0:n, i:i + 1], in1=g2b[0:n, :].rearrange("t (p c) -> t p c", c=KT), op0=ALU.mult,
                    op1=ALU.mult).then_inc(h2_ready, 1)
                if i < H:
                    add_outer(i, 1)
                if i + 1 < H:
                    spread_values(i + 1)

            ts = nc.vector.tensor_scalar
            reduce = nc.vector.tensor_reduce
            m, other, hit, one, chosen, two, rank = (eight[n] for n in range(7))
            total = other

            def over_tiles(column, width, count):
                return cst[:, column:column + width].unsqueeze(1).broadcast_to([P, count, width])

            def first_of(hit, index, onehot, iota):
                link(ts(hit, hit, -99.0, 99.0, ALU.mult, ALU.add))
                link(tt(hit, hit, iota, ALU.add))
                link(reduce(index, hit, AX_X, ALU.min))
                link(tt(onehot, iota, bcast(index, NE), ALU.is_equal))

            def choose(start, end):
                r, count = slice(start, end), end - start
                gl, el = L[:, r, 0:NG], L[:, r, NG:]
                iota = over_tiles(C_IO, NE, count)
                vec.wait_ge(logits_ready, 2 if start == 0 else 3)
                link(reduce(ns[:, 0, r], gl, AX_X, ALU.max))
                link(tt(g4[:, 0, r], gl, bcast(ns[:, 0, r], NG), ALU.subtract))
                link(tt(g4[:, 2, r], gl, bcast(ns[:, 0, r], NG), ALU.is_equal))
                link(ts(g4[:, 2, r], g4[:, 2, r], -99.0, 99.0, ALU.mult, ALU.add))
                link(tt(g4[:, 2, r], g4[:, 2, r], iota[:, :, 0:NG], ALU.add))
                link(reduce(ns[:, 3, r], g4[:, 2, r], AX_X, ALU.min))
                link(tt(m[:, r], over_tiles(C_GI, NE, count), bcast(ns[:, 3, r], NE), ALU.is_equal))
                link(ts(rank[:, r], m[:, r], 1e30, -1e30, ALU.mult, ALU.add))
                link(tt(m[:, r], m[:, r], el, ALU.mult))
                link(tt(m[:, r], m[:, r], rank[:, r], ALU.add))
                link(reduce(ns[:, 6, r], m[:, r], AX_X, ALU.max))
                link(tt(hit[:, r], m[:, r], bcast(ns[:, 6, r], NE), ALU.is_equal))
                first_of(hit[:, r], ns[:, 8, r], one[:, r], iota)
                link(stt(out=m[:, r], in0=one[:, r], scalar=-3e30, in1=m[:, r], op0=ALU.mult, op1=ALU.add))
                link(reduce(ns[:, 7, r], m[:, r], AX_X, ALU.max))
                link(tt(hit[:, r], m[:, r], bcast(ns[:, 7, r], NE), ALU.is_equal))
                first_of(hit[:, r], ns[:, 9, r], two[:, r], iota)
                link(tt(chosen[:, r], one[:, r], two[:, r], ALU.add))
                tt(chosen[:, r], chosen[:, r], bcast(cst[:, C_TILE + start:C_TILE + end], NE), ALU.mult).then_inc(routed, 1)
                tt(ns[:, 4, r], ns[:, 7, r], ns[:, 6, r], ALU.subtract).then_inc(rt_vec, 1)

            def place(start, end):
                r, count = slice(start, end), end - start
                vec.wait_ge(ranked, 1 if start == 0 else 2)
                link(nc.vector.tensor_copy(total[:, r], ps[:, 3, 0:count * NE].rearrange("p (a b) -> p a b", b=NE)))
                for i in range(max(1, start), end):
                    link(tt(total[:, i], total[:, i], total[:, i - 1], ALU.add))
                link(nc.vector.tensor_copy(rank[:, r], ps[:, 2, 0:count * NE].rearrange("p (a b) -> p a b", b=NE)))
                after = max(1, start)
                link(tt(rank[:, after:end], rank[:, after:end], total[:, after - 1:end - 1], ALU.add))
                link(stt(out=rank[:, r], in0=rank[:, r], scalar=float(NE), in1=over_tiles(C_EC, NE, count), op0=ALU.mult, op1=ALU.add))
                for n, onehot in enumerate((one, two)):
                    link(tt(hit[:, r], onehot[:, r], rank[:, r], ALU.mult))
                    link(reduce(ns[:, 8 + n, r], hit[:, r], AX_X, ALU.add))
                    tt(where[:, n, r], ns[:, 8 + n, r], cst[:, C_PAD + start:C_PAD + end], ALU.add).then_inc(routed, 1)

            link(nc.vector.tensor_copy(pid[:, 0], cst[:, C_ROWID:C_ROWID + NT]))
            link(ts(pid[:, 1], cst[:, C_ROWID:C_ROWID + NT], float(T), None, ALU.add))
            for i in range(NT):
                if i == NT - 1:
                    choose(0, SPLIT)
                add_mixers(i)
            place(0, SPLIT)
            choose(SPLIT, NT)
            place(SPLIT, NT)
            count = total[0:1, NT - 1, :]
            link(ts(moref[:, 0, :], count, float(CAP), None, ALU.is_gt))
            for n in range(2, MORE + 1):
                link(ts(moref[:, 1, :], count, float(n * CAP), None, ALU.is_gt))
                link(tt(moref[:, 0, :], moref[:, 0, :], moref[:, 1, :], ALU.add))
            nc.vector.tensor_copy(more[:, :], moref[:, 0, :]).then_inc(routed, 1)
            vec.wait_ge(rt_act, 2)
            link(reduce(ns[:, 1], g4[:, 1], AX_X, ALU.add))
            link(nc.vector.reciprocal(ns[:, 2], ns[:, 1]))
            link(ts(ns[:, 10], ns[:, 5], 1.0, None, ALU.add))
            link(nc.vector.reciprocal(ns[:, 11], ns[:, 10]))
            link(tt(wgt[:, 0], ns[:, 11], ns[:, 2], ALU.mult))
            link(tt(wgt[:, 1], wgt[:, 0], ns[:, 5], ALU.mult))
            vec.wait_ge(slots_in, 7 * 16)
            link(nc.vector.tensor_copy(idf[:, 0, 0:NE // 2], graw[:, :]))
            link(ts(idf[:, 1, 0:NE // 2], idf[:, 0, 0:NE // 2], float(T), -float(T), ALU.is_ge, ALU.mult))
            tt(gidx[:, :], idf[:, 0, 0:NE // 2], idf[:, 1, 0:NE // 2], ALU.add).then_inc(idx_ready, 1)
            vec.wait_ge(idx_ready, 1)
            link(nc.vector.tensor_copy(idf[:, 0, :], sraw[:, :]))
            ts(sidx[:, :], idf[:, 0, :], 2.0, cst[:, C_HALF:C_HALF + 1], ALU.mult, ALU.add).then_inc(idx_ready, 1)
            slot_of, past = (t[:, :, :].rearrange("p a b -> p (a b)") for t in oidf)
            link(nc.vector.tensor_copy(slot_of, oraw[:, :, :].rearrange("p a b -> p (a b)")))
            link(ts(past, slot_of, float(T), -float(T), ALU.is_ge, ALU.mult))
            tt(otoks[:, 0:MORE * NE], slot_of, past, ALU.add).then_inc(idx_ready, 1)
            ts(osids[:, :], slot_of, 2.0, cst[:, C_HALF:C_HALF + 1], ALU.mult, ALU.add).then_inc(idx_ready, 1)
            count_groups(vec, "vec")
            vec.wait_ge(routed, 7)

            def swiglu(e, s):
                vec.wait_ge(up_tanh, e + 1)
                stt(out=gact[s][:, :], in0=gth[s][:, :], scalar=1.0, in1=ps[:, s, 0:P], op0=ALU.add, op1=ALU.mult).then_inc(act_half, 1)
                vec.wait_ge(act_half, e + 1)
                stt(out=gact[s][:, :], in0=gact[s][:, :], scalar=0.5, in1=ps[:, s, P:2 * P], op0=ALU.mult, op1=ALU.mult).then_inc(
                    act_ready, 1)

            def vec_round(it, first, last):
                for u in range(ROUND):
                    e = ROUND * it + u
                    if u < 3:
                        if u == 0:
                            swiglu(e, 0)
                        swiglu(e + 1, (u + 1) % 2)
                    vec.wait_ge(down_done, e + 1)
                    if not first:
                        vec.wait_ge(y_out[u], 16 * it)
                    nc.vector.tensor_copy(ysb[u][:, :], ps[:, 4 + u % 2, :]).then_inc(y_ready, 1)

                    def body(g, done, needed):
                        vec.wait_ge(m_act, done * 3 + 2)
                        stt(out=oact[:, :], in0=oth[:, :], scalar=1.0, in1=ps[:, 3, 0:P], op0=ALU.add, op1=ALU.mult).then_inc(m_vec, 1)
                        vec.wait_ge(m_vec, done * 3 + 1)
                        stt(out=oact[:, :], in0=oact[:, :], scalar=0.5, in1=ps[:, 3, P:2 * P], op0=ALU.mult, op1=ALU.mult).then_inc(m_vec, 1)
                        vec.wait_ge(m_pe, done * 4 + 4)
                        vec.wait_ge(m_saved, done + 1)
                        nc.vector.tensor_copy(yo[:, :], ps[:, 3, :]).then_inc(m_vec, 1)

                    more_groups(vec, e, body)
                    vec.sem_inc(expert_done, 1)

            rounds(vec, vec_round)
            def add_rows(i):
                n = rows(i)
                for k in range(2):
                    vec.wait_ge(x_in[i], 16 + 2 * 16)
                    if k:
                        vec.wait_ge(fin_added, 2 * i + 1)
                    stt(out=x[0:n, ORDER[i], :], in0=yk[i][0:n, k, :], scalar=wgt[0:n, k, i:i + 1], in1=x[0:n, ORDER[i], :], op0=ALU.mult,
                        op1=ALU.add).then_inc(fin_added, 1)

            def finish(i):
                n = rows(i)
                vec.wait_ge(x1_squared, 2 * (NT + i) + 2)
                nc.vector.reciprocal(rstd[0:n, i:i + 1], ss[0:n, i:i + 1]).then_inc(r2_ready, 1)
                vec.wait_ge(r2_ready, NT + i + 1)
                stt(out=x[0:n, ORDER[i], :], in0=x[0:n, ORDER[i], :], scalar=rstd[0:n, i:i + 1], in1=gfb[0:n, :], op0=ALU.mult,
                    op1=ALU.mult).then_inc(fin_ready, 1)

            for i in range(NT + 1):
                if i < NT:
                    add_rows(i)
                if i >= 1:
                    finish(i - 1)

        @block.tensor
        def _(pe):
            mm = nc.tensor.matmul
            turn = nc.tensor.transpose
            pe.wait_ge(consts_in, 16)
            for i in range(NT):
                n = P if i < TT else NS
                pe.wait_ge(hrow_ready, i + 1)
                if i >= 2:
                    pe.wait_ge(hT_ready, i - 1)
                for c in range(KT):
                    last = turn(ps[:, 2 * (i % 2) + c // 4, c % 4 * P:c % 4 * P + n], hrow[i % 2][0:n, c, :], ident[0:n, 0:n])
                last.then_inc(h_turned, 1)
            pe.wait_ge(rows_in, 8 * 16)
            for n in range(CQ):
                last = turn(ps[:, 4, n * ROWS_Q:(n + 1) * ROWS_Q], rowq[:, n * P:(n + 1) * P], ident[0:ROWS_Q, 0:ROWS_Q])
            last.then_inc(rows_turned, 1)
            for t in range(2):
                last = turn(ps[:, 5, t * ROWS_AB:(t + 1) * ROWS_AB], rowab[:, t * P:(t + 1) * P], ident[0:ROWS_AB, 0:ROWS_AB])
            last.then_inc(rows_turned, 1)
            for t in range(2):
                for a in range(2):
                    last = turn(ps[:, 6, (2 * t + a) * 120:(2 * t + a + 1) * 120], rowsb[:, a, t * P:(t + 1) * P],
                                ident[0:120, 0:120])
            last.then_inc(rows_turned, 1)
            def project_scalars():
                pe.wait_ge(small_in, 5 * 16)
                pe.wait_ge(hT_ready, NT)
                for i in range(NT):
                    n = P if i < TT else NS
                    for c in range(KT):
                        last = mm(ps[0:n, 7, i * 8:(i + 1) * 8], hT[:, c, tokens(i)], wba[:, c, :], start=c == 0, stop=c == KT - 1)
                last.then_inc(ba_done, 1)

            def project(n):
                s = n % WSLOTS
                pe.wait_ge(w_lo, n + 1)
                if n == 0:
                    pe.wait_ge(hT_ready, NT)
                if n >= 2:
                    pe.wait_ge(z_evac, n - 1)
                for half, (lo, hi) in enumerate(((0, 256), (256, T))):
                    if n == 0:
                        pe.wait_ge(h_lo, NT)
                    parts = [(weights[s], h) for weights, h in ((whi, hhi), (wlo, hhi), (whi, hlo))]
                    for c in range(KT):
                        for j, (weights, h) in enumerate(parts):
                            last = mm(ps[:, 2 * (n % 2) + half, 0:hi - lo], weights[:, c, :], h[:, c, lo:hi],
                                      start=c == 0 and j == 0, stop=c == KT - 1 and j == len(parts) - 1)
                last.then_inc(z_done, 1)

            def sum_squares(m):
                if m not in qk_index:
                    return
                j = qk_index[m]
                pe.wait_ge(squared, j + 1)
                if j == 4:
                    pe.wait_ge(sums_ready, 1)
                for half in range(2):
                    last = mm(ps[0:8, 4 + half, 0:HC], column(j % 4), sq[j % 2][:, half * HC:(half + 1) * HC], start=j % 4 == 0,
                              stop=j % 4 == 3)
                last.then_inc(sums_done, 1)

            def spread_norm(j):
                pe.wait_ge(norms_ready, j // 4 + 1)
                if j:
                    pe.wait_ge(qk_ready, j)
                else:
                    pe.wait_ge(g_cols, 2)
                for half in range(2):
                    last = mm(ps[:, 6 + half, 0:HC], select(j % 4), rn[:, 1, half * HC:(half + 1) * HC], start=True, stop=True)
                last.then_inc(norms_spread, 1)

            for n in range(NZ + 4):
                if n < NZ:
                    project(n)
                if n == 1:
                    project_scalars()
                if n == ZQ - 1:
                    pe.wait_ge(g_ready, 2)
                    mm(ps[:, 7, 0:TT * H], incl, gw[:, 7, 0:TT, :], start=True, stop=True).then_inc(g_summed, 1)
                sum_squares(n - ZQ - 3)
                if n in SPREAD:
                    spread_norm(SPREAD.index(n))

            pe.wait_ge(qk_ready, len(qk_index))

            def beside_level(hp, n):
                if n == 1:
                    for z in range(2):
                        pe.wait_ge(A_ready, both(z, 2 * hp + 2))
                if hp == 0 and n in (1, 3):
                    if n == 1:
                        pe.wait_ge(b_conved, 2 * WB)
                    else:
                        pe.wait_ge(b_act, 2)
                    for half in range(2):
                        c = slice(half * HT, (half + 1) * HT)
                        for t in range(2):
                            last = mm(ps[:, 3 + 4 * half, 0:HT], ones, yT[:, 2 + t, c] if n == 1 else bsq[t][:, c],
                                      start=t == 0, stop=t == 1)
                    last.then_inc(b_pe, 1)
                if hp == 1 and n == 2:
                    pe.wait_ge(ds_vec, 3)
                    mm(ps[:, 7, 0:H * NS], ones, sb[:, 0, :], start=True, stop=True).then_inc(ds_prod, 1)
                    mm(ps[:, 7, 2 * H * NS:4 * H * NS], ones[0:NS, :], dg[:, :, :, :].rearrange("p a b c -> p (a b c)"), start=True,
                       stop=True).then_inc(ds_prod, 1)
                if hp == 1:
                    if n == 1:
                        pe.wait_ge(small_saved, 2)
                        pe.wait_ge(s0_in, H * 16)
                    for j in range(6 * (n - 1), min(6 * n, H * NS)):
                        last = mm(ps[:, 3, 2 * j:2 * j + 2], s0[:, j // NS, j % NS, :], kq[:, j // NS, j % NS, :], start=True, stop=True)
                    if n == LEVELS - 1:
                        last.then_inc(ds_prod, 1)

            def chunk(t, i):
                return t[:, i * P:(i + 1) * P]

            def four_products(bank, left, right):
                for i in range(TT):
                    last = mm(ps[:, bank, i * P:(i + 1) * P], left(i), right(i), start=True, stop=True)
                return last

            for hp in range(2):
                pairs = [(z, 2 * hp + z, 4 * z) for z in range(2)]
                for z, h, B in pairs:
                    pe.wait_ge(rep_ready, both(z, 2 * hp + 2, 2))
                    if z == 1:
                        pe.wait_ge(g_cols, 2)
                    if hp:
                        pe.wait_ge(o_ready, both(z, hp))
                        pe.wait_ge(S_ready, both(z, TT * hp))
                    four_products(B, lambda i: grep[z][:, i, :], lambda i: incl).then_inc(spread, 1)
                    four_products(B + 1, lambda i: brep[z][:, i, :], lambda i: ident).then_inc(spread, 1)
                for z, h, B in pairs:
                    q, k, v = cv[h], cv[4 + h], cv[8 + h]
                    pe.wait_ge(kb_ready, both(z, hp + 1))
                    four_products(B + 2, lambda i: chunk(k, i), lambda i: kb[z][:, i, :])
                    four_products(B + 3, lambda i: chunk(k, i), lambda i: chunk(q, i)).then_inc(scored, 1)
                    pe.wait_ge(eG_ready, both(z, hp + 1))
                    pe.wait_ge(D_ready, both(z, 2 * hp + 2, 2))
                    for i in range(TT):
                        turn(ps[:, B, i * P:(i + 1) * P], chunk(k, i), ident)
                    for i in range(TT):
                        last = turn(ps[:, B + 1, i * P:(i + 1) * P], chunk(v, i), ident)
                    last.then_inc(rows_done, 1)
                for z, h, B in pairs:
                    pe.wait_ge(XT0_ready, both(z, hp + 1))
                    for i in range(TT):
                        last = turn(ps[:, B + 2, i * P:(i + 1) * P], XX[z][:, 1, i, :], ident)
                    last.then_inc(X0_done, 1)
                for n in range(1, LEVELS):
                    for z, h, B in pairs:
                        before = (LEVELS - 1) * hp + n
                        pe.wait_ge(BT_ready, both(z, before))
                        pe.wait_ge(X0_ready, both(z, hp + 1))
                        if n > 1:
                            pe.wait_ge(X_ready, both(z, before - 1))
                        four_products(B + 2, lambda i: BT[z][n % 2][:, i, :], lambda i: XX[z][:, 0, i, :]).then_inc(T1_done, 1)
                    beside_level(hp, n)
                    for z, h, B in pairs:
                        pe.wait_ge(T1_ready, both(z, before))
                        if n == 1:
                            pe.wait_ge(rows_scaled, both(z, 3 * hp + 3, 3))
                        if n < LEVELS - 1:
                            four_products(B, lambda i: XX[z][:, 1, i, :], lambda i: t1[z][:, i, :])
                        four_products(B + 1, lambda i: t1[z][:, i, :], lambda i: XX[z][:, 1, i, :]).then_inc(T2_done, 1)
                for z, h, B in pairs:
                    pe.wait_ge(X_ready, both(z, (LEVELS - 1) * (hp + 1)))
                    four_products(B + 2, lambda i: kbG[z][:, i, :], lambda i: XX[z][:, 1, i, :]).then_inc(wT_done, 1)
                if hp == 0:
                    pe.wait_ge(b_act, 3)
                else:
                    pe.wait_ge(ds_act, 4)
                for i in range(TT):
                    for z, h, B in pairs:
                        pv = ps[:, B + 3, i * P:(i + 1) * P]
                        last = mm(pv, XX[z][:, 1, i, :], vb[z][:, i, :], start=True, stop=i == 0)
                        if i:
                            if i == 1:
                                pe.wait_ge(wT_ready, both(z, hp + 1))
                            pe.wait_ge(S_ready, both(z, TT * hp + i))
                            last = mm(pv, wT[z][:, i, :], S[z][(i - 1) % 2][:, :], start=False, stop=True)
                        last.then_inc(vn_done, 1)
                    for z, h, B in pairs:
                        pe.wait_ge(vn_ready, both(z, TT * hp + i + 1))
                        mm(ps[:, B, i * P:(i + 1) * P], kd[z][:, i, :], vn[z][:, i, :], start=True, stop=True).then_inc(S_done, 1)
                        po = ps[:, B + 1, i * P:(i + 1) * P]
                        if i:
                            if i == 1:
                                pe.wait_ge(qG_ready, both(z, hp + 1))
                            mm(po, S[z][(i - 1) % 2][:, :], qG[z][:, i, :], start=True, stop=False)
                        last = mm(po, vn[z][:, i, :], att[z][:, i, :], start=i == 0, stop=True)
                        if i == TT - 1:
                            last.then_inc(o_done, 1)

            for z in range(2):
                pe.wait_ge(o_ready, both(z, 2))
                pe.wait_ge(S_ready, both(z, 2 * TT))
            pe.wait_ge(ds_vec, 4)
            for h in range(H):
                turn(ps[0:NS, 4, h * P:(h + 1) * P], sb[:, 5, h * NS:(h + 1) * NS], ident)
            for h in range(H):
                last = turn(ps[0:NS, 5, h * P:(h + 1) * P], kq[:, h, :, 0], ident)
            last.then_inc(ds_row, 1)
            for n in range(H):
                pe.wait_ge(osq_ready, n + 1)
                for half in range(2):
                    last = mm(ps[0:8, 2 + half, 0:HT], column(n), osq[n % 2][:, half * HT:(half + 1) * HT],
                              start=n == 0, stop=n == H - 1)
                last.then_inc(osum_done, 1)
            for n in range(8):
                last = turn(ps[0:27, 6 + n // 4, n % 4 * P:(n % 4 + 1) * P], stq[:, n, :], ident)
            last.then_inc(rows_turned, 1)
            pe.wait_ge(states_ready, 1)
            for n in range(8, CQ):
                turn(ps[0:27, 6, n % 4 * P:(n % 4 + 1) * P], stq[:, n, :], ident)
            for t in range(2):
                turn(ps[0:18, 7, t * P:(t + 1) * P], sta[:, t, :], ident)
                last = turn(ps[0:WB - 1, 7, DB + t * P:DB + (t + 1) * P], stp[:, t, :], ident)
            last.then_inc(rows_turned, 1)
            pe.wait_ge(onorm_ready, 1)
            pe.wait_ge(ds_rowed, 2)
            for n in range(H):
                if n >= 2:
                    pe.wait_ge(oscaled, n - 1)
                for half in range(2):
                    last = mm(ps[:, (2, 4)[n % 2] + half, 0:HT], select(n), rno[:, 1, half * HT:(half + 1) * HT], start=True, stop=True)
                last.then_inc(ospread, 1)
            pe.wait_ge(states_ready, 2)
            for a in range(2):
                for t in range(2):
                    last = turn(ps[0:120, 6, a * DB + t * P:a * DB + (t + 1) * P], stb[:, t, a * 120:(a + 1) * 120], ident)
            last.then_inc(rows_turned, 1)
            pe.wait_ge(wout_in, 32)
            pe.wait_ge(a_mixed, 2)
            pe.wait_ge(yb_ready, 2)

            def outer(h, half):
                pe.wait_ge(ds_diag, h + 1)
                if h == half == 0:
                    pe.wait_ge(states_ready, 5)
                if 2 * h + half:
                    pe.wait_ge(s0_ready, 2 * h + half)
                mm(ps[:, 7, :], srow[:, 1, h * P:(h + 1) * P], vnd[:, 4 * half:4 * half + 4, :], start=True,
                   stop=True).then_inc(s0_outer, 1)

            def out_project_samples():
                for k in range(KT):
                    if k >= 4:
                        pe.wait_ge(oscaled, k - 3)
                    for g in range(4):
                        last = mm(ps[32 * g:32 * g + NS, 0, 0:D // 4], yT[:, k, tokens(TT)],
                                  wout[:, k, g * D // 4:(g + 1) * D // 4], start=k == 0, stop=k == KT - 1)
                last.then_inc(wout_done, 1)

            def out_project(i, half):
                if half == 0 and i >= 2:
                    pe.wait_ge(x1_ready, i - 1)
                for k in range(KT):
                    last = mm(ps[:, 2 * (i % 2) + half, :], yT[:, k, tokens(ORDER[i])], wout[:, k, half * 512:(half + 1) * 512],
                              start=k == 0, stop=k == KT - 1)
                if half:
                    last.then_inc(wout_done, 1)

            def turn_h2(i):
                n = rows(i)
                pe.wait_ge(h2_ready, i + 1)
                if i >= 1:
                    pe.wait_ge(h2T_ready, i)
                for c in range(KT):
                    last = turn(ps[:, 4 + c // 4, c % 4 * P:c % 4 * P + n], h2row[i % 2][0:n, c, :], ident[0:n, 0:n])
                last.then_inc(h2_turned, 1)

            def logits(i):
                n = rows(i)
                pe.wait_ge(h2T_ready, i + 1)
                pe.wait_ge(wr_in, (1 + NG) * 16)
                if i == SPLIT:
                    pe.wait_ge(logits_ready, 2)
                for c in range(KT):
                    last = mm(ps[0:n, 6, i * (NG + NE):(i + 1) * (NG + NE)], h2T[:, c, 0:n], wr[:, c, :], start=c == 0,
                              stop=c == KT - 1)
                last.then_inc(logits_done, 1)

            def count_pairs(start, end):
                pe.wait_ge(routed, 1 if start == 0 else 4)
                pe.wait_ge(x1_ready, NT - 1)
                picked = eight[4][:, start:end, :].rearrange("p a b -> p (a b)")
                mm(ps[:, 2, 0:(end - start) * NE], cst[:, C_US:C_US + P], picked, start=True, stop=True)
                mm(ps[:, 3, 0:(end - start) * NE], ones, picked, start=True, stop=True).then_inc(ranked, 1)

            out_project_samples()
            outer(0, 0)
            outer(0, 1)
            for i in range(1, NT):
                out_project(i, 0)
                if i < H:
                    outer(i, 0)
                turn_h2(i - 1)
                logits(i - 1)
                out_project(i, 1)
                if i < H:
                    outer(i, 1)
            count_pairs(0, SPLIT)
            turn_h2(NT - 1)
            logits(NT - 1)
            count_pairs(SPLIT, NT)
            count_groups(pe, "pe")
            slot_groups = [pe.alloc_register(f"slot_groups{s}") for s in range(2)]
            for r in slot_groups:
                pe.reg_mov(r, 0)
            pe.wait_ge(routed, 7)

            def halves(bank, left, right, steps, width):
                for c in range(steps):
                    for g in range(2):
                        last = mm(ps[g * CAP:(g + 1) * CAP, bank, 0:width], left(c), right(c, g), start=c == 0, stop=c == steps - 1)
                return last

            def up(u, bank, left):
                return halves(bank, left, lambda c, g: gu[u][:, :, c, g * P:(g + 1) * P], KT, 2 * P)

            def down(u, bank, a):
                return halves(bank, lambda c: a[:, c * CAP:(c + 1) * CAP], lambda c, g: wd[u][:, c, g * 512:(g + 1) * 512], 2, 512)

            def pe_up(it, u):
                e = ROUND * it + u
                s = u // 2
                pe.wait_ge(weights_in[u], tiles_in[u] + 3 * 16 * (it + 1))
                pe.wait_ge(xT_ready, 2 * it + s + 1)
                up(u, u % 2, lambda c: xT[s][:, c, u % 2 * CAP:(u % 2 + 1) * CAP]).then_inc(up_done, 1)

            def pe_round(it, first, last):
                for u in range(ROUND):
                    e = ROUND * it + u
                    if u == 0:
                        pe_up(it, 0)
                    if u < 3:
                        pe_up(it, u + 1)
                    if u == 0 or (u == 2 and not last):
                        j = 2 * it + u // 2 + 1
                        s = (u // 2 + 1) % 2
                        pe.wait_ge(xg_in[s], 16 * (it + 1) if s else 16 * (it + 2))
                        pe.wait_ge(xT_ready, j)
                        for c in range(KT):
                            ins = turn(ps[:, 6 + c // 4, c % 4 * P:(c % 4 + 1) * P], xg[s][:, c * P:(c + 1) * P], ident)
                        ins.then_inc(xg_turned, 1)
                    pe.wait_ge(act_ready, e + 1)
                    turn(ps[:, 2, 0:P], gact[u % 2][:, :], ident).then_inc(act_turned, 1)
                    pe.wait_ge(aT_ready, e + 1)
                    down(u, 4 + u % 2, aT[u % 2]).then_inc(down_done, 1)

                    def body(g, done, needed):
                        pe.wait_ge(m_rows[u % 2], pe.snap(slot_groups[u % 2]) * 16 + 16)
                        pe.reg_add(slot_groups[u % 2], slot_groups[u % 2], 1)
                        for c in range(KT):
                            out, part = ps[:, 3, c * CAP:(c + 1) * CAP], xo[u % 2][:, c * P:(c + 1) * P]
                            if c == 0:
                                mm(out, part, ident[0:CAP, 0:CAP], start=True, stop=True)
                            else:
                                ins = turn(out, part, ident[0:CAP, 0:CAP])
                        ins.then_inc(m_pe, 1)
                        pe.wait_ge(m_act, done * 3 + 1)
                        up(u, 3, lambda c: xTo[:, c, :]).then_inc(m_pe, 1)
                        pe.wait_ge(m_vec, done * 3 + 2)
                        turn(ps[:, 3, 0:P], oact[:, :], ident).then_inc(m_pe, 1)
                        pe.wait_ge(m_act, done * 3 + 3)
                        down(u, 3, oaT).then_inc(m_pe, 1)
                        pe.wait_ge(m_vec, done * 3 + 3)

                    more_groups(pe, e, body)

            pe.wait_ge(xg_in[0], 16)
            for c in range(KT):
                last = turn(ps[:, 6 + c // 4, c % 4 * P:(c % 4 + 1) * P], xg[0][:, c * P:(c + 1) * P], ident)
            last.then_inc(xg_turned, 1)
            rounds(pe, pe_round)


OUTS = {
    "y_p": (1, SEQ, D), "y_s": (NS, 1, D),
    "ca_p": (1, 1, WA - 1, DA), "cb_p": (1, 1, WB - 1, DB), "cq_p": (1, 1, WC - 1, CQ * P), "d_p": (1, 1, H, P, P),
    "ca_s": (1, NS, WA - 1, DA), "cb_s": (1, NS, WB - 1, DB), "cq_s": (1, NS, WC - 1, CQ * P), "d_s": (1, NS, H, P, P),
}


def kernel(**inputs):
    import concourse.bacc as bacc
    from concourse.bass_utils import run_bass_kernel_spmd

    nc = bacc.Bacc("TRN2", target_bir_lowering=False, num_devices=1)
    arrays = {name: np.ascontiguousarray(a) for name, a in inputs.items()}
    arrays["consts"] = constants()
    A = {name: nc.dram_tensor(name, a.shape, mybir.dt.from_np(a.dtype), kind="ExternalInput").ap() for name, a in arrays.items()}
    R = {name: nc.dram_tensor(name + "_out", shape, F32, kind="ExternalOutput").ap() for name, shape in OUTS.items()}
    build(nc, A, R)
    got = run_bass_kernel_spmd(nc, [arrays], core_ids=[0]).results[0]
    return tuple(got[name + "_out"] for name in OUTS)
```
